# Optimizing a Trainium2 kernel written in Bass

```python
import math
import jax, jax.numpy as jnp
from jax import lax
import numpy as np

D_MODEL = 1024
BATCH = 1
SEQ = 2048
DEPTH = 1
DEC_BATCH = 8
DEC_SEQ = 1
PAST_LEN = 16384
PAGE_SIZE = 128

MIX_W = D_MODEL
H_A = D_MODEL // 256
DK = 128
DV = 128
W_A = H_A * DV
QKV_DIM = 2 * H_A * DK + H_A * DV
CONV_W = 4
DN_CHUNK = 64
W_B = MIX_W - W_A
H_B = 4
DH_B = W_B // H_B
GM_CHUNK = 128
D_FF = 4 * D_MODEL
OFF_G = QKV_DIM
OFF_A = OFF_G + W_A
OFF_B = OFF_A + H_A
OFF_U = OFF_B + H_A
OFF_V = OFF_U + W_B
PROJ_DIM = OFF_V + W_B
EPS = 1e-6

kernel_name = "hymba_gdn_gmlp_decode_step"

def rmsnorm(x, g):
    xf = x.astype(jnp.float32)
    y = xf * lax.rsqrt(jnp.mean(xf * xf, axis=-1, keepdims=True) + EPS)
    return (y * g.astype(jnp.float32)).astype(x.dtype)

def l2norm(x):
    return x * lax.rsqrt(jnp.sum(x * x, axis=-1, keepdims=True) + EPS)

def causal_conv(x, buf, w):
    L = x.shape[1]
    xp = jnp.concatenate([buf.astype(x.dtype), x], axis=1)
    y = xp[:, 0:L] * w[0]
    for j in range(1, CONV_W):
        y = y + xp[:, j:j + L] * w[j]
    return y, xp[:, L:]

def gated_delta_chunked(q, k, v, gdec, beta, S0):
    B, L, H, _ = q.shape
    C = DN_CHUNK
    N = L // C
    q = q.reshape(B, N, C, H, DK)
    k = k.reshape(B, N, C, H, DK)
    v = v.reshape(B, N, C, H, DV)
    beta = beta.reshape(B, N, C, H)
    gc = jnp.cumsum(gdec.reshape(B, N, C, H), axis=2)
    gct = jnp.swapaxes(gc, 2, 3)
    idx = jnp.arange(C)
    lower = idx[:, None] >= idx[None, :]
    strict = idx[:, None] > idx[None, :]
    diff = gct[..., :, None] - gct[..., None, :]
    decay = jnp.where(lower, jnp.exp(jnp.where(lower, diff, 0.0)), 0.0)
    k_beta = k * beta[..., None]
    v_beta = v * beta[..., None]
    kk = jnp.einsum('bnihd,bnjhd->bnhij', k_beta, k) * decay
    eye = jnp.eye(C, dtype=jnp.float32)
    A = eye + jnp.where(strict, kk, 0.0)
    T = lax.linalg.triangular_solve(A, jnp.broadcast_to(eye, A.shape), left_side=True,
                                    lower=True, unit_diagonal=True)
    u = jnp.einsum('bnhij,bnjhd->bnhid', T, v_beta)
    w = jnp.einsum('bnhij,bnjhd->bnhid', T, k_beta * jnp.exp(gc)[..., None])
    qk = jnp.einsum('bnihd,bnjhd->bnhij', q, k) * decay

    def step(S, inp):
        q_n, k_n, u_n, w_n, qk_n, g_n = inp
        v_new = u_n - jnp.einsum('bhid,bhde->bhie', w_n, S)
        o = (jnp.einsum('bihd,bhde->bhie', q_n, S) * jnp.exp(g_n)[..., None]
             + jnp.einsum('bhij,bhje->bhie', qk_n, v_new))
        g_last = g_n[..., -1]
        k_dec = k_n * jnp.swapaxes(jnp.exp(g_last[..., None] - g_n), 1, 2)[..., None]
        S = S * jnp.exp(g_last)[..., None, None] + jnp.einsum('bihd,bhie->bhde', k_dec, v_new)
        return S, o

    xs = (jnp.moveaxis(q, 1, 0), jnp.moveaxis(k, 1, 0), jnp.moveaxis(u, 1, 0),
          jnp.moveaxis(w, 1, 0), jnp.moveaxis(qk, 1, 0), jnp.moveaxis(gct, 1, 0))
    S, o = lax.scan(step, S0, xs)
    o = jnp.transpose(o, (1, 0, 3, 2, 4)).reshape(B, L, H, DV)
    return o, S

def gated_delta_recurrent(q, k, v, gdec, beta, S0):
    def step(S, inp):
        q_t, k_t, v_t, g_t, b_t = inp
        S = S * jnp.exp(g_t)[..., None, None]
        kv = jnp.einsum('bhd,bhde->bhe', k_t, S)
        delta = (v_t - kv) * b_t[..., None]
        S = S + jnp.einsum('bhd,bhe->bhde', k_t, delta)
        o = jnp.einsum('bhd,bhde->bhe', q_t, S)
        return S, o

    xs = (jnp.moveaxis(q, 1, 0), jnp.moveaxis(k, 1, 0), jnp.moveaxis(v, 1, 0),
          jnp.moveaxis(gdec, 1, 0), jnp.moveaxis(beta, 1, 0))
    S, o = lax.scan(step, S0, xs)
    return jnp.moveaxis(o, 0, 1), S

def spatial_gate(u, vb, w_s, b_s):
    B, L, _ = u.shape
    c = min(L, GM_CHUNK)
    idx = jnp.arange(c)
    wm = jnp.where(idx[:, None] >= idx[None, :], w_s[:, :c, :c], 0.0).astype(vb.dtype)
    vc = vb.reshape(B, L // c, c, H_B, DH_B)
    s = jnp.einsum('hij,bnjhd->bnihd', wm, vc) + jnp.swapaxes(b_s[:, :c], 0, 1)[:, :, None].astype(vb.dtype)
    return u * s.reshape(B, L, W_B)

def mixer(h, conv_buf, S0, w_in, conv_w, A_log, dt_bias, o_norm_g, v_norm_g, w_s, b_s, w_o, chunked):
    B, L, _ = h.shape
    p = h @ w_in
    qkv, new_buf = causal_conv(p[..., :QKV_DIM], conv_buf, conv_w)
    qkv = jax.nn.silu(qkv).astype(jnp.float32)
    q = l2norm(qkv[..., :H_A * DK].reshape(B, L, H_A, DK)) * (DK ** -0.5)
    k = l2norm(qkv[..., H_A * DK:2 * H_A * DK].reshape(B, L, H_A, DK))
    v = qkv[..., 2 * H_A * DK:].reshape(B, L, H_A, DV)
    a = p[..., OFF_A:OFF_B].astype(jnp.float32)
    bl = p[..., OFF_B:OFF_U].astype(jnp.float32)
    gdec = -jnp.exp(A_log.astype(jnp.float32)) * jax.nn.softplus(a + dt_bias.astype(jnp.float32))
    beta = jax.nn.sigmoid(bl)
    S0f = S0.astype(jnp.float32)
    if chunked:
        o, S = gated_delta_chunked(q, k, v, gdec, beta, S0f)
    else:
        o, S = gated_delta_recurrent(q, k, v, gdec, beta, S0f)
    gate = p[..., OFF_G:OFF_A].astype(jnp.float32).reshape(B, L, H_A, DV)
    o_a = (rmsnorm(o, o_norm_g) * jax.nn.silu(gate)).reshape(B, L, W_A).astype(h.dtype)
    u = p[..., OFF_U:OFF_V]
    vb = rmsnorm(p[..., OFF_V:], v_norm_g)
    o_b = spatial_gate(u, vb, w_s, b_s)
    y = jnp.concatenate([o_a, o_b], axis=-1) @ w_o
    return y, new_buf, S.astype(S0.dtype), vb

def ffn(h, w_up, w_down):
    return jnp.square(jax.nn.relu(h @ w_up)) @ w_down

def setup_inputs(seed: int = 0) -> dict:
    key = jax.random.key(seed)
    ks = jax.random.split(key, 20)
    f32 = jnp.float32

    def nrm(k, shape, scale):
        return jax.random.normal(k, shape, f32) * scale

    dt = jnp.exp(jax.random.uniform(ks[8], (DEPTH, H_A), f32, math.log(1e-3), math.log(1e-1)))
    return {
        'x_prompt': nrm(ks[0], (BATCH, SEQ, D_MODEL), 1.0),
        'x_sample': nrm(ks[1], (DEC_BATCH, DEC_SEQ, D_MODEL), 1.0),
        'state_delta': nrm(ks[2], (DEPTH, DEC_BATCH, H_A, DK, DV), 0.05),
        'state_conv': nrm(ks[3], (DEPTH, DEC_BATCH, CONV_W - 1, QKV_DIM), 1.0),
        'norm_mix_g': 1.0 + nrm(ks[4], (DEPTH, D_MODEL), 0.05),
        'w_in': nrm(ks[5], (DEPTH, D_MODEL, PROJ_DIM), D_MODEL ** -0.5),
        'conv_w': nrm(ks[6], (DEPTH, CONV_W, QKV_DIM), CONV_W ** -0.5),
        'A_log': jnp.log(jax.random.uniform(ks[7], (DEPTH, H_A), f32, 1.0, 16.0)),
        'dt_bias': dt + jnp.log(-jnp.expm1(-dt)),
        'o_norm_g': 1.0 + nrm(ks[9], (DEPTH, DV), 0.05),
        'v_norm_g': 1.0 + nrm(ks[10], (DEPTH, W_B), 0.05),
        'w_s': nrm(ks[11], (DEPTH, H_B, GM_CHUNK, GM_CHUNK), GM_CHUNK ** -0.5),
        'b_s': 1.0 + nrm(ks[12], (DEPTH, H_B, GM_CHUNK), 0.1),
        'w_o': nrm(ks[13], (DEPTH, MIX_W, D_MODEL), MIX_W ** -0.5),
        'norm_ffn_g': 1.0 + nrm(ks[14], (DEPTH, D_MODEL), 0.05),
        'w_up': nrm(ks[15], (DEPTH, D_MODEL, D_FF), D_MODEL ** -0.5),
        'w_down': nrm(ks[16], (DEPTH, D_FF, D_MODEL), D_FF ** -0.5),
        'norm_f_g': 1.0 + nrm(ks[17], (D_MODEL,), 0.05),
    }

def reference(x_prompt, x_sample, state_delta, state_conv, norm_mix_g, w_in, conv_w, A_log,
              dt_bias, o_norm_g, v_norm_g, w_s, b_s, w_o, norm_ffn_g, w_up, w_down, norm_f_g):
    xp, xs = x_prompt, x_sample
    conv0 = jnp.zeros((xp.shape[0], CONV_W - 1, QKV_DIM), xp.dtype)
    S0p = jnp.zeros((xp.shape[0], H_A, DK, DV), state_delta.dtype)
    dp_list, cp_list, ds_list, cs_list, vs_list = [], [], [], [], []
    for l in range(DEPTH):
        lp = (w_in[l], conv_w[l], A_log[l], dt_bias[l], o_norm_g[l], v_norm_g[l], w_s[l], b_s[l], w_o[l])
        yp, cp, Sp, _ = mixer(rmsnorm(xp, norm_mix_g[l]), conv0, S0p, *lp, chunked=True)
        ys, cs, Ss, vrows = mixer(rmsnorm(xs, norm_mix_g[l]), state_conv[l], state_delta[l], *lp, chunked=False)
        xp = xp + yp
        xs = xs + ys
        xp = xp + ffn(rmsnorm(xp, norm_ffn_g[l]), w_up[l], w_down[l])
        xs = xs + ffn(rmsnorm(xs, norm_ffn_g[l]), w_up[l], w_down[l])
        dp_list.append(Sp)
        cp_list.append(cp)
        ds_list.append(Ss)
        cs_list.append(cs)
        vs_list.append(vrows)
    y_prompt = rmsnorm(xp, norm_f_g)
    y_sample = rmsnorm(xs, norm_f_g)
    new_delta_prompt = jnp.stack(dp_list)
    new_conv_prompt = jnp.stack(cp_list)
    new_delta_sample = jnp.stack(ds_list)
    new_conv_sample = jnp.stack(cs_list)
    new_gmlp_v_sample = jnp.stack(vs_list)
    return (y_prompt, y_sample, new_delta_prompt, new_conv_prompt, new_delta_sample, new_conv_sample, new_gmlp_v_sample)


_drawn_inputs = setup_inputs


def setup_inputs(seed=0):
    import zlib

    import numpy as np

    out = dict(_drawn_inputs(seed))
    spreads = {}
    factors = {'o_norm_g': 3.177}
    for name, (base, spread) in spreads.items():
        noise = np.random.default_rng([zlib.crc32(name.encode()), seed]).standard_normal(out[name].shape)
        drawn = base * np.exp(spread * noise) if base else spread * noise
        out[name] = __import__('jax').numpy.asarray(drawn.astype(out[name].dtype))
    for name, factor in factors.items():
        out[name] = (out[name] * factor).astype(out[name].dtype)
    return out
```

```python
from contextlib import ExitStack

import concourse.bass as bass
from concourse import mybir

F32 = mybir.dt.float32
F32R = mybir.dt.float32r
ALU = mybir.AluOpType
ACT = mybir.ActivationFunctionType
AX = mybir.AxisListType

P = 128
D = 1024
KT = D // P
T = 2048
NCH = T // P
NS = 8
TW = T + NS
H = 4
DK = 128
HW = H * DK
QKV = 3 * HW
OFF_A = QKV + HW
OFF_U = OFF_A + 2 * H
NF = 24
NCONV = QKV // P
FF = 4 * D
BLK = 1024
NBT = BLK // P
GH = 4
NG = FF // P // GH
EPS = 1e-6
LEVELS = 6


def head(ap, h, w=P):
    return ap[:, h * w:(h + 1) * w]


def heads(ap, n=H):
    return ap.rearrange("p (h d) -> p h d", h=n)


def along(ap, w=P):
    return ap.unsqueeze(2).to_broadcast([ap.shape[0], ap.shape[1], w])


def across(ap, n=H):
    return ap.unsqueeze(1).to_broadcast([ap.shape[0], n, ap.shape[1]])


def wait(eng, sem, value):
    if isinstance(value, int) and value <= 0:
        return
    eng.wait_ge(sem, value)


class Own:

    def __init__(self, sem):
        self.sem, self.n = sem, 0

    def did(self, eng, ins):
        self.n += 1
        ins.then_inc(self.sem, 1)
        eng.wait_ge(self.sem, self.n)


def three_pass(pe, out, pairs, start=True, stop=True, skip=False):
    n = len(pairs)
    for k, (wh, wl, xh, xl) in enumerate(pairs):
        pe.matmul(out, wl, xh, start=start and k == 0, stop=False, skip_group_check=skip)
        pe.matmul(out, wh, xl, start=False, stop=False, skip_group_check=skip)
        last = pe.matmul(out, wh, xh, start=False, stop=stop and k == n - 1, skip_group_check=skip)
    return last


def norm_transpose(c, block, st, src, gain, hi, lo, raw, n_iter, rows_extra, extra_src, extra_raw, tag, psum,
                   raw_from_dram=True):
    nc, sb, sem = c.nc, st.sb, c.sem
    NB = 8
    ss = sb(tag + "ss", [P, NB + 1])
    ms = sb(tag + "ms", [P, NB + 1])
    lnv = sb(tag + "lnv", [P, NB + 1])
    r0 = sb(tag + "r0", [P, NB + 1])
    tt = sb(tag + "tt", [P, NB + 1])
    rs = sb(tag + "rs", [P, NB + 1])
    junk = sb(tag + "junk", [P, D])
    xn = sb(tag + "xn", [P, 2, D])
    gb = sb(tag + "gb", [P, D])
    x_loaded = [sem(tag + "x_loaded0"), sem(tag + "x_loaded1")]
    xs_loaded = sem(tag + "xs_loaded")
    gain_loaded = sem(tag + "gain_loaded")
    squared = sem(tag + "squared")
    ms_made = sem(tag + "ms_made")
    ln_made = sem(tag + "ln_made")
    r0_made = sem(tag + "r0_made")
    refine = sem(tag + "refine")
    xn_made = sem(tag + "xn_made")
    turned = sem(tag + "turned")
    hi_made = sem(tag + "hi_made")
    lo_made = sem(tag + "lo_made")
    xsrc = src.rearrange("(i s k p) d -> i s p k d", s=2, k=4, p=P)
    extra = rows_extra > 0
    total = n_iter * NB
    PER = NB

    def sp(eng):
        eng.dma_start(gb[:], gain.to_broadcast([P, D])).then_inc(gain_loaded, 16)
        for i in range(n_iter):
            for s in range(2):
                wait(eng, xn_made, (i - 1) * PER + 4 * s + 4)
                eng.dma_start(raw[:, 4 * s:4 * s + 4, :], xsrc[i, s]).then_inc(x_loaded[s], 16)
        if extra and extra_src is not None:
            eng.dma_start(extra_raw, extra_src).then_inc(xs_loaded, 16)

    def act_stats(eng, i):
        for s in range(2):
            eng.wait_ge(x_loaded[s], (i + 1) * 16)
            for k in range(4 * s, 4 * s + 4):
                eng.wait_ge(squared, i * NB + k + 1)
                eng.activation(junk[:], raw[:, k, :], ACT.Square, accum_out=ss[:, k:k + 1]).then_inc(squared, 1)
        eng.wait_ge(ms_made, i + 1)
        eng.activation(lnv[:, 0:NB], ms[:, 0:NB], ACT.Ln).then_inc(ln_made, 1)
        eng.wait_ge(ln_made, i + 1)
        eng.activation(r0[:, 0:NB], lnv[:, 0:NB], ACT.Exp, scale=-0.5).then_inc(r0_made, 1)

    def act(eng):
        eng.sem_inc(squared, 1)
        with eng.Fori(0, n_iter) as i:
            act_stats(eng, i)
            for k in range(NB):
                for half in range(2):
                    eng.wait_ge(turned, (i * NB + k) * 2 + half + 2)
                    eng.activation(hi[:, 4 * half:4 * half + 4, bass.ds(i * (NB * P) + k * P, P)],
                                   heads(psum[2 * (k % 2) + half][:, :]), ACT.Copy).then_inc(hi_made, 1)
        if extra:
            n = rows_extra
            if extra_src is not None:
                eng.wait_ge(xs_loaded, 16)
            eng.wait_ge(squared, total + 1)
            eng.activation(junk[0:n, :], extra_raw, ACT.Square, accum_out=ss[0:n, NB:NB + 1]).then_inc(squared, 1)
            eng.wait_ge(ms_made, n_iter + 1)
            eng.activation(lnv[0:n, NB:NB + 1], ms[0:n, NB:NB + 1], ACT.Ln).then_inc(ln_made, 1)
            eng.wait_ge(ln_made, n_iter + 1)
            eng.activation(r0[0:n, NB:NB + 1], lnv[0:n, NB:NB + 1], ACT.Exp, scale=-0.5).then_inc(r0_made, 1)
            for half in range(2):
                eng.wait_ge(turned, 2 * total + half + 2)
                eng.activation(hi[:, 4 * half:4 * half + 4, total * P:total * P + n],
                               psum[half][:, 0:4 * n].rearrange("p (k t) -> p k t", k=4), ACT.Copy).then_inc(hi_made, 1)

    def refine_rstd(eng, count, rows, c0, c1):
        eng.wait_ge(r0_made, count + 1)
        eng.tensor_tensor(tt[0:rows, c0:c1], r0[0:rows, c0:c1], r0[0:rows, c0:c1], ALU.mult).then_inc(refine, 1)
        eng.wait_ge(refine, count * 4 + 1)
        eng.tensor_tensor(tt[0:rows, c0:c1], tt[0:rows, c0:c1], ms[0:rows, c0:c1], ALU.mult).then_inc(refine, 1)
        eng.wait_ge(refine, count * 4 + 2)
        eng.tensor_scalar(tt[0:rows, c0:c1], tt[0:rows, c0:c1], -0.5, 1.5, ALU.mult, ALU.add).then_inc(refine, 1)
        eng.wait_ge(refine, count * 4 + 3)
        eng.tensor_tensor(rs[0:rows, c0:c1], r0[0:rows, c0:c1], tt[0:rows, c0:c1], ALU.mult).then_inc(refine, 1)
        eng.wait_ge(refine, count * 4 + 4)

    def dve(eng):
        eng.sem_inc(lo_made, 1)
        eng.wait_ge(gain_loaded, 16)
        with eng.Fori(0, n_iter) as i:
            eng.wait_ge(squared, i * NB + NB + 1)
            eng.tensor_scalar(ms[:, 0:NB], ss[:, 0:NB], 1.0 / D, EPS, ALU.mult, ALU.add).then_inc(ms_made, 1)
            refine_rstd(eng, i, P, 0, NB)

            def make_xn(k):
                if k >= 2:
                    eng.wait_ge(turned, i * (2 * NB) + 2 * (k - 1) + 1)
                else:
                    eng.wait_ge(turned, i * (2 * NB) + 1)
                eng.scalar_tensor_tensor(out=xn[:, k % 2, :], in0=raw[:, k, :], scalar=rs[:, k:k + 1], in1=gb[:],
                                         op0=ALU.mult, op1=ALU.mult).then_inc(xn_made, 1)

            make_xn(0)
            for k in range(NB):
                if k + 1 < NB:
                    make_xn(k + 1)
                for half in range(2):
                    eng.wait_ge(hi_made, (i * NB + k) * 2 + half + 1)
                    cols = bass.ds(i * (NB * P) + k * P, P)
                    eng.tensor_tensor(lo[:, 4 * half:4 * half + 4, cols], heads(psum[2 * (k % 2) + half][:, :]),
                                      hi[:, 4 * half:4 * half + 4, cols].bitcast(F32), ALU.subtract).then_inc(lo_made, 1)
        if extra:
            n = rows_extra
            eng.wait_ge(squared, total + 2)
            eng.tensor_scalar(ms[0:n, NB:NB + 1], ss[0:n, NB:NB + 1], 1.0 / D, EPS, ALU.mult, ALU.add).then_inc(ms_made, 1)
            refine_rstd(eng, n_iter, n, NB, NB + 1)
            eng.wait_ge(turned, 2 * total + 1)
            eng.scalar_tensor_tensor(out=xn[0:n, 0, :], in0=extra_raw, scalar=rs[0:n, NB:NB + 1], in1=gb[0:n, :],
                                     op0=ALU.mult, op1=ALU.mult).then_inc(xn_made, 1)
            for half in range(2):
                eng.wait_ge(hi_made, 2 * total + half + 1)
                cols = slice(total * P, total * P + n)
                eng.tensor_tensor(lo[:, 4 * half:4 * half + 4, cols],
                                  psum[half][:, 0:4 * n].rearrange("p (k t) -> p k t", k=4),
                                  hi[:, 4 * half:4 * half + 4, cols].bitcast(F32), ALU.subtract).then_inc(lo_made, 1)

    def pe(eng):
        eng.sem_inc(turned, 1)
        with eng.Fori(0, n_iter) as i:
            for k in range(NB):
                eng.wait_ge(xn_made, i * NB + k + 1)
                for half in range(2):
                    if k >= 2:
                        eng.wait_ge(lo_made, i * (2 * NB) + 2 * (k - 2) + half + 2)
                    else:
                        eng.wait_ge(lo_made, i * (2 * NB) + 1)
                    for q in range(4):
                        last = eng.transpose(psum[2 * (k % 2) + half][:, q * P:(q + 1) * P],
                                             xn[:, k % 2, (4 * half + q) * P:(4 * half + q + 1) * P], c.ident[:])
                    last.then_inc(turned, 1)
        if extra:
            n = rows_extra
            eng.wait_ge(xn_made, total + 1)
            eng.wait_ge(lo_made, 2 * total + 1)
            for half in range(2):
                for q in range(4):
                    last = eng.transpose(psum[half][:, q * n:(q + 1) * n],
                                         xn[0:n, 0, (4 * half + q) * P:(4 * half + q + 1) * P], c.ident[0:n, 0:n])
                last.then_inc(turned, 1)

    lo_total = 1 + 2 * total + (2 if extra else 0)
    return sp, act, dve, pe, lo_made, lo_total


class Shared:
    pass


class Stage:

    def __init__(self, nc, stack):
        self.nc, self.stack = nc, stack

    def sb(self, name, shape, dt=F32):
        return self.stack.enter_context(self.nc.sbuf_tensor(name, shape, dt))


def constants(c):
    nc = c.nc
    made = c.sem("const_made")
    with nc.Block() as block:
        @block.gpsimd
        def _(pool):
            n = 0

            def did(ins):
                nonlocal n
                n += 1
                ins.then_inc(made, 1)
                pool.wait_ge(made, n)

            did(pool.memset(c.ident[:], 0.0))
            did(pool.affine_select(out=c.ident[:], in_=c.ident[:], compare_op=ALU.not_equal, fill=1.0, base=0,
                                   pattern=[[-1, P]], channel_multiplier=1))
            did(pool.memset(c.ones[:], 1.0))
            did(pool.affine_select(out=c.upto[:], in_=c.ones[:], compare_op=ALU.is_ge, fill=0.0, base=0,
                                   pattern=[[1, P]], channel_multiplier=-1))
            did(pool.memset(c.eye8[:], 0.0))
            did(pool.affine_select(out=c.eye8[:], in_=c.eye8[:], compare_op=ALU.not_equal, fill=1.0, base=0,
                                   pattern=[[1, NS], [-1, NS]], channel_multiplier=0))
            for l in range(LEVELS + 1):
                s = 1 << l
                m = c.masks[:, l, :]
                did(pool.memset(m, -1.0))
                v = m.rearrange("p (g two i) -> p g two i", two=2, i=s)
                did(pool.affine_select(out=v, in_=v, compare_op=ALU.is_ge, fill=0.0, base=0,
                                       pattern=[[-2 * s, P // (2 * s)], [0, 2], [0, s]], channel_multiplier=1))
                did(pool.affine_select(out=v, in_=v, compare_op=ALU.is_ge, fill=0.0, base=s - 1,
                                       pattern=[[2 * s, P // (2 * s)], [0, 2], [0, s]], channel_multiplier=-1))
                did(pool.memset(v[:, :, 0, :], 0.0))


def project(c, io, stack):
    nc, sem, psum = c.nc, c.sem, c.psum
    st = Stage(nc, stack)
    sb = st.sb
    h_hi = sb("h_hi", [P, KT, TW], F32R)
    h_lo = sb("h_lo", [P, KT, TW], F32R)
    with ExitStack() as inner:
        si = Stage(nc, inner)
        raw = si.sb("x_raw", [P, 8, D])
        n_sp, n_act, n_dve, n_pe, _, _ = norm_transpose(
            c, None, si, io["x_prompt"][0], io["norm_mix_g"][0:1, :], h_hi, h_lo, raw, 2, NS,
            io["x_sample"].rearrange("b s d -> (b s) d"), c.x_s[:], "n0_", psum)
        cw_in = si.sb("cw_in", [28, QKV])
        cw_loaded = sem("cw_loaded")
        cw_turned = sem("cw_turned")
        cw_made = sem("cw_made")
        with nc.Block() as block:
            @block.sync
            def _(eng):
                n_sp(eng)
                eng.dma_start(cw_in[0:24, :], io["state_conv"][0].rearrange("b j f -> (b j) f")).then_inc(cw_loaded, 16)
                eng.dma_start(cw_in[24:28, :], io["conv_w"][0]).then_inc(cw_loaded, 16)

            @block.scalar
            def _(eng):
                n_act(eng)

            @block.vector
            def _(eng):
                n_dve(eng)
                eng.wait_ge(cw_turned, 1)
                eng.tensor_copy(c.taps[:], psum[4][:, 0:NCONV * 28].rearrange("p (f r) -> p f r", r=28)).then_inc(cw_made, 1)

            @block.tensor
            def _(eng):
                n_pe(eng)
                eng.wait_ge(cw_loaded, 32)
                for f in range(NCONV):
                    last = eng.transpose(psum[4][:, f * 28:(f + 1) * 28], cw_in[:, f * P:(f + 1) * P], c.ident[0:28, 0:28])
                last.then_inc(cw_turned, 1)

    w_raw = sb("w_raw", [P, 2, KT, P])
    w_hi = [sb(f"w_hi{i}", [P, KT, P], F32R) for i in range(2)]
    w_lo = [sb(f"w_lo{i}", [P, KT, P], F32R) for i in range(2)]
    line = sb("line", [P, 3 + T])
    y = sb("y", [P, T])
    cwt = sb("cwt", [P, 4])
    w_loaded = [sem("w_loaded0"), sem("w_loaded1")]
    whi_made = sem("whi_made")
    wlo_made = sem("wlo_made")
    p_ready = sem("p_ready")
    bank_free = sem("bank_free")
    tail_made = sem("tail_made")
    zeroed = sem("zeroed")
    conv = sem("conv")
    conv_made = sem("conv_made")
    y_made = sem("y_made")
    y_stored = sem("y_stored")
    NB5 = 5
    w_in = io["w_in"][0].rearrange("(k p) n -> p k n", p=P)

    def blocks():
        return [(g, slice(g * 512, (g + 1) * 512), psum[g][:, :]) for g in range(4)] + \
               [(4, slice(T, TW), psum[4][:, 0:NS])]

    with nc.Block() as block:
        @block.sync
        def _(eng):
            for t in range(2):
                eng.dma_start(w_raw[:, t], w_in[:, :, t * P:(t + 1) * P]).then_inc(w_loaded[t], 16)

            eng.sem_inc(y_stored, 16)

            def step(ii, s, off, kind):
                t = ii * 2 + s
                eng.wait_ge(wlo_made, t + 1)
                if off is None and s == 0:
                    eng.dma_start(w_raw[:, 0, :, 0:2 * H], w_in[:, :, OFF_A:OFF_U],
                                  allow_slow_non_contiguous=True).then_inc(w_loaded[0], 16)
                elif off is not None:
                    eng.dma_start(w_raw[:, s], w_in[:, :, bass.ds(ii * (2 * P) + (s + 2) * P + off, P)]).then_inc(w_loaded[s], 16)
                if kind == "conv":
                    eng.wait_ge(y_made, t + 1)
                else:
                    eng.wait_ge(bank_free, t * NB5 + 4 + NB5)
                eng.dma_start(io["p_dram"][bass.ds(t * P, P), :], y[:]).then_inc(y_stored, 16)

            for a, b, off, kind in ((0, 6, 0, "conv"), (6, 7, 0, "plain"), (7, 11, 2 * H, "plain"), (11, 12, None, "plain")):
                with eng.Fori(a, b) as ii:
                    for s in range(2):
                        step(ii, s, off, kind)
            eng.wait_ge(y_stored, NF * 16 + 16)

        def split_hi(eng, ii, s):
            eng.wait_ge(w_loaded[s], ii * 16 + 16)
            wait(eng, p_ready, (ii * 2 + s - 1) * NB5 + 1)
            eng.activation(w_hi[s][:], w_raw[:, s], ACT.Copy).then_inc(whi_made, 1)

        @block.scalar
        def _(eng):
            split_hi(eng, 0, 0)

            def tile(ii, s, kind):
                t = ii * 2 + s
                if s == 0:
                    split_hi(eng, ii, 1)
                else:
                    split_hi(eng, ii + 1, 0)
                if kind == "conv":
                    eng.wait_ge(tail_made, t + 1)
                else:
                    eng.wait_ge(y_stored, t * 16 + 16)
                for g, cols, bank in blocks():
                    eng.wait_ge(p_ready, t * NB5 + g + 2)
                    if g == 4:
                        eng.activation(c.p_s[:, bass.ds(t, 1), :], bank.unsqueeze(1), ACT.Copy).then_inc(bank_free, 1)
                    elif kind == "conv":
                        eng.activation(line[:, 3 + g * 512:3 + (g + 1) * 512], bank, ACT.Copy).then_inc(bank_free, 1)
                    else:
                        eng.activation(y[:, cols], bank, ACT.Silu if kind == "gate" else ACT.Copy).then_inc(bank_free, 1)
                if kind == "conv":
                    eng.wait_ge(conv_made, t + 1)
                    eng.activation(y[:], y[:], ACT.Silu).then_inc(y_made, 1)

            for kind, a, b in (("conv", 0, 6), ("gate", 6, 8), ("plain", 8, 12)):
                with eng.Fori(a, b) as ii:
                    for s in range(2):
                        tile(ii, s, kind)
            for g, cols, bank in blocks():
                eng.wait_ge(p_ready, NF * NB5 + g + 2)
                eng.activation(c.ab[:, cols], bank[0:2 * H, :], ACT.Copy).then_inc(bank_free, 1)

        @block.vector
        def _(eng):
            def split_lo(t, s):
                eng.wait_ge(whi_made, t + 1)
                eng.tensor_tensor(w_lo[s][:], w_raw[:, s], w_hi[s][:].bitcast(F32), ALU.subtract).then_inc(wlo_made, 1)

            eng.memset(line[:, 0:3], 0.0).then_inc(zeroed, 1)
            eng.wait_ge(zeroed, 1)
            eng.sem_inc(tail_made, 1)
            split_lo(0, 0)
            with eng.Fori(0, 6) as ii:
                for s in range(2):
                    t = ii * 2 + s
                    split_lo(t + 1, 1 - s)
                    eng.tensor_copy(cwt[:].unsqueeze(1), c.taps[:, bass.ds(t, 1), 24:28]).then_inc(conv, 1)
                    eng.wait_ge(conv, t * 4 + 1)
                    eng.wait_ge(bank_free, t * NB5 + NB5 + NB5)
                    eng.wait_ge(y_stored, t * 16 + 16)
                    eng.tensor_scalar(y[:], line[:, 0:T], cwt[:, 0:1], None, ALU.mult).then_inc(conv, 1)
                    for j in range(1, 4):
                        eng.wait_ge(conv, t * 4 + 1 + j)
                        ins = eng.scalar_tensor_tensor(out=y[:], in0=line[:, j:j + T], scalar=cwt[:, j:j + 1], in1=y[:],
                                                       op0=ALU.mult, op1=ALU.add)
                        if j == 3:
                            ins.then_inc(conv_made, 1)
                        else:
                            ins.then_inc(conv, 1)
                    eng.tensor_copy(c.tail[:, bass.ds(t, 1), :], line[:, T:T + 3].unsqueeze(1)).then_inc(tail_made, 1)
            with eng.Fori(6, 12) as ii:
                for s in range(2):
                    split_lo(ii * 2 + s + 1, 1 - s)

        @block.tensor
        def _(eng):
            eng.sem_inc(bank_free, NB5)
            eng.sem_inc(p_ready, 1)

            def tile(t, s, m):
                eng.wait_ge(wlo_made, t + 1)
                for g, cols, bank in blocks():
                    eng.wait_ge(bank_free, t * NB5 + g + 1)
                    three_pass(eng, bank[0:m, :], [(w_hi[s][:, k, 0:m], w_lo[s][:, k, 0:m], h_hi[:, k, cols], h_lo[:, k, cols])
                                                   for k in range(KT)]).then_inc(p_ready, 1)
            with eng.Fori(0, 12) as ii:
                for s in range(2):
                    t = ii * 2 + s
                    tile(t, s, P)
            tile(NF, 0, 2 * H)


def load_w_o(c, io, stack):
    nc, sem = c.nc, c.sem
    keep = Stage(nc, stack)
    c.wo_hi = keep.sb("wo_hi", [P, KT, D], F32R)
    c.wo_lo = keep.sb("wo_lo", [P, KT, D], F32R)
    loaded = [sem("wo_loaded0"), sem("wo_loaded1")]
    hi_made, lo_made = sem("wo_hi_made"), sem("wo_lo_made")
    w_o = io["w_o"][0].rearrange("(k p) n -> p k n", p=P)
    with ExitStack() as inner:
        raw = Stage(nc, inner).sb("wo_raw", [P, KT, D])
        with nc.Block() as block:
            @block.sync
            def _(eng):
                for s in range(2):
                    eng.dma_start(raw[:, 4 * s:4 * s + 4, :], w_o[:, 4 * s:4 * s + 4, :]).then_inc(loaded[s], 16)

            @block.scalar
            def _(eng):
                for k in range(KT):
                    eng.wait_ge(loaded[k // 4], 16)
                    eng.activation(c.wo_hi[:, k, :], raw[:, k, :], ACT.Copy).then_inc(hi_made, 1)

            @block.vector
            def _(eng):
                for k in range(KT):
                    eng.wait_ge(hi_made, k + 1)
                    eng.tensor_tensor(c.wo_lo[:, k, :], raw[:, k, :], c.wo_hi[:, k, :].bitcast(F32), ALU.subtract).then_inc(lo_made, 1)


def newton(eng, own, r, r0, ms, tmp):
    own.did(eng, eng.tensor_tensor(tmp, r0, r0, ALU.mult))
    own.did(eng, eng.tensor_tensor(tmp, tmp, ms, ALU.mult))
    own.did(eng, eng.tensor_scalar(tmp, tmp, -0.5, 1.5, ALU.mult, ALU.add))
    own.did(eng, eng.tensor_tensor(r, r0, tmp, ALU.mult))


def softplus_gates(c, block, st, ab_tok, rows, cols, a_log, dtb, g, beta, tag):
    sb, sem = st.sb, c.sem
    shape = [rows, cols, H]
    x, ax, e, l1, eb, nea, eb1 = (sb(tag + n, shape if n != "nea" else [rows, H])
                                  for n in ("x", "ax", "e", "l1", "eb", "nea", "eb1"))
    own_d, own_a = Own(sem(tag + "dve")), Own(sem(tag + "act"))
    x_made, e_made, logs, g_made = sem(tag + "x_made"), sem(tag + "e_made"), sem(tag + "logs"), sem(tag + "g_made")

    def act(eng):
        eng.activation(nea[:], a_log, ACT.Exp).then_inc(e_made, 1)
        eng.wait_ge(x_made, 1)
        own_a.did(eng, eng.activation(e[:], ax[:], ACT.Exp, scale=-1.0))
        eng.activation(eb[:], ab_tok[:, :, H:2 * H], ACT.Exp, scale=-1.0).then_inc(e_made, 1)
        eng.activation(l1[:], e[:], ACT.Ln, bias=1.0).then_inc(logs, 1)

    def dve(eng):
        bc = lambda ap: ap.unsqueeze(1).to_broadcast(shape)
        own_d.did(eng, eng.tensor_tensor(x[:], ab_tok[:, :, 0:H], bc(dtb), ALU.add))
        own_d.did(eng, eng.tensor_scalar(ax[:], x[:], -1.0, None, ALU.mult))
        eng.tensor_tensor(ax[:], ax[:], x[:], ALU.max).then_inc(x_made, 1)
        own_d.did(eng, eng.tensor_scalar(x[:], x[:], 0.0, None, ALU.max))
        eng.wait_ge(e_made, 2)
        own_d.did(eng, eng.tensor_scalar(eb1[:], eb[:], 1.0, None, ALU.add))
        own_d.did(eng, eng.reciprocal(beta, eb1[:]))
        eng.wait_ge(logs, 1)
        own_d.did(eng, eng.tensor_tensor(x[:], x[:], l1[:], ALU.add))
        own_d.did(eng, eng.tensor_tensor(x[:], x[:], bc(nea[:]), ALU.mult))
        eng.tensor_scalar(g, x[:], -1.0, None, ALU.mult).then_inc(g_made, 1)

    return act, dve, g_made


def gates(c, io):
    nc, sem, psum = c.nc, c.sem, c.psum
    with ExitStack() as inner:
        st = Stage(nc, inner)
        al = st.sb("al_b", [P, H])
        dtb = st.sb("dtb_b", [P, H])
        ab_turned, sums, sums_copied, loaded = sem("ab_turned"), sem("sums"), sem("sums_copied"), sem("al_loaded")
        ab_tok = psum[0][:, 0:NCH * 8].rearrange("p (c q) -> p c q", q=8)
        ga = c.ga
        g_flat = st.sb("g_flat", [P, NCH, H])
        dif = st.sb("g_dif", [P, NCH, H])
        own = Own(sem("gates_dve"))
        ga_exp = sem("ga_exp")
        with nc.Block() as block:
            act_g, dve_g, g_made = softplus_gates(c, block, st, ab_tok, P, NCH, al[:], dtb[:], g_flat[:],
                                                  ga[:, :, 1, :], "gp_")

            @block.sync
            def _(eng):
                eng.dma_start(al[:], io["A_log"][0:1, :].to_broadcast([P, H])).then_inc(loaded, 16)
                eng.dma_start(dtb[:], io["dt_bias"][0:1, :].to_broadcast([P, H])).then_inc(loaded, 16)

            @block.tensor
            def _(eng):
                for t in range(NCH):
                    last = eng.transpose(psum[0][:, t * 8:(t + 1) * 8], c.ab[:, t * P:(t + 1) * P], c.ident[0:8, 0:8])
                last.then_inc(ab_turned, 1)
                eng.wait_ge(g_made, 1)
                flat = g_flat[:].rearrange("p c h -> p (c h)")
                eng.matmul(psum[1][:, 0:NCH * H], c.upto[:], flat, start=True, stop=True).then_inc(sums, 1)
                eng.matmul(psum[2][:, 0:NCH * H], c.ones[:], flat, start=True, stop=True).then_inc(sums, 1)

            @block.scalar
            def _(eng):
                eng.wait_ge(loaded, 32)
                eng.wait_ge(ab_turned, 1)
                act_g(eng)
                eng.wait_ge(sums, 2)
                upto = psum[1][:, 0:NCH * H].rearrange("p (c h) -> p c h", h=H)
                total = psum[2][:, 0:NCH * H].rearrange("p (c h) -> p c h", h=H)
                eng.activation(ga[:, :, 3, :], upto, ACT.Exp).then_inc(ga_exp, 1)
                eng.activation(ga[:, :, 5, :], total, ACT.Exp).then_inc(ga_exp, 1)
                eng.wait_ge(sums_copied, 1)
                eng.activation(ga[:, :, 4, :], dif[:], ACT.Exp).then_inc(ga_exp, 1)

            @block.vector
            def _(eng):
                eng.wait_ge(loaded, 32)
                eng.wait_ge(ab_turned, 1)
                dve_g(eng)
                eng.wait_ge(g_made, 1)
                own.did(eng, eng.tensor_copy(ga[:, :, 0, :], g_flat[:]))
                eng.wait_ge(ga_exp, 2)
                own.did(eng, eng.tensor_copy(ga[:, :, 2, :], psum[1][:, 0:NCH * H].rearrange("p (c h) -> p c h", h=H)))
                own.did(eng, eng.tensor_tensor(dif[:], psum[2][:, 0:NCH * H].rearrange("p (c h) -> p c h", h=H),
                                               ga[:, :, 2, :], ALU.subtract))
                eng.tensor_scalar(dif[:], dif[:], 0.0, None, ALU.min).then_inc(sums_copied, 1)


def mix(c, io, stack):
    nc, sem, psum = c.nc, c.sem, c.psum
    st = Stage(nc, stack)
    sb = st.sb
    b0, b1, b2, b3, b4, b5, b6, b7 = (b[:, :] for b in psum)

    pt = sb("pt", [P, NF, P])
    xres = sb("xres", [P, D])
    x1 = sb("x1", [P, D])
    cg = sb("cg", [P, 6, H])
    gu = sb("gu", [P, HW])
    sq = sb("sq", [P, 2 * HW])
    sqv = sb("sqv", [P, HW])
    ss, ms, lnv, r0, rt, rs = (sb("mx_" + n, [P, 9]) for n in ("ss", "ms", "lnv", "r0", "rt", "rs"))
    qn, kn, vt, ut, gg, vbn = (sb(n, [P, HW]) for n in ("qn", "kn", "vt", "ut", "gg", "vbn"))
    kb, kbe, kd, vbt, qe = (sb(n, [P, HW]) for n in ("kb", "kbe", "kd", "vbt", "qe"))
    kT, kbT, qT, qeT = (sb(n, [P, HW]) for n in ("kT", "kbT", "qT", "qeT"))
    dif, em, nt, qkm = (sb(n, [P, HW]) for n in ("dif", "em", "nt", "qkm"))
    tinv, ttinv, xs = (sb(n, [P, HW]) for n in ("tinv", "ttinv", "xs"))
    mt = [sb(f"mt{i}", [P, HW]) for i in range(2)]
    nwT, vn, oa, ob, sqo = (sb(n, [P, HW]) for n in ("nwT", "vn", "oa", "ob", "sqo"))
    oss, oms, oln, or0, ort, ors = (sb("mo_" + n, [P, H]) for n in ("ss", "ms", "lnv", "r0", "rt", "rs"))
    oT_hi = sb("oT_hi", [P, KT, P], F32R)
    oT_lo = sb("oT_lo", [P, KT, P], F32R)
    S = c.S

    names = """pt_loaded xres_loaded x1_stored cg_made gu_made pt_q pt_k pt_v pt_g pt_u pt_b
        qk_squared vb_squared v_copied u_copied ss_made ms_made ln_made r0_made newt rs_made
        qn_made kn_made vbn_made gg_made kb_made pool_made knT kbT_ready qnT qeT_ready kT_made kbT_made qT_made qeT_made
        g_ready dif_made e_made em_made kk_ready qk_ready nt_made qkm_made tt0_part t2_made t2_turned t_copied
        m_made x_ready x_copied y_ready yt_ready t_added tt_added
        wT_ready nwT_made gm_ready vn_ready vn_made o_ready sd_ready s_updated ob_made
        o_squared oss_made oms_made oln_made or0_made onewt ors_made oa_part oa_made
        oT_ready oT_hi_made oT_lo_made wo_ready x1_made S_zeroed""".split()
    s = {n: sem("m_" + n) for n in names}
    pv = io["p_dram"].rearrange("(f p) t -> p f t", p=P)

    def pe_front(pe, c_, n):
        wait(pe, s["pt_loaded"], n * 16)
        wait(pe, s["x_copied"], c_ * LEVELS)
        for h in range(H):
            last = pe.transpose(head(b0, h), pt[:, h, :], c.ident[:])
        last.then_inc(s["pt_q"], 1)
        wait(pe, s["t_added"], c_ * (LEVELS - 1))
        for h in range(H):
            last = pe.transpose(head(b1, h), pt[:, H + h, :], c.ident[:])
        last.then_inc(s["pt_k"], 1)
        wait(pe, s["oa_part"], c_)
        for h in range(H):
            last = pe.transpose(head(b5, h), pt[:, 5 * H + h, :], c.ident[:])
        last.then_inc(s["pt_b"], 1)
        wait(pe, s["tt_added"], c_ * LEVELS)
        for h in range(H):
            last = pe.transpose(head(b2, h), pt[:, 2 * H + h, :], c.ident[:])
        last.then_inc(s["pt_v"], 1)
        wait(pe, s["vn_made"], c_)
        for h in range(H):
            last = pe.transpose(head(b3, h), pt[:, 3 * H + h, :], c.ident[:])
        last.then_inc(s["pt_g"], 1)
        wait(pe, s["nwT_made"], c_)
        for h in range(H):
            last = pe.transpose(head(b4, h), pt[:, 4 * H + h, :], c.ident[:])
        last.then_inc(s["pt_u"], 1)
        pe.wait_ge(s["u_copied"], n)
        pe.wait_ge(s["gu_made"], n)
        pe.matmul(b4, c.ones[:], gu[:], start=True, stop=True).then_inc(s["g_ready"], 1)
        pe.wait_ge(s["qn_made"], n)
        pe.wait_ge(s["kn_made"], n)
        for h in range(H):
            last = pe.transpose(head(b0, h), head(kn, h), c.ident[:])
        last.then_inc(s["knT"], 1)
        pe.wait_ge(s["kb_made"], n)
        for h in range(H):
            last = pe.transpose(head(b1, h), head(kb, h), c.ident[:])
        last.then_inc(s["kbT_ready"], 1)
        pe.wait_ge(s["v_copied"], n)
        for h in range(H):
            last = pe.transpose(head(b2, h), head(qn, h), c.ident[:])
        last.then_inc(s["qnT"], 1)
        pe.wait_ge(s["gg_made"], n)
        pe.wait_ge(s["pool_made"], n * 4)
        for h in range(H):
            last = pe.transpose(head(b3, h), head(qe, h), c.ident[:])
        last.then_inc(s["qeT_ready"], 1)
        pe.wait_ge(s["kT_made"], n)
        pe.wait_ge(s["kbT_made"], n)
        pe.wait_ge(s["vbn_made"], n)
        for h in range(H):
            last = pe.matmul(head(b5, h), head(kT, h), head(kbT, h), start=True, stop=True)
        last.then_inc(s["kk_ready"], 1)
        pe.wait_ge(s["qT_made"], n)
        wait(pe, s["s_updated"], c_)
        for h in range(H):
            last = pe.matmul(head(b6, h), head(kT, h), head(qT, h), start=True, stop=True)
        last.then_inc(s["qk_ready"], 1)
        wait(pe, s["ob_made"], c_)
        pe.wait_ge(s["t2_made"], n)
        for h in range(H):
            last = pe.transpose(head(b7, h), head(ttinv, h), c.ident[:])
        last.then_inc(s["t2_turned"], 1)

    def out_products():
        return [(half, k, q) for half in range(2) for k in range(KT) for q in range(3)]

    def pe_out(pe, count, part):
        if part and part[0] == (0, 0, 0):
            pe.wait_ge(s["oa_made"], count)
            pe.wait_ge(s["ob_made"], count)
            for i, (src, bank) in enumerate(((oa, b4), (ob, b5))):
                for h in range(H):
                    last = pe.transpose(head(bank, h), head(src, h), c.ident[:])
                last.then_inc(s["oT_ready"], 1)
            pe.wait_ge(s["oT_lo_made"], count * 2)
        for half, k, q in part:
            bank = (b6, b7)[half]
            w, o = ((c.wo_lo, oT_hi), (c.wo_hi, oT_lo), (c.wo_hi, oT_hi))[q]
            last = pe.matmul(bank, o[:, k, :], w[:, k, half * 512:(half + 1) * 512],
                             start=(k == 0 and q == 0), stop=(k == KT - 1 and q == 2))
            if k == KT - 1 and q == 2:
                last.then_inc(s["wo_ready"], 1)

    def pe_levels(pe, c_, n, filler):
        todo = out_products() if filler else []
        cuts = [0, 6, 16, 26, 36, 44, 48]
        for l in range(1, LEVELS + 1):
            pe.wait_ge(s["m_made"], c_ * LEVELS + l)
            if l == 1:
                pe.wait_ge(s["t_copied"], n)
                pe.wait_ge(s["kT_made"], n)
            else:
                pe.wait_ge(s["t_added"], c_ * (LEVELS - 1) + l - 1)
            for h in range(H):
                last = pe.matmul(head(b0, h), head(mt[l % 2], h), head(tinv, h), start=True, stop=True)
            last.then_inc(s["x_ready"], 1)
            if filler and l == 1:
                pe.wait_ge(s["dif_made"], n)
                pe.wait_ge(s["nt_made"], n)
                pe.wait_ge(s["qkm_made"], n)
            if filler:
                pe_out(pe, c_, todo[cuts[l - 1]:cuts[l]])
            if l > 1:
                pe.wait_ge(s["tt_added"], c_ * LEVELS + l - 1)
            pe.wait_ge(s["x_copied"], c_ * LEVELS + l)
            if l < LEVELS:
                if l == 1:
                    pe.wait_ge(s["kbT_made"], n)
                for h in range(H):
                    last = pe.matmul(head(b1, h), head(ttinv, h), head(xs, h), start=True, stop=True)
                last.then_inc(s["y_ready"], 1)
            for h in range(H):
                last = pe.matmul(head(b2, h), head(xs, h), head(ttinv, h), start=True, stop=True)
            last.then_inc(s["yt_ready"], 1)

    def pe_tail(pe, c_, n, filler):
        if filler:
            wait(pe, s["x1_made"], c_ * 2)
        for h in range(H):
            last = pe.matmul(head(b7, h), head(c.wsT, h), head(vbn, h), start=True, stop=True)
        last.then_inc(s["gm_ready"], 1)
        pe.wait_ge(s["tt_added"], n * LEVELS)
        for h in range(H):
            last = pe.matmul(head(b4, h), head(kbe, h), head(ttinv, h), start=True, stop=True)
        last.then_inc(s["wT_ready"], 1)
        for h in range(H):
            pe.matmul(head(b3, h), head(ttinv, h), head(vbt, h), start=(h == 0), stop=False, skip_group_check=True)
        if isinstance(c_, int):
            pe.wait_ge(s["S_zeroed"], 1)
        else:
            pe.wait_ge(s["s_updated"], c_)
        for h in range(H):
            pe.matmul(head(b5, h), head(qeT, h), head(S, h), start=(h == 0), stop=False, skip_group_check=True)
        pe.wait_ge(s["nwT_made"], n)
        for h in range(H):
            last = pe.matmul(head(b3, h), head(nwT, h), head(S, h), start=False, stop=(h == H - 1), skip_group_check=True)
        last.then_inc(s["vn_ready"], 1)
        pe.wait_ge(s["vn_made"], n)
        for h in range(H):
            last = pe.matmul(head(b6, h), head(kd, h), head(vn, h), start=True, stop=True)
        last.then_inc(s["sd_ready"], 1)
        for h in range(H):
            last = pe.matmul(head(b5, h), head(qkm, h), head(vn, h), start=False, stop=(h == H - 1), skip_group_check=True)
        last.then_inc(s["o_ready"], 1)

    def dve_front(dve, c_, n):
        dve.tensor_copy(cg[:].unsqueeze(1), c.ga[:, bass.ds(c_, 1), :, :]).then_inc(s["cg_made"], 1)
        dve.wait_ge(s["cg_made"], n)
        dve.tensor_tensor(heads(gu[:]), across(c.upto[:]), along(cg[:, 0, :]), ALU.mult).then_inc(s["gu_made"], 1)
        dve.wait_ge(s["qk_squared"], n)
        dve.tensor_reduce(ss[:, 0:8], sq[:].rearrange("p (n d) -> p n d", d=P), AX.X, ALU.add).then_inc(s["ss_made"], 1)
        dve.wait_ge(s["vb_squared"], n)
        dve.tensor_scalar(ms[:, 8:9], ss[:, 8:9], 1.0 / HW, EPS, ALU.mult, ALU.add).then_inc(s["ms_made"], 1)
        dve.wait_ge(s["ss_made"], n)
        dve.tensor_scalar(ms[:, 0:8], ss[:, 0:8], EPS, None, ALU.add).then_inc(s["ms_made"], 1)
        dve.wait_ge(s["r0_made"], n)
        dve.tensor_tensor(rt[:], r0[:], r0[:], ALU.mult).then_inc(s["newt"], 1)
        dve.wait_ge(s["newt"], c_ * 4 + 1)
        dve.tensor_tensor(rt[:], rt[:], ms[:], ALU.mult).then_inc(s["newt"], 1)
        dve.wait_ge(s["newt"], c_ * 4 + 2)
        dve.tensor_scalar(rt[:], rt[:], -0.5, 1.5, ALU.mult, ALU.add).then_inc(s["newt"], 1)
        dve.wait_ge(s["newt"], c_ * 4 + 3)
        dve.tensor_tensor(rs[:], r0[:], rt[:], ALU.mult).then_inc(s["newt"], 1)
        dve.wait_ge(s["newt"], c_ * 4 + 4)
        dve.tensor_scalar(rs[:, 0:H], rs[:, 0:H], DK ** -0.5, None, ALU.mult).then_inc(s["rs_made"], 1)
        dve.tensor_tensor(heads(kn[:]), heads(b1), along(rs[:, 4:8]), ALU.mult).then_inc(s["kn_made"], 1)
        dve.wait_ge(s["rs_made"], n)
        dve.tensor_tensor(heads(qn[:]), heads(b0), along(rs[:, 0:4]), ALU.mult).then_inc(s["qn_made"], 1)
        dve.wait_ge(s["kn_made"], n)
        dve.tensor_tensor(heads(kb[:]), heads(kn[:]), along(cg[:, 1, :]), ALU.mult).then_inc(s["kb_made"], 1)
        dve.wait_ge(s["g_ready"], n)
        for h in range(H):
            ins = dve.tensor_scalar(head(dif, h), head(b4, h), cg[:, 2, h:h + 1], 0.0, ALU.subtract, ALU.min)
        ins.then_inc(s["dif_made"], 1)
        dve.wait_ge(s["pt_g"], n)
        dve.tensor_tensor(heads(gg[:]), heads(b3), across(c.o_gain[:]), ALU.mult).then_inc(s["gg_made"], 1)
        dve.scalar_tensor_tensor(out=vbn[:], in0=b5, scalar=rs[:, 8:9], in1=c.v_gain[:],
                                 op0=ALU.mult, op1=ALU.mult).then_inc(s["vbn_made"], 1)
        dve.wait_ge(s["e_made"], n)
        dve.tensor_tensor(heads(em[:]), heads(em[:]), across(c.upto[:]), ALU.mult).then_inc(s["em_made"], 1)
        dve.wait_ge(s["em_made"], n)
        dve.wait_ge(s["kk_ready"], n)
        dve.tensor_tensor(nt[:], b5, em[:], ALU.mult).then_inc(s["nt_made"], 1)
        dve.wait_ge(s["nt_made"], n)
        dve.tensor_tensor(heads(ttinv[:]), heads(nt[:]), across(c.masks[:, 0, :]), ALU.mult).then_inc(s["tt0_part"], 1)
        dve.wait_ge(s["tt0_part"], n)
        dve.tensor_tensor(heads(ttinv[:]), heads(ttinv[:]), across(c.ident[:]), ALU.add).then_inc(s["t2_made"], 1)
        dve.wait_ge(s["qk_ready"], n)
        dve.tensor_tensor(qkm[:], b6, em[:], ALU.mult).then_inc(s["qkm_made"], 1)
        dve.wait_ge(s["t2_made"], n)

    def dve_out_turn(dve, count):
        for i, bank in enumerate((b4, b5)):
            dve.wait_ge(s["oT_hi_made"], count * 2 - 1 + i)
            dve.tensor_tensor(oT_lo[:, 4 * i:4 * i + 4, :], heads(bank), oT_hi[:, 4 * i:4 * i + 4, :].bitcast(F32),
                              ALU.subtract).then_inc(s["oT_lo_made"], 1)

    def dve_out_add(dve, count, half):
        dve.wait_ge(s["wo_ready"], count * 2 - 1 + half)
        dve.wait_ge(s["xres_loaded"], count * 16)
        dve.wait_ge(s["x1_stored"], count * 16)
        dve.tensor_tensor(x1[:, half * 512:(half + 1) * 512], (b6, b7)[half], xres[:, half * 512:(half + 1) * 512],
                          ALU.add).then_inc(s["x1_made"], 1)

    def dve_levels(dve, c_, n, filler):
        for l in range(1, LEVELS + 1):
            if filler and l == 1:
                dve_out_turn(dve, c_)
            if l < LEVELS:
                dve.wait_ge(s["y_ready"], c_ * (LEVELS - 1) + l)
                if l == 1:
                    dve.wait_ge(s["t_copied"], n)
                dve.tensor_tensor(tinv[:], b1, tinv[:], ALU.add).then_inc(s["t_added"], 1)
            dve.wait_ge(s["yt_ready"], c_ * LEVELS + l)
            dve.tensor_tensor(ttinv[:], b2, ttinv[:], ALU.add).then_inc(s["tt_added"], 1)
            if l > 1 or True:
                if l < LEVELS:
                    dve.wait_ge(s["t_added"], c_ * (LEVELS - 1) + l)
                dve.wait_ge(s["tt_added"], c_ * LEVELS + l)
            if filler and l == 4:
                dve_out_add(dve, c_, 0)
        if filler:
            dve_out_add(dve, c_, 1)

    def dve_tail(dve, c_, n):
        dve.wait_ge(s["gm_ready"], n)
        for h in range(H):
            ins = dve.scalar_tensor_tensor(out=head(ob, h), in0=head(b7, h), scalar=c.b_col[:, h:h + 1], in1=head(ut, h),
                                           op0=ALU.add, op1=ALU.mult)
        ins.then_inc(s["ob_made"], 1)
        dve.wait_ge(s["vn_ready"], n)
        dve.tensor_copy(vn[:], b3).then_inc(s["vn_made"], 1)
        dve.wait_ge(s["sd_ready"], n)
        for h in range(H):
            ins = dve.scalar_tensor_tensor(out=head(S, h), in0=head(S, h), scalar=cg[:, 5, h:h + 1], in1=head(b6, h),
                                           op0=ALU.mult, op1=ALU.add)
        ins.then_inc(s["s_updated"], 1)
        dve.wait_ge(s["o_squared"], n)
        dve.tensor_reduce(oss[:], heads(sqo[:]), AX.X, ALU.add).then_inc(s["oss_made"], 1)
        dve.wait_ge(s["oss_made"], n)
        dve.tensor_scalar(oms[:], oss[:], 1.0 / DK, EPS, ALU.mult, ALU.add).then_inc(s["oms_made"], 1)
        dve.wait_ge(s["or0_made"], n)
        dve.tensor_tensor(ort[:], or0[:], or0[:], ALU.mult).then_inc(s["onewt"], 1)
        dve.wait_ge(s["onewt"], c_ * 3 + 1)
        dve.tensor_tensor(ort[:], ort[:], oms[:], ALU.mult).then_inc(s["onewt"], 1)
        dve.wait_ge(s["onewt"], c_ * 3 + 2)
        dve.tensor_scalar(ort[:], ort[:], -0.5, 1.5, ALU.mult, ALU.add).then_inc(s["onewt"], 1)
        dve.wait_ge(s["onewt"], c_ * 3 + 3)
        dve.tensor_tensor(ors[:], or0[:], ort[:], ALU.mult).then_inc(s["ors_made"], 1)
        dve.wait_ge(s["ors_made"], n)
        dve.tensor_tensor(heads(oa[:]), heads(b5), along(ors[:]), ALU.mult).then_inc(s["oa_part"], 1)
        dve.wait_ge(s["oa_part"], n)
        dve.tensor_tensor(oa[:], oa[:], gg[:], ALU.mult).then_inc(s["oa_made"], 1)

    def act_front(act, c_, n):
        act.wait_ge(s["pt_q"], n)
        act.activation(sq[:, 0:HW], b0, ACT.Square)
        act.wait_ge(s["pt_k"], n)
        act.activation(sq[:, HW:2 * HW], b1, ACT.Square).then_inc(s["qk_squared"], 1)
        act.wait_ge(s["pt_b"], n)
        act.activation(sqv[:], b5, ACT.Square, accum_out=ss[:, 8:9]).then_inc(s["vb_squared"], 1)
        act.wait_ge(s["ms_made"], n * 2)
        act.activation(lnv[:], ms[:], ACT.Ln).then_inc(s["ln_made"], 1)
        act.wait_ge(s["ln_made"], n)
        act.activation(r0[:], lnv[:], ACT.Exp, scale=-0.5).then_inc(s["r0_made"], 1)
        wait(act, s["ob_made"], c_)
        act.wait_ge(s["pt_u"], n)
        act.activation(ut[:], b4, ACT.Copy).then_inc(s["u_copied"], 1)
        act.wait_ge(s["pt_v"], n)
        act.activation(vt[:], b2, ACT.Copy).then_inc(s["v_copied"], 1)
        act.wait_ge(s["knT"], n)
        act.activation(kT[:], b0, ACT.Copy).then_inc(s["kT_made"], 1)
        act.wait_ge(s["kbT_ready"], n)
        act.activation(kbT[:], b1, ACT.Copy).then_inc(s["kbT_made"], 1)
        act.wait_ge(s["dif_made"], n)
        act.activation(em[:], dif[:], ACT.Exp).then_inc(s["e_made"], 1)
        act.wait_ge(s["qnT"], n)
        act.activation(qT[:], b2, ACT.Copy).then_inc(s["qT_made"], 1)
        act.wait_ge(s["qeT_ready"], n)
        act.activation(qeT[:], b3, ACT.Copy).then_inc(s["qeT_made"], 1)
        act.wait_ge(s["t2_turned"], n)
        act.activation(tinv[:], b7, ACT.Copy).then_inc(s["t_copied"], 1)

    def act_out_turn(act, count):
        for i, bank in enumerate((b4, b5)):
            act.wait_ge(s["oT_ready"], count * 2 - 1 + i)
            act.activation(oT_hi[:, 4 * i:4 * i + 4, :], heads(bank), ACT.Copy).then_inc(s["oT_hi_made"], 1)

    def act_levels(act, c_, n, filler):
        for l in range(1, LEVELS + 1):
            act.wait_ge(s["x_ready"], c_ * LEVELS + l)
            act.activation(xs[:], b0, ACT.Copy).then_inc(s["x_copied"], 1)
            if filler and l == 1:
                act_out_turn(act, c_)

    def act_tail(act, c_, n):
        act.wait_ge(s["wT_ready"], n)
        act.activation(nwT[:], b4, ACT.Copy, scale=-1.0).then_inc(s["nwT_made"], 1)
        act.wait_ge(s["o_ready"], n)
        act.activation(sqo[:], b5, ACT.Square).then_inc(s["o_squared"], 1)
        act.wait_ge(s["oms_made"], n)
        act.activation(oln[:], oms[:], ACT.Ln).then_inc(s["oln_made"], 1)
        act.wait_ge(s["oln_made"], n)
        act.activation(or0[:], oln[:], ACT.Exp, scale=-0.5).then_inc(s["or0_made"], 1)

    def pool_chunk(pool, c_, n):
        pool.wait_ge(s["qn_made"], n)
        pool.tensor_tensor(heads(qe[:]), heads(qn[:]), along(cg[:, 3, :]), ALU.mult).then_inc(s["pool_made"], 1)
        pool.wait_ge(s["kb_made"], n)
        pool.wait_ge(s["v_copied"], n)
        pool.tensor_tensor(heads(kbe[:]), heads(kb[:]), along(cg[:, 3, :]), ALU.mult).then_inc(s["pool_made"], 1)
        pool.tensor_tensor(heads(kd[:]), heads(kn[:]), along(cg[:, 4, :]), ALU.mult).then_inc(s["pool_made"], 1)
        pool.tensor_tensor(heads(vbt[:]), heads(vt[:]), along(cg[:, 1, :]), ALU.mult).then_inc(s["pool_made"], 1)
        pool.wait_ge(s["nt_made"], n)
        for l in range(1, LEVELS + 1):
            wait(pool, s["x_ready"], c_ * LEVELS + l - 2)
            pool.tensor_tensor(heads(mt[l % 2][:]), heads(nt[:]), across(c.masks[:, l, :]), ALU.mult).then_inc(s["m_made"], 1)

    with nc.Block() as block:
        @block.sync
        def _(sp):
            sp.dma_start(pt[:], pv[:, :, 0:P]).then_inc(s["pt_loaded"], 16)
            with sp.Fori(1, NCH) as i:
                sp.wait_ge(s["pt_u"], i)
                sp.dma_start(pt[:], pv[:, :, bass.ds(i * P, P)]).then_inc(s["pt_loaded"], 16)
                sp.dma_start(xres[:], io["x_prompt"][0, bass.ds(i * P - P, P), :]).then_inc(s["xres_loaded"], 16)
                sp.wait_ge(s["x1_made"], i * 2)
                sp.dma_start(io["x1_dram"][bass.ds(i * P - P, P), :], x1[:]).then_inc(s["x1_stored"], 16)
            sp.dma_start(xres[:], io["x_prompt"][0, T - P:T, :]).then_inc(s["xres_loaded"], 16)
            sp.wait_ge(s["x1_made"], NCH * 2)
            sp.dma_start(io["x1_dram"][T - P:T, :], x1[:]).then_inc(s["x1_stored"], 16)
            sp.wait_ge(s["s_updated"], NCH)
            sp.dma_start(io["new_delta_prompt"][0, 0].rearrange("h k v -> k h v"), heads(S[:])).then_inc(s["x1_stored"], 16)
            sp.wait_ge(s["x1_stored"], NCH * 16 + 32)

        @block.tensor
        def _(pe):
            pe_front(pe, 0, 1)
            pe_levels(pe, 0, 1, False)
            pe_tail(pe, 0, 1, False)
            with pe.Fori(1, NCH) as i:
                pe_front(pe, i, i + 1)
                pe_levels(pe, i, i + 1, True)
                pe_tail(pe, i, i + 1, True)
            pe.wait_ge(s["s_updated"], NCH)
            pe_out(pe, NCH, out_products())

        @block.vector
        def _(dve):
            dve.memset(S[:], 0.0).then_inc(s["S_zeroed"], 1)
            dve.wait_ge(s["S_zeroed"], 1)
            dve.sem_inc(s["x1_stored"], 16)
            dve_front(dve, 0, 1)
            dve_levels(dve, 0, 1, False)
            dve_tail(dve, 0, 1)
            with dve.Fori(1, NCH) as i:
                dve_front(dve, i, i + 1)
                dve_levels(dve, i, i + 1, True)
                dve_tail(dve, i, i + 1)
            dve_out_turn(dve, NCH)
            dve_out_add(dve, NCH, 0)
            dve_out_add(dve, NCH, 1)

        @block.scalar
        def _(act):
            act_front(act, 0, 1)
            act_levels(act, 0, 1, False)
            act_tail(act, 0, 1)
            with act.Fori(1, NCH) as i:
                act_front(act, i, i + 1)
                act_levels(act, i, i + 1, True)
                act_tail(act, i, i + 1)
            act_out_turn(act, NCH)

        @block.gpsimd
        def _(pool):
            pool_chunk(pool, 0, 1)
            with pool.Fori(1, NCH) as i:
                pool_chunk(pool, i, i + 1)


def mix_constants(c, io):
    nc, sem, psum = c.nc, c.sem, c.psum
    with ExitStack() as inner:
        st = Stage(nc, inner)
        ws = st.sb("ws", [P, H, P])
        loaded, masked, turned, copied = sem("ws_loaded"), sem("ws_masked"), sem("ws_turned"), sem("ws_copied")
        with nc.Block() as block:
            @block.sync
            def _(eng):
                eng.dma_start(ws[:], io["w_s"][0].rearrange("h i j -> i h j")).then_inc(loaded, 16)
                eng.dma_start(c.b_col[:], io["b_s"][0].rearrange("h i -> i h"), allow_slow_non_contiguous=True).then_inc(loaded, 16)
                eng.dma_start(c.o_gain[:], io["o_norm_g"][0:1, :].to_broadcast([P, P])).then_inc(loaded, 16)
                eng.dma_start(c.v_gain[:], io["v_norm_g"][0:1, :].to_broadcast([P, HW])).then_inc(loaded, 16)

            @block.gpsimd
            def _(eng):
                eng.wait_ge(loaded, 64)
                eng.affine_select(out=ws[:], in_=ws[:], compare_op=ALU.is_ge, fill=0.0, base=0,
                                  pattern=[[0, H], [-1, P]], channel_multiplier=1).then_inc(masked, 1)

            @block.tensor
            def _(eng):
                eng.wait_ge(masked, 1)
                for h in range(H):
                    last = eng.transpose(head(psum[3], h), ws[:, h, :], c.ident[:])
                last.then_inc(turned, 1)

            @block.vector
            def _(eng):
                eng.wait_ge(turned, 1)
                eng.tensor_copy(c.wsT[:], psum[3][:, :]).then_inc(copied, 1)


def sample(c, io, stack):
    nc, sem, psum = c.nc, c.sem, c.psum
    st = Stage(nc, stack)
    sb = st.sb
    N = NS
    names = """states_loaded small_loaded acc_made silu_made raw_turned turned ab_turned tok_made squared ms_made
        ln_made r0_made knT_ready kT_made kv_ready delta_made outer_ready outer_added o_ready osq oms_made oln or0
        o_made oT_ready oT_hi_made oT_lo_made y_ready stored rows_made rest_made eg_ready eg_made masks_made""".split()
    s = {n: sem("s_" + n) for n in names}
    own_d, own_a = Own(sem("s_dve")), Own(sem("s_act"))

    states = sb("states", [P, N * H, DK])
    al, dtb = sb("s_al", [N, H]), sb("s_dtb", [N, H])
    w00, b00 = sb("s_w00", [N, H]), sb("s_b00", [N, H])
    acc, part = sb("s_acc", [P, NCONV, N]), sb("s_part", [P, NCONV, N])
    qkvT, gateT = sb("s_qkvT", [P, NCONV, N]), sb("s_gateT", [P, H, N])
    rows = sb("s_rows", [N, QKV])
    prow = sb("s_prow", [3, QKV])
    tok = [sb(f"s_tok{i}", [N, HW]) for i in range(6)]
    sq = sb("s_sq", [N, 3 * HW])
    ss, ms, lnv, r0, rt, rs = (sb("s_" + n, [N, 9]) for n in ("ss", "ms", "lnv", "r0", "rt", "rs"))
    oss, oms, oln, or0, ort, ors = (sb("so_" + n, [N, H]) for n in ("ss", "ms", "lnv", "r0", "rt", "rs"))
    g, beta, eg = sb("s_g", [N, 1, H]), sb("s_beta", [N, 1, H]), sb("s_eg", [N, H])
    egm, egb = sb("s_egm", [N, N, H]), sb("s_egb", [P, N, H])
    kT, qT = sb("s_kT", [P, H, N]), sb("s_qT", [P, H, N])
    km, qm = sb("s_km", [P, H, N, N]), sb("s_qm", [P, H, N, N])
    delta = sb("s_delta", [N, HW])
    dmask = sb("s_dmask", [N, H, N, DK])
    oa, ob = sb("s_oa", [N, HW]), sb("s_ob", [N, HW])
    og, vg = sb("s_og", [N, HW]), sb("s_vg", [N, HW])
    oT_hi, oT_lo = sb("s_oT_hi", [P, KT, N], F32R), sb("s_oT_lo", [P, KT, N], F32R)
    i8 = c.ident[0:N, 0:N]
    bank = [b[0:N, :] for b in psum]
    act_g, dve_g, g_made = softplus_gates(c, None, st, psum[6][0:N, 0:8].unsqueeze(1), N, 1, al[:], dtb[:],
                                          g[:], beta[:], "gs_")
    st_view = states[:].rearrange("p (b h) v -> p b h v", h=H)

    with nc.Block() as block:
        @block.sync
        def _(eng):
            eng.dma_start(al[:], io["A_log"][0:1, :].to_broadcast([N, H])).then_inc(s["small_loaded"], 16)
            eng.dma_start(dtb[:], io["dt_bias"][0:1, :].to_broadcast([N, H])).then_inc(s["small_loaded"], 16)
            eng.dma_start(w00[:], io["w_s"][0, :, 0, 0:1].rearrange("h o -> o h").to_broadcast([N, H]),
                          allow_slow_non_contiguous=True).then_inc(s["small_loaded"], 16)
            eng.dma_start(b00[:], io["b_s"][0, :, 0:1].rearrange("h o -> o h").to_broadcast([N, H]),
                          allow_slow_non_contiguous=True).then_inc(s["small_loaded"], 16)
            eng.dma_start(states[:], io["state_delta"][0].rearrange("b h k v -> k (b h) v")).then_inc(s["states_loaded"], 16)
            eng.dma_start(io["new_conv_sample"][0, :, 0:2, :], io["state_conv"][0, :, 1:3, :]).then_inc(s["stored"], 16)
            eng.wait_ge(s["rows_made"], 6)
            eng.dma_start(io["new_conv_sample"][0, :, 2, :], rows[:]).then_inc(s["stored"], 16)
            eng.dma_start(io["new_conv_prompt"][0, 0], prow[:]).then_inc(s["stored"], 16)
            eng.wait_ge(s["tok_made"], 1)
            eng.dma_start(io["new_gmlp_v_sample"][0, :, 0, :], tok[5][:]).then_inc(s["stored"], 16)
            eng.wait_ge(s["outer_added"], 8)
            eng.dma_start(io["new_delta_sample"][0].rearrange("b h k v -> k (b h) v"), states[:]).then_inc(s["stored"], 16)
            eng.wait_ge(s["stored"], 16 * 5)

        @block.tensor
        def _(pe):
            for f in range(NCONV):
                pe.transpose(bank[f // 4][:, (f % 4) * P:(f % 4 + 1) * P], c.p_s[:, f, :], c.ident[:])
            for f in range(NCONV):
                last = pe.transpose(psum[3 + f // 4][0:3, (f % 4) * P:(f % 4 + 1) * P], c.tail[:, f, :], c.ident[:])
            last.then_inc(s["raw_turned"], 1)
            pe.transpose(bank[6][:, 0:8], c.ab[:, T:TW], c.ident[0:8, 0:8]).then_inc(s["ab_turned"], 1)
            pe.wait_ge(s["rows_made"], 6)
            pe.wait_ge(s["silu_made"], 2)
            for f in range(NCONV):
                pe.transpose(bank[f // 4][:, (f % 4) * P:(f % 4 + 1) * P], qkvT[:, f, :], c.ident[:])
            for f in range(H):
                pe.transpose(bank[3][:, f * P:(f + 1) * P], gateT[:, f, :], c.ident[:])
            for f in range(2 * H):
                last = pe.transpose(bank[4 + f // 4][:, (f % 4) * P:(f % 4 + 1) * P], c.p_s[:, 4 * H + f, :], c.ident[:])
            last.then_inc(s["turned"], 1)
            pe.wait_ge(s["tok_made"], 1)
            for i, t in enumerate((tok[1], tok[0])):
                for h in range(H):
                    last = pe.transpose(psum[7][:, (i * H + h) * N:(i * H + h + 1) * N], head(t, h), i8)
            last.then_inc(s["knT_ready"], 1)
            pe.wait_ge(s["eg_made"], 1)
            pe.matmul(psum[3][:, 0:N * H], c.ones[0:N, :], egm[:].rearrange("t b h -> t (b h)"), start=True, stop=True).then_inc(s["eg_ready"], 1)
            pe.wait_ge(s["states_loaded"], 16)
            pe.wait_ge(s["masks_made"], 1)
            for h in range(H):
                for b in range(N):
                    last = pe.matmul(head(bank[0], h), km[:, h, b, :], states[:, b * H + h, :], start=(b == 0), stop=(b == N - 1))
            last.then_inc(s["kv_ready"], 1)
            pe.wait_ge(s["delta_made"], 1)
            for h in range(H):
                for half in range(2):
                    u = 2 * h + half
                    wait(pe, s["outer_added"], u - 1)
                    pe.matmul(psum[1 + u % 2][:, :], head(tok[1], h),
                              dmask[:, h, 4 * half:4 * half + 4, :].rearrange("t b v -> t (b v)"),
                              start=True, stop=True).then_inc(s["outer_ready"], 1)
            pe.wait_ge(s["outer_added"], 8)
            for h in range(H):
                for b in range(N):
                    last = pe.matmul(head(bank[0], h), qm[:, h, b, :], states[:, b * H + h, :], start=(b == 0), stop=(b == N - 1))
            last.then_inc(s["o_ready"], 1)
            pe.wait_ge(s["o_made"], 1)
            for i, t in enumerate((oa, ob)):
                for h in range(H):
                    last = pe.transpose(psum[7][:, (i * H + h) * N:(i * H + h + 1) * N], head(t, h), i8)
            last.then_inc(s["oT_ready"], 1)
            pe.wait_ge(s["oT_lo_made"], 1)
            for half in range(2):
                cols = slice(half * 512, (half + 1) * 512)
                three_pass(pe, bank[1 + half], [(oT_hi[:, k, :], oT_lo[:, k, :], c.wo_hi[:, k, cols], c.wo_lo[:, k, cols])
                                                for k in range(KT)]).then_inc(s["y_ready"], 1)

        @block.scalar
        def _(act):
            act.wait_ge(s["small_loaded"], 64)
            act.wait_ge(s["acc_made"], 1)
            act.activation(qkvT[:], acc[:], ACT.Silu).then_inc(s["silu_made"], 1)
            act.activation(gateT[:], c.p_s[:, NCONV:NCONV + H, :], ACT.Silu).then_inc(s["silu_made"], 1)
            act.wait_ge(s["ab_turned"], 1)
            act_g(act)
            act.wait_ge(s["turned"], 1)
            for i, bk in enumerate((0, 1, 5)):
                act.activation(sq[:, i * HW:(i + 1) * HW], bank[bk], ACT.Square).then_inc(s["squared"], 1)
            act.wait_ge(s["ms_made"], 1)
            own_a.did(act, act.activation(lnv[:], ms[:], ACT.Ln))
            act.activation(r0[:], lnv[:], ACT.Exp, scale=-0.5).then_inc(s["r0_made"], 1)
            act.wait_ge(g_made, 1)
            own_a.did(act, act.activation(eg[:], g[:, 0, :], ACT.Exp))
            act.activation(egm[:, 0, :], eg[:], ACT.Copy).then_inc(s["rest_made"], 1)
            act.wait_ge(s["o_ready"], 1)
            act.activation(sq[:, 0:HW], bank[0], ACT.Square).then_inc(s["osq"], 1)
            act.wait_ge(s["oms_made"], 1)
            own_a.did(act, act.activation(oln[:], oms[:], ACT.Ln))
            act.activation(or0[:], oln[:], ACT.Exp, scale=-0.5).then_inc(s["or0"], 1)
            act.wait_ge(s["oT_ready"], 1)
            act.activation(oT_hi[:], psum[7][:, 0:KT * N].rearrange("p (k t) -> p k t", k=KT), ACT.Copy).then_inc(s["oT_hi_made"], 1)

        @block.vector
        def _(dve):
            did = lambda ins: own_d.did(dve, ins)
            old = c.taps[:, :, 0:24].rearrange("p f (b j) -> p f b j", j=3)
            tap = lambda j: c.taps[:, :, 24 + j:25 + j].to_broadcast([P, NCONV, N])
            did(dve.tensor_tensor(acc[:], old[:, :, :, 0], tap(0), ALU.mult))
            for j in (1, 2):
                did(dve.tensor_tensor(part[:], old[:, :, :, j], tap(j), ALU.mult))
                did(dve.tensor_tensor(acc[:], acc[:], part[:], ALU.add))
            did(dve.tensor_tensor(part[:], c.p_s[:, 0:NCONV, :], tap(3), ALU.mult))
            dve.tensor_tensor(acc[:], acc[:], part[:], ALU.add).then_inc(s["acc_made"], 1)
            dve.wait_ge(s["raw_turned"], 1)
            for i in range(3):
                dve.tensor_copy(rows[:, i * 512:(i + 1) * 512], bank[i]).then_inc(s["rows_made"], 1)
                dve.tensor_copy(prow[:, i * 512:(i + 1) * 512], psum[3 + i][0:3, :]).then_inc(s["rows_made"], 1)
            dve.wait_ge(s["small_loaded"], 64)
            dve.wait_ge(s["ab_turned"], 1)
            dve_g(dve)
            dve.wait_ge(s["squared"], 3)
            did(dve.tensor_reduce(ss[:, 0:8], sq[:, 0:2 * HW].rearrange("p (n d) -> p n d", d=P), AX.X, ALU.add))
            did(dve.tensor_reduce(ss[:, 8:9], sq[:, 2 * HW:3 * HW], AX.X, ALU.add))
            did(dve.tensor_scalar(ms[:, 0:8], ss[:, 0:8], EPS, None, ALU.add))
            dve.tensor_scalar(ms[:, 8:9], ss[:, 8:9], 1.0 / HW, EPS, ALU.mult, ALU.add).then_inc(s["ms_made"], 1)
            dve.wait_ge(s["r0_made"], 1)
            newton(dve, own_d, rs[:], r0[:], ms[:], rt[:])
            did(dve.tensor_scalar(rs[:, 0:4], rs[:, 0:4], DK ** -0.5, None, ALU.mult))
            did(dve.tensor_tensor(heads(tok[0][:]), heads(bank[0]), along(rs[:, 0:4]), ALU.mult))
            did(dve.tensor_tensor(heads(tok[1][:]), heads(bank[1]), along(rs[:, 4:8]), ALU.mult))
            did(dve.tensor_copy(tok[2][:], bank[2]))
            did(dve.tensor_tensor(heads(tok[3][:]), heads(bank[3]), across(c.o_gain[0:N, :]), ALU.mult))
            did(dve.tensor_copy(tok[4][:], bank[4]))
            dve.scalar_tensor_tensor(out=tok[5][:], in0=bank[5], scalar=rs[:, 8:9], in1=c.v_gain[0:N, :],
                                     op0=ALU.mult, op1=ALU.mult).then_inc(s["tok_made"], 1)
            dve.wait_ge(s["rest_made"], 1)
            dve.tensor_tensor(egm[:], eg[:].unsqueeze(1).to_broadcast([N, N, H]), along(i8, H), ALU.mult).then_inc(s["eg_made"], 1)
            dve.wait_ge(s["knT_ready"], 1)
            did(dve.tensor_copy(kT[:], psum[7][:, 0:H * N].rearrange("p (h t) -> p h t", h=H)))
            did(dve.tensor_copy(qT[:], psum[7][:, H * N:2 * H * N].rearrange("p (h t) -> p h t", h=H)))
            for h in range(H):
                dve.tensor_tensor(km[:, h], kT[:, h, :].unsqueeze(1).to_broadcast([P, N, N]), c.eye8[:], ALU.mult)
                ins = dve.tensor_tensor(qm[:, h], qT[:, h, :].unsqueeze(1).to_broadcast([P, N, N]), c.eye8[:], ALU.mult)
            ins.then_inc(s["masks_made"], 1)
            dve.wait_ge(s["eg_ready"], 1)
            did(dve.tensor_copy(egb[:], psum[3][:, 0:N * H].rearrange("p (b h) -> p b h", h=H)))
            dve.wait_ge(s["kv_ready"], 1)
            did(dve.tensor_tensor(heads(delta[:]), heads(bank[0]), along(eg[:]), ALU.mult))
            did(dve.tensor_tensor(delta[:], tok[2][:], delta[:], ALU.subtract))
            did(dve.tensor_tensor(heads(delta[:]), heads(delta[:]), along(beta[:, 0, :]), ALU.mult))
            for h in range(H):
                ins = dve.tensor_tensor(dmask[:, h], across(head(delta, h), N), along(i8, DK), ALU.mult)
            ins.then_inc(s["delta_made"], 1)
            for h in range(H):
                for half in range(2):
                    u = 2 * h + half
                    part_s = st_view[:, 4 * half:4 * half + 4, h, :]
                    if u == 0:
                        dve.wait_ge(s["states_loaded"], 16)
                    did(dve.tensor_tensor(part_s, part_s, along(egb[:, 4 * half:4 * half + 4, h], DK), ALU.mult))
                    dve.wait_ge(s["outer_ready"], u + 1)
                    dve.tensor_tensor(part_s, psum[1 + u % 2][:, :].rearrange("p (b v) -> p b v", b=4), part_s,
                                      ALU.add).then_inc(s["outer_added"], 1)
            dve.wait_ge(s["osq"], 1)
            did(dve.tensor_reduce(oss[:], heads(sq[:, 0:HW]), AX.X, ALU.add))
            dve.tensor_scalar(oms[:], oss[:], 1.0 / DK, EPS, ALU.mult, ALU.add).then_inc(s["oms_made"], 1)
            dve.wait_ge(s["or0"], 1)
            newton(dve, own_d, ors[:], or0[:], oms[:], ort[:])
            did(dve.tensor_tensor(heads(oa[:]), heads(bank[0]), along(ors[:]), ALU.mult))
            did(dve.tensor_tensor(oa[:], oa[:], tok[3][:], ALU.mult))
            did(dve.tensor_tensor(heads(ob[:]), heads(tok[5][:]), along(w00[:]), ALU.mult))
            did(dve.tensor_tensor(heads(ob[:]), heads(ob[:]), along(b00[:]), ALU.add))
            dve.tensor_tensor(ob[:], ob[:], tok[4][:], ALU.mult).then_inc(s["o_made"], 1)
            dve.wait_ge(s["oT_hi_made"], 1)
            dve.tensor_tensor(oT_lo[:], psum[7][:, 0:KT * N].rearrange("p (k t) -> p k t", k=KT), oT_hi[:].bitcast(F32),
                              ALU.subtract).then_inc(s["oT_lo_made"], 1)
            for half in range(2):
                cols = slice(half * 512, (half + 1) * 512)
                dve.wait_ge(s["y_ready"], half + 1)
                did(dve.tensor_tensor(c.x_s[:, cols], bank[1 + half], c.x_s[:, cols], ALU.add))


def ffn(c, io, stack, blk):
    c.acc = Stage(c.nc, stack).sb(f"f{blk}_acc", [P, NBT, D])
    with ExitStack() as inner:
        ffn_products(c, io, inner, blk)
    final_norm(c, io, stack, blk)


def ffn_products(c, io, stack, blk):
    nc, sem, psum = c.nc, c.sem, c.psum
    st = Stage(nc, stack)
    sb = st.sb
    tg = f"f{blk}_"
    extra = blk == 1
    n = NS if extra else 0
    W = BLK + n
    acc = c.acc
    h_hi = sb(tg + "h_hi", [P, KT, W], F32R)
    h_lo = sb(tg + "h_lo", [P, KT, W], F32R)
    with ExitStack() as inner:
        n_sp, n_act, n_dve, n_pe, _, _ = norm_transpose(
            c, None, Stage(nc, inner), io["x1_dram"][blk * BLK:(blk + 1) * BLK, :], io["norm_ffn_g"][0:1, :], h_hi, h_lo, acc, 1,
            n, None, c.x_s[:] if extra else None, tg + "n_", psum)
        with nc.Block() as block:
            block.sync(n_sp)
            block.scalar(n_act)
            block.vector(n_dve)
            block.tensor(n_pe)

    up_raw = sb(tg + "up_raw", [P, 2, KT, P])
    dn_raw = sb(tg + "dn_raw", [P, D])
    up_hi = [sb(f"{tg}up_hi{i}", [P, KT, P], F32R) for i in range(2)]
    up_lo = [sb(f"{tg}up_lo{i}", [P, KT, P], F32R) for i in range(2)]
    dn_hi = sb(tg + "dn_hi", [P, GH, D], F32R)
    dn_lo = sb(tg + "dn_lo", [P, GH, D], F32R)
    z_hi = sb(tg + "z_hi", [P, GH, W], F32R)
    z_lo = sb(tg + "z_lo", [P, GH, W], F32R)
    relu = [sb(f"{tg}relu{i}", [P, 512]) for i in range(3 if extra else 2)]
    sqr = sb(tg + "sqr", [P, 512])
    names = """up_loaded0 up_loaded1 dn_loaded up_hi_made up_lo_made dn_hi_made dn_lo_made z_ready relu_made zhi_made
        sqr_made zlo_made y_ready y_added""".split()
    s = {nm: sem(tg + nm) for nm in names}
    up_loaded = [s["up_loaded0"], s["up_loaded1"]]
    w_up = io["w_up"][0].rearrange("(k p) n -> p k n", p=P)
    w_down = io["w_down"][0]
    NZ = 3 if extra else 2
    UN = 2 * NBT + (2 if extra else 0)

    def zblocks(j):
        out = [(b, slice(b * 512, (b + 1) * 512), psum[2 * (j % 2) + b][:, :]) for b in range(2)]
        if extra:
            out.append((2, slice(BLK, W), psum[7][:, 0:n]))
        return out

    def units():
        out = [(u, slice((u // 2) * P, (u // 2 + 1) * P), u % 2, psum[4 + u % 3][:, :],
                acc[:, u // 2, (u % 2) * 512:(u % 2 + 1) * 512]) for u in range(2 * NBT)]
        if extra:
            out += [(u, slice(BLK, W), u % 2, psum[4 + u % 3][0:n, :], c.x_s[:, (u % 2) * 512:(u % 2 + 1) * 512])
                    for u in range(2 * NBT, UN)]
        return out

    with nc.Block() as block:
        @block.sync
        def _(eng):
            for t in range(2):
                eng.dma_start(up_raw[:, t], w_up[:, :, t * P:(t + 1) * P]).then_inc(up_loaded[t], 16)
            eng.dma_start(dn_raw[:], w_down[0:P, :]).then_inc(s["dn_loaded"], 16)

            def step(t, p, up, dn):
                if up:
                    eng.wait_ge(s["up_lo_made"], t + 1)
                    eng.dma_start(up_raw[:, p], w_up[:, :, bass.ds(t * P + 2 * P, P)]).then_inc(up_loaded[p], 16)
                if dn:
                    eng.wait_ge(s["dn_lo_made"], t + 1)
                    eng.dma_start(dn_raw[:], w_down[bass.ds(t * P + P, P), :]).then_inc(s["dn_loaded"], 16)
            NTL = FF // P
            with eng.Fori(0, NTL // 2 - 1) as ii:
                for p in range(2):
                    step(ii * 2 + p, p, True, True)
            step(NTL - 2, 0, False, True)

        def up_hi_cut(act, t, p):
            act.wait_ge(up_loaded[p], (t - p) * 8 + 16)
            wait(act, s["z_ready"], (t - 1) * NZ + 1)
            act.activation(up_hi[p][:], up_raw[:, p], ACT.Copy).then_inc(s["up_hi_made"], 1)

        def act_group(act, gi, last):
            for j in range(GH):
                t = gi * GH + j
                if not (last and j == GH - 1):
                    up_hi_cut(act, t + 1, (j + 1) % 2)
                act.wait_ge(s["dn_loaded"], t * 16 + 16)
                act.wait_ge(s["y_ready"], gi * UN + 1)
                act.activation(dn_hi[:, j, :], dn_raw[:], ACT.Copy).then_inc(s["dn_hi_made"], 1)
                for b, cols, bank in zblocks(j):
                    q = t * NZ + b
                    act.wait_ge(s["z_ready"], q + 2)
                    act.wait_ge(s["sqr_made"], q + 1)
                    rl = relu[b][:, 0:cols.stop - cols.start]
                    act.activation(rl, bank, ACT.Relu).then_inc(s["relu_made"], 1)
                    act.wait_ge(s["relu_made"], q + 1 + 2 * NZ)
                    act.activation(z_hi[:, j, cols], rl, ACT.Square).then_inc(s["zhi_made"], 1)

        @block.scalar
        def _(act):
            up_hi_cut(act, 0, 0)
            with act.Fori(0, NG - 1) as gi:
                act_group(act, gi, False)
            act_group(act, NG - 1, True)

        def up_lo_cut(dve, t, p):
            dve.wait_ge(s["up_hi_made"], t + 1)
            dve.tensor_tensor(up_lo[p][:], up_raw[:, p], up_hi[p][:].bitcast(F32), ALU.subtract).then_inc(s["up_lo_made"], 1)

        def dve_group(dve, gi, last):
            for j in range(GH):
                t = gi * GH + j
                if not (last and j == GH - 1):
                    up_lo_cut(dve, t + 1, (j + 1) % 2)
                dve.wait_ge(s["dn_hi_made"], t + 1)
                dve.tensor_tensor(dn_lo[:, j, :], dn_raw[:], dn_hi[:, j, :].bitcast(F32), ALU.subtract).then_inc(s["dn_lo_made"], 1)
                for b, cols, bank in zblocks(j):
                    q = t * NZ + b
                    m = cols.stop - cols.start
                    dve.wait_ge(s["relu_made"], q + 1 + 2 * NZ)
                    dve.wait_ge(s["zlo_made"], q + 1)
                    dve.tensor_tensor(sqr[:, 0:m], relu[b][:, 0:m], relu[b][:, 0:m], ALU.mult).then_inc(s["sqr_made"], 1)
                    dve.wait_ge(s["zhi_made"], q + 1)
                    dve.wait_ge(s["sqr_made"], q + 3)
                    dve.tensor_tensor(z_lo[:, j, cols], sqr[:, 0:m], z_hi[:, j, cols].bitcast(F32), ALU.subtract).then_inc(s["zlo_made"], 1)
            for u, toks, half, bank, dst in units():
                dve.wait_ge(s["y_ready"], gi * UN + u + 2)
                dve.tensor_tensor(dst, bank, dst, ALU.add).then_inc(s["y_added"], 1)

        @block.vector
        def _(dve):
            dve.sem_inc(s["zlo_made"], 1)
            dve.sem_inc(s["sqr_made"], 2)
            dve.sem_inc(s["y_added"], 1)
            up_lo_cut(dve, 0, 0)
            with dve.Fori(0, NG - 1) as gi:
                dve_group(dve, gi, False)
            dve_group(dve, NG - 1, True)

        def down(pe, unit, js, first, last):
            u, toks, half, bank, _ = unit
            cols = slice(half * 512, (half + 1) * 512)
            return three_pass(pe, bank, [(z_hi[:, j, toks], z_lo[:, j, toks], dn_hi[:, j, cols], dn_lo[:, j, cols]) for j in js],
                              start=first, stop=last)

        def pe_group(pe, gi):
            for j in range(GH):
                t = gi * GH + j
                p = j % 2
                pe.wait_ge(s["up_lo_made"], t + 1)
                for b, cols, bank in zblocks(j):
                    pe.wait_ge(s["relu_made"], t * NZ + b + 1 + (NZ if b == 2 else 0))
                    three_pass(pe, bank, [(up_hi[p][:, k, :], up_lo[p][:, k, :], h_hi[:, k, cols], h_lo[:, k, cols])
                                          for k in range(KT)]).then_inc(s["z_ready"], 1)
            us = units()
            pe.wait_ge(s["zlo_made"], gi * (GH * NZ) + (GH - 1) * NZ + 1)
            pe.wait_ge(s["dn_lo_made"], gi * GH + GH - 1)
            for unit in us[0:3]:
                pe.wait_ge(s["y_added"], gi * UN + 1)
                down(pe, unit, range(GH - 1), True, False)
            pe.wait_ge(s["zlo_made"], gi * (GH * NZ) + GH * NZ + 1)
            pe.wait_ge(s["dn_lo_made"], gi * GH + GH)
            for unit in us[0:3]:
                down(pe, unit, [GH - 1], False, True).then_inc(s["y_ready"], 1)
            for unit in us[3:]:
                pe.wait_ge(s["y_added"], gi * UN + unit[0] - 1)
                down(pe, unit, range(GH), True, True).then_inc(s["y_ready"], 1)

        @block.tensor
        def _(pe):
            pe.sem_inc(s["relu_made"], 2 * NZ)
            pe.sem_inc(s["z_ready"], 1)
            pe.sem_inc(s["y_ready"], 1)
            with pe.Fori(0, NG) as gi:
                pe_group(pe, gi)


def final_norm(c, io, stack, blk):
    nc, sem = c.nc, c.sem
    sb = Stage(nc, stack).sb
    tg = f"f{blk}_"
    extra = blk == 1
    n = NS if extra else 0
    acc = c.acc
    junk, fgain = sb(tg + "junk", [P, D]), sb(tg + "fgain", [P, D])
    fss, fms, fln, fr0, frt, frs = (sb(tg + nm, [P, NBT + 1]) for nm in ("fss", "fms", "fln", "fr0", "frt", "frs"))
    s = {nm: sem(tg + nm) for nm in "f_squared fms_made fr0_made fss_set out_made gain_loaded stored".split()}
    own_d, own_a = Own(sem(tg + "dve")), Own(sem(tg + "act"))
    with nc.Block() as block:
        @block.scalar
        def _(act):
            act.wait_ge(s["fss_set"], 1)
            for m in range(NBT + (1 if extra else 0)):
                src, r = (acc[:, m, :], P) if m < NBT else (c.x_s[:], n)
                wait(act, s["f_squared"], m)
                act.activation(junk[0:r, :], src, ACT.Square, accum_out=fss[0:r, m:m + 1]).then_inc(s["f_squared"], 1)
            act.wait_ge(s["fms_made"], 1)
            own_a.did(act, act.activation(fln[:], fms[:], ACT.Ln))
            act.activation(fr0[:], fln[:], ACT.Exp, scale=-0.5).then_inc(s["fr0_made"], 1)

        @block.vector
        def _(dve):
            dve.memset(fss[:], 1.0).then_inc(s["fss_set"], 1)
            nm = NBT + (1 if extra else 0)
            dve.wait_ge(s["f_squared"], nm)
            dve.tensor_scalar(fms[:], fss[:], 1.0 / D, EPS, ALU.mult, ALU.add).then_inc(s["fms_made"], 1)
            dve.wait_ge(s["fr0_made"], 1)
            newton(dve, own_d, frs[:], fr0[:], fms[:], frt[:])
            dve.wait_ge(s["gain_loaded"], 16)
            for m in range(nm):
                src, r = (acc[:, m, :], P) if m < NBT else (c.x_s[:], n)
                dve.scalar_tensor_tensor(out=src, in0=src, scalar=frs[0:r, m:m + 1], in1=fgain[0:r, :],
                                         op0=ALU.mult, op1=ALU.mult).then_inc(s["out_made"], 1)

        @block.gpsimd
        def _(pool):
            pool.dma_start(fgain[:], io["norm_f_g"].rearrange("(a d) -> a d", a=1).to_broadcast([P, D])).then_inc(s["gain_loaded"], 16)
            for m in range(NBT):
                pool.wait_ge(s["out_made"], m + 1)
                pool.dma_start(io["y_prompt"][0, blk * BLK + m * P:blk * BLK + (m + 1) * P, :], acc[:, m, :]).then_inc(s["stored"], 16)
            if extra:
                pool.wait_ge(s["out_made"], NBT + 1)
                pool.dma_start(io["y_sample"].rearrange("b s d -> (b s) d"), c.x_s[:]).then_inc(s["stored"], 16)
            pool.wait_ge(s["stored"], 16 * (NBT + (1 if extra else 0)))


def build(nc, named):
    with ExitStack() as stack:
        c, io = Shared(), named
        c.nc = nc
        zeroing = []

        def done(st):
            for owner, zero in zeroing:
                if owner is st:
                    zero()
        def use(st):
            mine = []

            def sem(name):
                mine.append(st.enter_context(nc.semaphore(name)))
                return mine[-1]

            def zero():
                nums = sorted(x.num for x in mine)
                runs = []
                for n in nums:
                    if runs and runs[-1][1] == n:
                        runs[-1][1] = n + 1
                    else:
                        runs.append([n, n + 1])
                for a, z in runs:
                    nc.gpsimd.sem_clear(range(a, z))
                nc.all_engine_barrier()
            c.sem = sem
            zeroing.append((st, zero))
        use(stack)
        io["p_dram"] = nc.dram_tensor("p_dram", (NF * P, T), F32).ap()
        io["x1_dram"] = nc.dram_tensor("x1_dram", (T, D), F32).ap()
        c.psum = [stack.enter_context(nc.psum_tensor(f"bank{i}", [P, 512], F32)) for i in range(8)]
        keep = Stage(nc, stack)
        c.ident = keep.sb("ident", [P, P])
        c.x_s = keep.sb("x_s", [NS, D])
        with ExitStack() as mixing:
            keep = Stage(nc, mixing)
            c.ones = keep.sb("ones", [P, P])
            c.upto = keep.sb("upto", [P, P])
            c.masks = keep.sb("masks", [P, LEVELS + 1, P])
            c.eye8 = keep.sb("eye8", [P, NS, NS])
            c.p_s = keep.sb("p_s", [P, NF, NS])
            c.tail = keep.sb("tail", [P, NCONV, 3])
            c.taps = keep.sb("taps", [P, NCONV, 28])
            c.ab = keep.sb("ab", [2 * H, TW])
            constants(c)
            with ExitStack() as s1:
                use(s1)
                project(c, io, s1)
                done(s1)
            with ExitStack() as s2:
                k2 = Stage(nc, s2)
                use(s2)
                c.ga = k2.sb("ga", [P, NCH, 6, H])
                c.S = k2.sb("S", [P, HW])
                c.wsT = k2.sb("wsT", [P, HW])
                c.b_col = k2.sb("b_col", [P, H])
                c.o_gain = k2.sb("o_gain", [P, P])
                c.v_gain = k2.sb("v_gain", [P, HW])
                mix_constants(c, io)
                gates(c, io)
                load_w_o(c, io, s2)
                with ExitStack() as s3:
                    use(s3)
                    mix(c, io, s3)
                    done(s3)
                with ExitStack() as s4:
                    use(s4)
                    sample(c, io, s4)
                    done(s4)
                done(s2)
        for blk in range(T // BLK):
            with ExitStack() as s5:
                use(s5)
                ffn(c, io, s5, blk)
                done(s5)


_INS = ['x_prompt', 'x_sample', 'state_delta', 'state_conv', 'norm_mix_g', 'w_in', 'conv_w', 'A_log', 'dt_bias',
        'o_norm_g', 'v_norm_g', 'w_s', 'b_s', 'w_o', 'norm_ffn_g', 'w_up', 'w_down', 'norm_f_g']
_OUTS = [('y_prompt', (1, 2048, 1024)), ('y_sample', (8, 1, 1024)), ('new_delta_prompt', (1, 1, 4, 128, 128)),
         ('new_conv_prompt', (1, 1, 3, 1536)), ('new_delta_sample', (1, 8, 4, 128, 128)),
         ('new_conv_sample', (1, 8, 3, 1536)), ('new_gmlp_v_sample', (1, 8, 1, 512))]


def kernel(**inputs):
    import numpy as _np
    import concourse.bacc as _bacc
    from concourse import mybir as _mybir
    from concourse.bass_utils import run_bass_kernel_spmd as _run

    nc = _bacc.Bacc("TRN2", target_bir_lowering=False, num_devices=1)
    arrays, io = {}, {}
    for name in _INS:
        a = _np.ascontiguousarray(inputs[name])
        arrays[f"in_{name}_dram"] = a
        io[name] = nc.dram_tensor(f"in_{name}_dram", a.shape, _mybir.dt.from_np(a.dtype), kind="ExternalInput").ap()
    for name, shape in _OUTS:
        io[name] = nc.dram_tensor(f"out_{name}_dram", shape, _mybir.dt.float32, kind="ExternalOutput").ap()
    build(nc, io)
    r = _run(nc, [arrays], core_ids=[0])
    return tuple(r.results[0][f"out_{name}_dram"] for name, _ in _OUTS)
```

```python
from contextlib import ExitStack

import concourse.bass as bass
from concourse import mybir

F32 = mybir.dt.float32
F32R = mybir.dt.float32r
I32 = mybir.dt.int32
ALU = mybir.AluOpType
ACT = mybir.ActivationFunctionType
AX = mybir.AxisListType

P = 128
D = 1024
KT = D // P
T = 2048
NCH = T // P
NS = 8
TW = T + NS
H = 4
DK = 128
HW = H * DK
QKV = 3 * HW
OFF_A = QKV + HW
OFF_U = OFF_A + 2 * H
NF = 24
NCONV = QKV // P
FF = 4 * D
BLK = 1024
NBT = BLK // P
GH = 4
NG = FF // P // GH
EPS = 1e-6
LEVELS = 6


def head(ap, h, w=P):
    return ap[:, h * w:(h + 1) * w]


def heads(ap, n=H):
    return ap.rearrange("p (h d) -> p h d", h=n)


def along(ap, w=P):
    return ap.unsqueeze(2).to_broadcast([ap.shape[0], ap.shape[1], w])


def across(ap, n=H):
    return ap.unsqueeze(1).to_broadcast([ap.shape[0], n, ap.shape[1]])


def wait(eng, sem, value):
    if isinstance(value, int) and value <= 0:
        return
    eng.wait_ge(sem, value)


class Own:

    def __init__(self, sem):
        self.sem, self.n = sem, 0

    def did(self, eng, ins):
        self.n += 1
        ins.then_inc(self.sem, 1)
        eng.wait_ge(self.sem, self.n)


RSQRT_STEPS = 13


def rsqrt(dve, sem, base, r, m, tmp):
    n = 0

    def did(ins):
        nonlocal n
        n += 1
        ins.then_inc(sem, 1)
        dve.wait_ge(sem, base + n)

    did(dve.tensor_scalar(r.bitcast(I32), m.bitcast(I32), -0.5, float(0x5F3759DF), ALU.mult, ALU.add))
    for _ in range(3):
        did(dve.tensor_tensor(tmp, r, r, ALU.mult))
        did(dve.tensor_tensor(tmp, tmp, m, ALU.mult))
        did(dve.tensor_scalar(tmp, tmp, -0.5, 1.5, ALU.mult, ALU.add))
        did(dve.tensor_tensor(r, r, tmp, ALU.mult))


def three_pass(pe, out, pairs, start=True, stop=True, skip=False):
    n = len(pairs)
    for k, (wh, wl, xh, xl) in enumerate(pairs):
        pe.matmul(out, wl, xh, start=start and k == 0, stop=False, skip_group_check=skip)
        pe.matmul(out, wh, xl, start=False, stop=False, skip_group_check=skip)
        last = pe.matmul(out, wh, xh, start=False, stop=stop and k == n - 1, skip_group_check=skip)
    return last


def norm_transpose(c, block, st, src, gain, hi, lo, raw, n_iter, rows_extra, extra_src, extra_raw, tag, psum,
                   raw_from_dram=True):
    nc, sb, sem = c.nc, st.sb, c.sem
    NB = 8
    ss = sb(tag + "ss", [P, NB + 1])
    ms = sb(tag + "ms", [P, NB + 1])
    tt = sb(tag + "tt", [P, NB + 1])
    rs = sb(tag + "rs", [P, NB + 1])
    junk = sb(tag + "junk", [P, D])
    xn = sb(tag + "xn", [P, 2, D])
    gb = sb(tag + "gb", [P, D])
    x_loaded = [sem(tag + "x_loaded0"), sem(tag + "x_loaded1")]
    xs_loaded = sem(tag + "xs_loaded")
    gain_loaded = sem(tag + "gain_loaded")
    squared = sem(tag + "squared")
    ms_made = sem(tag + "ms_made")
    refine = sem(tag + "refine")
    xn_made = sem(tag + "xn_made")
    turned = sem(tag + "turned")
    hi_made = sem(tag + "hi_made")
    lo_made = sem(tag + "lo_made")
    xsrc = src.rearrange("(i s k p) d -> i s p k d", s=2, k=4, p=P)
    extra = rows_extra > 0
    total = n_iter * NB
    PER = NB

    def sp(eng):
        eng.dma_start(gb[:], gain.to_broadcast([P, D])).then_inc(gain_loaded, 16)
        for i in range(n_iter):
            for s in range(2):
                wait(eng, xn_made, (i - 1) * PER + 4 * s + 4)
                eng.dma_start(raw[:, 4 * s:4 * s + 4, :], xsrc[i, s]).then_inc(x_loaded[s], 16)
        if extra and extra_src is not None:
            eng.dma_start(extra_raw, extra_src).then_inc(xs_loaded, 16)

    def act_stats(eng, i):
        for s in range(2):
            eng.wait_ge(x_loaded[s], (i + 1) * 16)
            for k in range(4 * s, 4 * s + 4):
                eng.wait_ge(squared, i * NB + k + 1)
                eng.activation(junk[:], raw[:, k, :], ACT.Square, accum_out=ss[:, k:k + 1]).then_inc(squared, 1)

    def act(eng):
        eng.sem_inc(squared, 1)
        with eng.Fori(0, n_iter) as i:
            act_stats(eng, i)
            for k in range(NB):
                for half in range(2):
                    eng.wait_ge(turned, (i * NB + k) * 2 + half + 2)
                    eng.activation(hi[:, 4 * half:4 * half + 4, bass.ds(i * (NB * P) + k * P, P)],
                                   heads(psum[2 * (k % 2) + half][:, :]), ACT.Copy).then_inc(hi_made, 1)
        if extra:
            n = rows_extra
            if extra_src is not None:
                eng.wait_ge(xs_loaded, 16)
            eng.wait_ge(squared, total + 1)
            eng.activation(junk[0:n, :], extra_raw, ACT.Square, accum_out=ss[0:n, NB:NB + 1]).then_inc(squared, 1)
            for half in range(2):
                eng.wait_ge(turned, 2 * total + half + 2)
                eng.activation(hi[:, 4 * half:4 * half + 4, total * P:total * P + n],
                               psum[half][:, 0:4 * n].rearrange("p (k t) -> p k t", k=4), ACT.Copy).then_inc(hi_made, 1)

    def dve(eng):
        eng.sem_inc(lo_made, 1)
        eng.wait_ge(gain_loaded, 16)
        with eng.Fori(0, n_iter) as i:
            eng.wait_ge(squared, i * NB + NB + 1)
            eng.tensor_scalar(ms[:, 0:NB], ss[:, 0:NB], 1.0 / D, EPS, ALU.mult, ALU.add).then_inc(ms_made, 1)
            eng.wait_ge(ms_made, i + 1)
            rsqrt(eng, refine, i * RSQRT_STEPS, rs[:, 0:NB], ms[:, 0:NB], tt[:, 0:NB])

            def make_xn(k):
                if k >= 2:
                    eng.wait_ge(turned, i * (2 * NB) + 2 * (k - 1) + 1)
                else:
                    eng.wait_ge(turned, i * (2 * NB) + 1)
                eng.scalar_tensor_tensor(out=xn[:, k % 2, :], in0=raw[:, k, :], scalar=rs[:, k:k + 1], in1=gb[:],
                                         op0=ALU.mult, op1=ALU.mult).then_inc(xn_made, 1)

            make_xn(0)
            for k in range(NB):
                if k + 1 < NB:
                    make_xn(k + 1)
                for half in range(2):
                    eng.wait_ge(hi_made, (i * NB + k) * 2 + half + 1)
                    cols = bass.ds(i * (NB * P) + k * P, P)
                    eng.tensor_tensor(lo[:, 4 * half:4 * half + 4, cols], heads(psum[2 * (k % 2) + half][:, :]),
                                      hi[:, 4 * half:4 * half + 4, cols].bitcast(F32), ALU.subtract).then_inc(lo_made, 1)
        if extra:
            n = rows_extra
            eng.wait_ge(squared, total + 2)
            eng.tensor_scalar(ms[0:n, NB:NB + 1], ss[0:n, NB:NB + 1], 1.0 / D, EPS, ALU.mult, ALU.add).then_inc(ms_made, 1)
            eng.wait_ge(ms_made, n_iter + 1)
            rsqrt(eng, refine, n_iter * RSQRT_STEPS, rs[0:n, NB:NB + 1], ms[0:n, NB:NB + 1], tt[0:n, NB:NB + 1])
            eng.wait_ge(turned, 2 * total + 1)
            eng.scalar_tensor_tensor(out=xn[0:n, 0, :], in0=extra_raw, scalar=rs[0:n, NB:NB + 1], in1=gb[0:n, :],
                                     op0=ALU.mult, op1=ALU.mult).then_inc(xn_made, 1)
            for half in range(2):
                eng.wait_ge(hi_made, 2 * total + half + 1)
                cols = slice(total * P, total * P + n)
                eng.tensor_tensor(lo[:, 4 * half:4 * half + 4, cols],
                                  psum[half][:, 0:4 * n].rearrange("p (k t) -> p k t", k=4),
                                  hi[:, 4 * half:4 * half + 4, cols].bitcast(F32), ALU.subtract).then_inc(lo_made, 1)

    def pe(eng):
        eng.sem_inc(turned, 1)
        with eng.Fori(0, n_iter) as i:
            for k in range(NB):
                eng.wait_ge(xn_made, i * NB + k + 1)
                for half in range(2):
                    if k >= 2:
                        eng.wait_ge(lo_made, i * (2 * NB) + 2 * (k - 2) + half + 2)
                    else:
                        eng.wait_ge(lo_made, i * (2 * NB) + 1)
                    for q in range(4):
                        last = eng.transpose(psum[2 * (k % 2) + half][:, q * P:(q + 1) * P],
                                             xn[:, k % 2, (4 * half + q) * P:(4 * half + q + 1) * P], c.ident[:])
                    last.then_inc(turned, 1)
        if extra:
            n = rows_extra
            eng.wait_ge(xn_made, total + 1)
            eng.wait_ge(lo_made, 2 * total + 1)
            for half in range(2):
                for q in range(4):
                    last = eng.transpose(psum[half][:, q * n:(q + 1) * n],
                                         xn[0:n, 0, (4 * half + q) * P:(4 * half + q + 1) * P], c.ident[0:n, 0:n])
                last.then_inc(turned, 1)

    lo_total = 1 + 2 * total + (2 if extra else 0)
    return sp, act, dve, pe, lo_made, lo_total


class Shared:
    pass


class Stage:

    def __init__(self, nc, stack):
        self.nc, self.stack = nc, stack

    def sb(self, name, shape, dt=F32):
        return self.stack.enter_context(self.nc.sbuf_tensor(name, shape, dt))


def constants(c):
    nc = c.nc
    made = c.sem("const_made")
    with nc.Block() as block:
        @block.gpsimd
        def _(pool):
            n = 0

            def did(ins):
                nonlocal n
                n += 1
                ins.then_inc(made, 1)
                pool.wait_ge(made, n)

            did(pool.memset(c.ident[:], 0.0))
            did(pool.affine_select(out=c.ident[:], in_=c.ident[:], compare_op=ALU.not_equal, fill=1.0, base=0,
                                   pattern=[[-1, P]], channel_multiplier=1))
            did(pool.memset(c.ones[:], 1.0))
            did(pool.affine_select(out=c.upto[:], in_=c.ones[:], compare_op=ALU.is_ge, fill=0.0, base=0,
                                   pattern=[[1, P]], channel_multiplier=-1))
            did(pool.memset(c.eye8[:], 0.0))
            did(pool.affine_select(out=c.eye8[:], in_=c.eye8[:], compare_op=ALU.not_equal, fill=1.0, base=0,
                                   pattern=[[1, NS], [-1, NS]], channel_multiplier=0))
            for l in range(LEVELS + 1):
                s = 1 << l
                m = c.masks[:, l, :]
                did(pool.memset(m, -1.0))
                v = m.rearrange("p (g two i) -> p g two i", two=2, i=s)
                did(pool.affine_select(out=v, in_=v, compare_op=ALU.is_ge, fill=0.0, base=0,
                                       pattern=[[-2 * s, P // (2 * s)], [0, 2], [0, s]], channel_multiplier=1))
                did(pool.affine_select(out=v, in_=v, compare_op=ALU.is_ge, fill=0.0, base=s - 1,
                                       pattern=[[2 * s, P // (2 * s)], [0, 2], [0, s]], channel_multiplier=-1))
                did(pool.memset(v[:, :, 0, :], 0.0))


def project(c, io, stack):
    nc, sem, psum = c.nc, c.sem, c.psum
    st = Stage(nc, stack)
    sb = st.sb
    h_hi = sb("h_hi", [P, KT, TW], F32R)
    h_lo = sb("h_lo", [P, KT, TW], F32R)
    with ExitStack() as inner:
        si = Stage(nc, inner)
        raw = si.sb("x_raw", [P, 8, D])
        n_sp, n_act, n_dve, n_pe, _, _ = norm_transpose(
            c, None, si, io["x_prompt"][0], io["norm_mix_g"][0:1, :], h_hi, h_lo, raw, 2, NS,
            io["x_sample"].rearrange("b s d -> (b s) d"), c.x_s[:], "n0_", psum)
        cw_in = si.sb("cw_in", [28, QKV])
        cw_loaded = sem("cw_loaded")
        cw_turned = sem("cw_turned")
        cw_made = sem("cw_made")
        with nc.Block() as block:
            @block.sync
            def _(eng):
                n_sp(eng)
                eng.dma_start(cw_in[0:24, :], io["state_conv"][0].rearrange("b j f -> (b j) f")).then_inc(cw_loaded, 16)
                eng.dma_start(cw_in[24:28, :], io["conv_w"][0]).then_inc(cw_loaded, 16)

            @block.scalar
            def _(eng):
                n_act(eng)

            @block.vector
            def _(eng):
                n_dve(eng)
                eng.wait_ge(cw_turned, 1)
                eng.tensor_copy(c.taps[:], psum[4][:, 0:NCONV * 28].rearrange("p (f r) -> p f r", r=28)).then_inc(cw_made, 1)

            @block.tensor
            def _(eng):
                n_pe(eng)
                eng.wait_ge(cw_loaded, 32)
                for f in range(NCONV):
                    last = eng.transpose(psum[4][:, f * 28:(f + 1) * 28], cw_in[:, f * P:(f + 1) * P], c.ident[0:28, 0:28])
                last.then_inc(cw_turned, 1)

    w_raw = sb("w_raw", [P, 2, KT, P])
    w_hi = [sb(f"w_hi{i}", [P, KT, P], F32R) for i in range(2)]
    w_lo = [sb(f"w_lo{i}", [P, KT, P], F32R) for i in range(2)]
    line = sb("line", [P, 3 + T])
    y = sb("y", [P, T])
    cwt = sb("cwt", [P, 4])
    w_loaded = [sem("w_loaded0"), sem("w_loaded1")]
    whi_made = sem("whi_made")
    wlo_made = sem("wlo_made")
    p_ready = sem("p_ready")
    bank_free = sem("bank_free")
    tail_made = sem("tail_made")
    zeroed = sem("zeroed")
    conv = sem("conv")
    conv_made = sem("conv_made")
    y_made = sem("y_made")
    y_stored = sem("y_stored")
    NB5 = 5
    WB = 412
    w_in = io["w_in"][0].rearrange("(k p) n -> p k n", p=P)

    def blocks():
        out = []
        for g in range(NB5):
            cols = slice(g * WB, min((g + 1) * WB, TW))
            out.append((g, cols, psum[g][:, 0:cols.stop - cols.start]))
        return out

    with nc.Block() as block:
        @block.sync
        def _(eng):
            for t in range(2):
                eng.dma_start(w_raw[:, t], w_in[:, :, t * P:(t + 1) * P]).then_inc(w_loaded[t], 16)

            eng.sem_inc(y_stored, 16)

            def step(ii, s, off, kind):
                t = ii * 2 + s
                eng.wait_ge(wlo_made, t + 1)
                if off is None and s == 0:
                    eng.dma_start(w_raw[:, 0, :, 0:2 * H], w_in[:, :, OFF_A:OFF_U],
                                  allow_slow_non_contiguous=True).then_inc(w_loaded[0], 16)
                elif off is not None:
                    eng.dma_start(w_raw[:, s], w_in[:, :, bass.ds(ii * (2 * P) + (s + 2) * P + off, P)]).then_inc(w_loaded[s], 16)
                if kind == "conv":
                    eng.wait_ge(y_made, t + 1)
                else:
                    eng.wait_ge(bank_free, t * NB5 + NB5 + NB5)
                eng.dma_start(io["p_dram"][bass.ds(t * P, P), :], y[:]).then_inc(y_stored, 16)

            for a, b, off, kind in ((0, 6, 0, "conv"), (6, 7, 0, "plain"), (7, 11, 2 * H, "plain"), (11, 12, None, "plain")):
                with eng.Fori(a, b) as ii:
                    for s in range(2):
                        step(ii, s, off, kind)
            eng.wait_ge(y_stored, NF * 16 + 16)

        def split_hi(eng, ii, s):
            eng.wait_ge(w_loaded[s], ii * 16 + 16)
            wait(eng, p_ready, (ii * 2 + s - 1) * NB5 + 1)
            eng.activation(w_hi[s][:], w_raw[:, s], ACT.Copy).then_inc(whi_made, 1)

        @block.scalar
        def _(eng):
            split_hi(eng, 0, 0)

            def tile(ii, s, kind):
                t = ii * 2 + s
                if s == 0:
                    split_hi(eng, ii, 1)
                else:
                    split_hi(eng, ii + 1, 0)
                if kind == "conv":
                    eng.wait_ge(tail_made, t + 1)
                else:
                    eng.wait_ge(y_stored, t * 16 + 16)
                for g, cols, bank in blocks():
                    eng.wait_ge(p_ready, t * NB5 + g + 2)
                    m = min(cols.stop, T) - cols.start
                    if kind == "conv":
                        ins = eng.activation(line[:, 3 + cols.start:3 + cols.start + m], bank[:, 0:m], ACT.Copy)
                    else:
                        ins = eng.activation(y[:, cols.start:cols.start + m], bank[:, 0:m],
                                             ACT.Silu if kind == "gate" else ACT.Copy)
                    if g == NB5 - 1:
                        ins = eng.activation(c.p_s[:, bass.ds(t, 1), :], bank[:, m:].unsqueeze(1), ACT.Copy)
                    ins.then_inc(bank_free, 1)
                if kind == "conv":
                    eng.wait_ge(conv_made, t + 1)
                    eng.activation(y[:], y[:], ACT.Silu).then_inc(y_made, 1)

            for kind, a, b in (("conv", 0, 6), ("gate", 6, 8), ("plain", 8, 12)):
                with eng.Fori(a, b) as ii:
                    for s in range(2):
                        tile(ii, s, kind)
            for g, cols, bank in blocks():
                eng.wait_ge(p_ready, NF * NB5 + g + 2)
                eng.activation(c.ab[:, cols], bank[0:2 * H, :], ACT.Copy).then_inc(bank_free, 1)

        @block.vector
        def _(eng):
            def split_lo(t, s):
                eng.wait_ge(whi_made, t + 1)
                eng.tensor_tensor(w_lo[s][:], w_raw[:, s], w_hi[s][:].bitcast(F32), ALU.subtract).then_inc(wlo_made, 1)

            eng.memset(line[:, 0:3], 0.0).then_inc(zeroed, 1)
            eng.wait_ge(zeroed, 1)
            eng.sem_inc(tail_made, 1)
            split_lo(0, 0)
            with eng.Fori(0, 6) as ii:
                for s in range(2):
                    t = ii * 2 + s
                    split_lo(t + 1, 1 - s)
                    eng.tensor_copy(cwt[:].unsqueeze(1), c.taps[:, bass.ds(t, 1), 24:28]).then_inc(conv, 1)
                    eng.wait_ge(conv, t * 4 + 1)
                    eng.wait_ge(bank_free, t * NB5 + NB5 + NB5)
                    eng.wait_ge(y_stored, t * 16 + 16)
                    eng.tensor_scalar(y[:], line[:, 0:T], cwt[:, 0:1], None, ALU.mult).then_inc(conv, 1)
                    for j in range(1, 4):
                        eng.wait_ge(conv, t * 4 + 1 + j)
                        ins = eng.scalar_tensor_tensor(out=y[:], in0=line[:, j:j + T], scalar=cwt[:, j:j + 1], in1=y[:],
                                                       op0=ALU.mult, op1=ALU.add)
                        if j == 3:
                            ins.then_inc(conv_made, 1)
                        else:
                            ins.then_inc(conv, 1)
                    eng.tensor_copy(c.tail[:, bass.ds(t, 1), :], line[:, T:T + 3].unsqueeze(1)).then_inc(tail_made, 1)
            with eng.Fori(6, 12) as ii:
                for s in range(2):
                    split_lo(ii * 2 + s + 1, 1 - s)

        @block.tensor
        def _(eng):
            eng.sem_inc(bank_free, NB5)
            eng.sem_inc(p_ready, 1)

            def tile(t, s, m):
                eng.wait_ge(wlo_made, t + 1)
                for g, cols, bank in blocks():
                    eng.wait_ge(bank_free, t * NB5 + g + 1)
                    three_pass(eng, bank[0:m, :], [(w_hi[s][:, k, 0:m], w_lo[s][:, k, 0:m], h_hi[:, k, cols], h_lo[:, k, cols])
                                                   for k in range(KT)]).then_inc(p_ready, 1)
            with eng.Fori(0, 12) as ii:
                for s in range(2):
                    t = ii * 2 + s
                    tile(t, s, P)
            tile(NF, 0, 2 * H)


def load_w_o(c, io, stack):
    nc, sem = c.nc, c.sem
    keep = Stage(nc, stack)
    c.wo_hi = keep.sb("wo_hi", [P, KT, D], F32R)
    c.wo_lo = keep.sb("wo_lo", [P, KT, D], F32R)
    loaded = [sem("wo_loaded0"), sem("wo_loaded1")]
    hi_made, lo_made = sem("wo_hi_made"), sem("wo_lo_made")
    w_o = io["w_o"][0].rearrange("(k p) n -> p k n", p=P)
    with ExitStack() as inner:
        raw = Stage(nc, inner).sb("wo_raw", [P, KT, D])
        with nc.Block() as block:
            @block.sync
            def _(eng):
                for s in range(2):
                    eng.dma_start(raw[:, 4 * s:4 * s + 4, :], w_o[:, 4 * s:4 * s + 4, :]).then_inc(loaded[s], 16)

            @block.scalar
            def _(eng):
                for k in range(KT):
                    eng.wait_ge(loaded[k // 4], 16)
                    eng.activation(c.wo_hi[:, k, :], raw[:, k, :], ACT.Copy).then_inc(hi_made, 1)

            @block.vector
            def _(eng):
                for k in range(KT):
                    eng.wait_ge(hi_made, k + 1)
                    eng.tensor_tensor(c.wo_lo[:, k, :], raw[:, k, :], c.wo_hi[:, k, :].bitcast(F32), ALU.subtract).then_inc(lo_made, 1)


def softplus_gates(c, block, st, ab_tok, rows, cols, a_log, dtb, g, beta, tag):
    sb, sem = st.sb, c.sem
    shape = [rows, cols, H]
    x, ax, e, l1, eb, nea, eb1 = (sb(tag + n, shape if n != "nea" else [rows, H])
                                  for n in ("x", "ax", "e", "l1", "eb", "nea", "eb1"))
    own_d, own_a = Own(sem(tag + "dve")), Own(sem(tag + "act"))
    x_made, e_made, logs, g_made = sem(tag + "x_made"), sem(tag + "e_made"), sem(tag + "logs"), sem(tag + "g_made")

    def act(eng):
        eng.activation(nea[:], a_log, ACT.Exp).then_inc(e_made, 1)
        eng.wait_ge(x_made, 1)
        own_a.did(eng, eng.activation(e[:], ax[:], ACT.Exp, scale=-1.0))
        eng.activation(eb[:], ab_tok[:, :, H:2 * H], ACT.Exp, scale=-1.0).then_inc(e_made, 1)
        eng.activation(l1[:], e[:], ACT.Ln, bias=1.0).then_inc(logs, 1)

    def dve(eng):
        bc = lambda ap: ap.unsqueeze(1).to_broadcast(shape)
        own_d.did(eng, eng.tensor_tensor(x[:], ab_tok[:, :, 0:H], bc(dtb), ALU.add))
        own_d.did(eng, eng.tensor_scalar(ax[:], x[:], -1.0, None, ALU.mult))
        eng.tensor_tensor(ax[:], ax[:], x[:], ALU.max).then_inc(x_made, 1)
        own_d.did(eng, eng.tensor_scalar(x[:], x[:], 0.0, None, ALU.max))
        eng.wait_ge(e_made, 2)
        own_d.did(eng, eng.tensor_scalar(eb1[:], eb[:], 1.0, None, ALU.add))
        own_d.did(eng, eng.reciprocal(beta, eb1[:]))
        eng.wait_ge(logs, 1)
        own_d.did(eng, eng.tensor_tensor(x[:], x[:], l1[:], ALU.add))
        own_d.did(eng, eng.tensor_tensor(x[:], x[:], bc(nea[:]), ALU.mult))
        eng.tensor_scalar(g, x[:], -1.0, None, ALU.mult).then_inc(g_made, 1)

    return act, dve, g_made


def gates(c, io):
    nc, sem, psum = c.nc, c.sem, c.psum
    with ExitStack() as inner:
        st = Stage(nc, inner)
        al = st.sb("al_b", [P, H])
        dtb = st.sb("dtb_b", [P, H])
        ab_turned, sums, sums_copied, loaded = sem("ab_turned"), sem("sums"), sem("sums_copied"), sem("al_loaded")
        ab_tok = psum[0][:, 0:NCH * 8].rearrange("p (c q) -> p c q", q=8)
        ga = c.ga
        g_flat = st.sb("g_flat", [P, NCH, H])
        dif = st.sb("g_dif", [P, NCH, H])
        own = Own(sem("gates_dve"))
        ga_exp = sem("ga_exp")
        with nc.Block() as block:
            act_g, dve_g, g_made = softplus_gates(c, block, st, ab_tok, P, NCH, al[:], dtb[:], g_flat[:],
                                                  ga[:, :, 1, :], "gp_")

            @block.sync
            def _(eng):
                eng.dma_start(al[:], io["A_log"][0:1, :].to_broadcast([P, H])).then_inc(loaded, 16)
                eng.dma_start(dtb[:], io["dt_bias"][0:1, :].to_broadcast([P, H])).then_inc(loaded, 16)

            @block.tensor
            def _(eng):
                for t in range(NCH):
                    last = eng.transpose(psum[0][:, t * 8:(t + 1) * 8], c.ab[:, t * P:(t + 1) * P], c.ident[0:8, 0:8])
                last.then_inc(ab_turned, 1)
                eng.wait_ge(g_made, 1)
                flat = g_flat[:].rearrange("p c h -> p (c h)")
                eng.matmul(psum[1][:, 0:NCH * H], c.upto[:], flat, start=True, stop=True).then_inc(sums, 1)
                eng.matmul(psum[2][:, 0:NCH * H], c.ones[:], flat, start=True, stop=True).then_inc(sums, 1)

            @block.scalar
            def _(eng):
                eng.wait_ge(loaded, 32)
                eng.wait_ge(ab_turned, 1)
                act_g(eng)
                eng.wait_ge(sums, 2)
                upto = psum[1][:, 0:NCH * H].rearrange("p (c h) -> p c h", h=H)
                total = psum[2][:, 0:NCH * H].rearrange("p (c h) -> p c h", h=H)
                eng.activation(ga[:, :, 3, :], upto, ACT.Exp).then_inc(ga_exp, 1)
                eng.activation(ga[:, :, 5, :], total, ACT.Exp).then_inc(ga_exp, 1)
                eng.wait_ge(sums_copied, 1)
                eng.activation(ga[:, :, 4, :], dif[:], ACT.Exp).then_inc(ga_exp, 1)

            @block.vector
            def _(eng):
                eng.wait_ge(loaded, 32)
                eng.wait_ge(ab_turned, 1)
                dve_g(eng)
                eng.wait_ge(g_made, 1)
                own.did(eng, eng.tensor_copy(ga[:, :, 0, :], g_flat[:]))
                eng.wait_ge(ga_exp, 2)
                own.did(eng, eng.tensor_copy(ga[:, :, 2, :], psum[1][:, 0:NCH * H].rearrange("p (c h) -> p c h", h=H)))
                own.did(eng, eng.tensor_tensor(dif[:], psum[2][:, 0:NCH * H].rearrange("p (c h) -> p c h", h=H),
                                               ga[:, :, 2, :], ALU.subtract))
                eng.tensor_scalar(dif[:], dif[:], 0.0, None, ALU.min).then_inc(sums_copied, 1)


F_STEPS = "f.vg f.uq f.kb n1 n2 n3 n4 f.T1 f.T2 f.G g2 f.kk f.qk f.prep f.t2".split()
L_STEPS = "x1 y1 r1 x2 y2 r2 x3 y3 r3 x4 y4 r4 x5 y5 r5 x6 yt w u gm ns qs sd o".split()
O_STEPS = "o.t m0 m1 m2 m3 m4 m5 m6 m7 m8 m9 m10 m11".split()
PASS = """f.vg x1 f.uq y1 f.kb r1 o.t n1 x2 m0 y2 m1 n2 r2 m2 x3 m3 n3 y3 m4 r3 n4 m5 x4 m6 f.T1 y4 f.T2 r4 f.G
    x5 m7 g2 y5 f.kk r5 m8 x6 f.qk yt m9 w u gm m10 ns qs m11 sd f.prep o f.t2""".split()
PART = 2 * KT * 3 // 12


def mix(c, io, stack):
    nc, sem, psum = c.nc, c.sem, c.psum
    st = Stage(nc, stack)
    sb = st.sb
    bX, bY, bR, bD, bE, bF, bG, bH = (b[:, :] for b in psum)

    def two(name, shape=(P, HW)):
        return [sb(f"{name}{i}", list(shape)) for i in range(2)]

    pt = sb("pt", [P, NF, P])
    xres = sb("xres", [P, D])
    x1 = sb("x1", [P, D])
    sq = sb("sq", [P, 2 * HW])
    ss, ms, rt, rs = (sb("mx_" + n, [P, 9]) for n in ("ss", "ms", "rt", "rs"))
    qn, kn, vt, kb, qe, kT, kbT, qT, em, dif, sqv = (sb(n, [P, HW]) for n in
                                                    ("qn", "kn", "vt", "kb", "qe", "kT", "kbT", "qT", "em", "dif", "sqv"))
    cg = two("cg", (P, 6, H))
    ut, gg, vbn, kbe, kd, vbt, qeT, nt, qkm = (two(n) for n in
                                               ("ut", "gg", "vbn", "kbe", "kd", "vbt", "qeT", "nt", "qkm"))
    tinv, ttinv, xs = (sb(n, [P, HW]) for n in ("tinv", "ttinv", "xs"))
    mt = two("mt")
    nwT, vn, oa, ob, sqo = (sb(n, [P, HW]) for n in ("nwT", "vn", "oa", "ob", "sqo"))
    oss, oms, ort, ors = (sb("mo_" + n, [P, H]) for n in ("ss", "ms", "rt", "rs"))
    oT_hi = sb("oT_hi", [P, KT, P], F32R)
    oT_lo = sb("oT_lo", [P, KT, P], F32R)
    S = c.S

    names = """pt_loaded xres_loaded x1_stored cg_made pt_v pt_g pt_u pt_q pt_k pt_b
        qk_squared vb_squared v_copied u_copied ss_made ms_made rsqrt rs_made
        qn_made kn_made vbn_made gg_made kb_made pool_made knT kbT_ready qnT qeT_ready kT_made kbT_made qT_made qeT_made
        g_ready dif_made e_made em_made kk_ready qk_ready nt_made qkm_made tt0_part t2_made t2_turned t_copied
        m_made x_ready x_copied y_ready yt_ready t_added t_turned tt_copied tt_final
        wT_ready nwT_made gm_ready vn_ready vn_made o_ready sd_ready s_updated ob_made
        o_squared oss_made oms_made orsqrt oa_part oa_made
        oT_ready oT_hi_made oT_lo_made wo_ready x1_made S_zeroed""".split()
    s = {n: sem("m_" + n) for n in names}
    pv = io["p_dram"].rearrange("(f p) t -> p f t", p=P)
    products = [(half, k, q) for half in range(2) for k in range(KT) for q in range(3)]

    def turn(pe, bank, src):
        for h in range(H):
            last = pe.transpose(head(bank, h), head(src, h), c.ident[:])
        return last

    def turn_pt(pe, bank, group):
        for h in range(H):
            last = pe.transpose(head(bank, h), pt[:, group * H + h, :], c.ident[:])
        return last

    def by_head(pe, bank, lhsT, rhs):
        for h in range(H):
            last = pe.matmul(head(bank, h), head(lhsT, h), head(rhs, h), start=True, stop=True)
        return last

    def pe_F(pe, step, f, p):
        n = f + 1
        if step == "f.vg":
            wait(pe, s["pt_loaded"], n * 16)
            wait(pe, s["qkm_made"], f)
            turn_pt(pe, bD, 2).then_inc(s["pt_v"], 1)
            wait(pe, s["dif_made"], f)
            turn_pt(pe, bE, 3).then_inc(s["pt_g"], 1)
        elif step == "f.uq":
            wait(pe, s["nt_made"], f)
            turn_pt(pe, bF, 4).then_inc(s["pt_u"], 1)
            pe.wait_ge(s["v_copied"], n)
            turn_pt(pe, bD, 0).then_inc(s["pt_q"], 1)
        elif step == "f.kb":
            pe.wait_ge(s["gg_made"], n)
            turn_pt(pe, bE, 1).then_inc(s["pt_k"], 1)
            pe.wait_ge(s["u_copied"], n)
            turn_pt(pe, bF, 5).then_inc(s["pt_b"], 1)
        elif step == "f.T1":
            pe.wait_ge(s["kn_made"], n)
            pe.wait_ge(s["qn_made"], n)
            turn(pe, bD, kn).then_inc(s["knT"], 1)
            pe.wait_ge(s["kb_made"], n)
            turn(pe, bE, kb).then_inc(s["kbT_ready"], 1)
        elif step == "f.T2":
            pe.wait_ge(s["vbn_made"], n)
            turn(pe, bF, qn).then_inc(s["qnT"], 1)
            pe.wait_ge(s["kT_made"], n)
            pe.wait_ge(s["pool_made"], n * 4)
            turn(pe, bD, qe).then_inc(s["qeT_ready"], 1)
        elif step == "f.G":
            pe.wait_ge(s["kbT_made"], n)
            pe.wait_ge(s["cg_made"], n)
            for h in range(H):
                last = pe.transpose(head(bE, h), cg[p][:, 2, h:h + 1].to_broadcast([P, P]), c.ident[:])
            last.then_inc(s["g_ready"], 1)
        elif step == "f.kk":
            pe.wait_ge(s["qT_made"], n)
            by_head(pe, bF, kT, kbT).then_inc(s["kk_ready"], 1)
        elif step == "f.qk":
            pe.wait_ge(s["qeT_made"], n)
            by_head(pe, bD, kT, qT).then_inc(s["qk_ready"], 1)
        elif step == "f.t2":
            wait(pe, s["vn_made"], f)
            pe.wait_ge(s["t2_made"], n)
            turn(pe, bY, ttinv).then_inc(s["t2_turned"], 1)

    def pe_L(pe, step, q, p, first):
        n = q + 1
        kind, l = step[0], int(step[1]) if step[1:].isdigit() else 0
        if kind == "x":
            pe.wait_ge(s["m_made"], q * LEVELS + l)
            if l == 1:
                wait(pe, s["s_updated"], q)
                pe.wait_ge(s["t_copied"], n)
            else:
                pe.wait_ge(s["t_added"], q * (LEVELS - 1) + l - 1)
            by_head(pe, bX, mt[l % 2], tinv).then_inc(s["x_ready"], 1)
        elif step == "yt":
            pe.wait_ge(s["x_copied"], q * LEVELS + LEVELS)
            pe.wait_ge(s["tt_copied"], (q + 1) * (LEVELS - 1))
            by_head(pe, bY, xs, ttinv).then_inc(s["yt_ready"], 1)
        elif kind == "y":
            pe.wait_ge(s["x_copied"], q * LEVELS + l)
            if l > 1:
                pe.wait_ge(s["tt_copied"], q * (LEVELS - 1) + l - 1)
            by_head(pe, bY, ttinv, xs).then_inc(s["y_ready"], 1)
        elif kind == "r":
            pe.wait_ge(s["t_added"], q * (LEVELS - 1) + l)
            if l == 1:
                wait(pe, s["oa_part"], q)
            turn(pe, bR, tinv).then_inc(s["t_turned"], 1)
        elif step == "w":
            pe.wait_ge(s["tt_final"], n)
            by_head(pe, bX, kbe[p], ttinv).then_inc(s["wT_ready"], 1)
        elif step == "u":
            for h in range(H):
                pe.matmul(head(bY, h), head(ttinv, h), head(vbt[p], h), start=(h == 0), stop=False, skip_group_check=True)
        elif step == "gm":
            by_head(pe, bR, c.wsT, vbn[p]).then_inc(s["gm_ready"], 1)
        elif step == "ns":
            pe.wait_ge(s["nwT_made"], n)
            if first:
                pe.wait_ge(s["S_zeroed"], 1)
            for h in range(H):
                last = pe.matmul(head(bY, h), head(nwT, h), head(S, h), start=False, stop=(h == H - 1), skip_group_check=True)
            last.then_inc(s["vn_ready"], 1)
        elif step == "qs":
            pe.wait_ge(s["ob_made"], n)
            for h in range(H):
                pe.matmul(head(bR, h), head(qeT[p], h), head(S, h), start=(h == 0), stop=False, skip_group_check=True)
        elif step == "sd":
            pe.wait_ge(s["vn_made"], n)
            by_head(pe, bX, kd[p], vn).then_inc(s["sd_ready"], 1)
        elif step == "o":
            for h in range(H):
                last = pe.matmul(head(bR, h), head(qkm[p], h), head(vn, h), start=False, stop=(h == H - 1), skip_group_check=True)
            last.then_inc(s["o_ready"], 1)

    def pe_O(pe, step, o):
        if step == "o.t":
            pe.wait_ge(s["oa_made"], o + 1)
            pe.wait_ge(s["ob_made"], o + 1)
            wait(pe, s["x1_made"], o * 2 + 1)
            turn(pe, bG, oa).then_inc(s["oT_ready"], 1)
            turn(pe, bH, ob).then_inc(s["oT_ready"], 1)
        else:
            i = int(step[1:]) * PART
            pe.wait_ge(s["oT_lo_made"], o * 2 + (2 if i >= 12 else 1))
            for half, k, q in products[i:i + PART]:
                if (half, k, q) == (0, KT // 2, 0):
                    pe.wait_ge(s["oT_lo_made"], o * 2 + 2)
                w, v = ((c.wo_lo, oT_hi), (c.wo_hi, oT_lo), (c.wo_hi, oT_hi))[q]
                last = pe.matmul((bG, bH)[half], v[:, k, :], w[:, k, half * 512:(half + 1) * 512],
                                 start=(k == 0 and q == 0), stop=(k == KT - 1 and q == 2))
                if k == KT - 1 and q == 2:
                    last.then_inc(s["wo_ready"], 1)

    def dve_F(dve, step, f, p):
        n = f + 1
        if step == "f.vg":
            wait(dve, s["oa_made"], f - 1)
            wait(dve, s["s_updated"], f - 1)
            dve.tensor_copy(cg[p][:].unsqueeze(1), c.ga[:, bass.ds(f, 1), :, :]).then_inc(s["cg_made"], 1)
            dve.wait_ge(s["pt_g"], n)
            dve.tensor_tensor(heads(gg[p][:]), heads(bE), across(c.o_gain[:]), ALU.mult).then_inc(s["gg_made"], 1)
        elif step == "n1":
            dve.wait_ge(s["qk_squared"], n)
            dve.tensor_reduce(ss[:, 0:8], sq[:].rearrange("p (n d) -> p n d", d=P), AX.X, ALU.add).then_inc(s["ss_made"], 1)
            dve.wait_ge(s["vb_squared"], n)
            dve.tensor_scalar(ms[:, 8:9], ss[:, 8:9], 1.0 / HW, EPS, ALU.mult, ALU.add).then_inc(s["ms_made"], 1)
            dve.wait_ge(s["ss_made"], n)
            dve.tensor_scalar(ms[:, 0:8], ss[:, 0:8], EPS, None, ALU.add).then_inc(s["ms_made"], 1)
            dve.wait_ge(s["ms_made"], n * 2)
        elif step == "n2":
            rsqrt(dve, s["rsqrt"], f * RSQRT_STEPS, rs[:], ms[:], rt[:])
            dve.tensor_scalar(rs[:, 0:H], rs[:, 0:H], DK ** -0.5, None, ALU.mult).then_inc(s["rs_made"], 1)
        elif step == "n3":
            dve.tensor_tensor(heads(kn[:]), heads(bE), along(rs[:, 4:8]), ALU.mult).then_inc(s["kn_made"], 1)
            dve.wait_ge(s["rs_made"], n)
            dve.tensor_tensor(heads(qn[:]), heads(bD), along(rs[:, 0:4]), ALU.mult).then_inc(s["qn_made"], 1)
        elif step == "n4":
            dve.wait_ge(s["kn_made"], n)
            dve.wait_ge(s["cg_made"], n)
            dve.tensor_tensor(heads(kb[:]), heads(kn[:]), along(cg[p][:, 1, :]), ALU.mult).then_inc(s["kb_made"], 1)
            dve.scalar_tensor_tensor(out=vbn[p][:], in0=bF, scalar=rs[:, 8:9], in1=c.v_gain[:],
                                     op0=ALU.mult, op1=ALU.mult).then_inc(s["vbn_made"], 1)
        elif step == "f.G":
            dve.wait_ge(s["g_ready"], n)
            for h in range(H):
                ins = dve.tensor_scalar(head(dif, h), head(bE, h), cg[p][:, 2, h:h + 1], 0.0, ALU.subtract, ALU.min)
            ins.then_inc(s["dif_made"], 1)
        elif step == "g2":
            dve.wait_ge(s["e_made"], n)
            dve.tensor_tensor(heads(em[:]), heads(em[:]), across(c.upto[:]), ALU.mult).then_inc(s["em_made"], 1)
        elif step == "f.kk":
            dve.wait_ge(s["em_made"], n)
            dve.wait_ge(s["kk_ready"], n)
            dve.tensor_tensor(nt[p][:], bF, em[:], ALU.mult).then_inc(s["nt_made"], 1)
        elif step == "f.qk":
            dve.wait_ge(s["qk_ready"], n)
            dve.tensor_tensor(qkm[p][:], bD, em[:], ALU.mult).then_inc(s["qkm_made"], 1)
        elif step == "f.prep":
            dve.wait_ge(s["nt_made"], n)
            dve.tensor_tensor(heads(ttinv[:]), heads(nt[p][:]), across(c.masks[:, 0, :]), ALU.mult).then_inc(s["tt0_part"], 1)
            dve.wait_ge(s["tt0_part"], n)
            dve.tensor_tensor(heads(ttinv[:]), heads(ttinv[:]), across(c.ident[:]), ALU.add).then_inc(s["t2_made"], 1)

    def dve_L(dve, step, q, p):
        n = q + 1
        kind, l = step[0], int(step[1]) if step[1:].isdigit() else 0
        if step == "yt":
            dve.wait_ge(s["yt_ready"], n)
            dve.tensor_tensor(ttinv[:], bY, ttinv[:], ALU.add).then_inc(s["tt_final"], 1)
        elif kind == "y":
            dve.wait_ge(s["y_ready"], q * (LEVELS - 1) + l)
            if l == 1:
                dve.wait_ge(s["t_copied"], n)
            else:
                dve.wait_ge(s["t_added"], q * (LEVELS - 1) + l - 1)
            dve.tensor_tensor(tinv[:], bY, tinv[:], ALU.add).then_inc(s["t_added"], 1)
        elif step == "gm":
            dve.wait_ge(s["gm_ready"], n)
            for h in range(H):
                ins = dve.scalar_tensor_tensor(out=head(ob, h), in0=head(bR, h), scalar=c.b_col[:, h:h + 1],
                                               in1=head(ut[p], h), op0=ALU.add, op1=ALU.mult)
            ins.then_inc(s["ob_made"], 1)
        elif step == "ns":
            dve.wait_ge(s["vn_ready"], n)
            dve.tensor_copy(vn[:], bY).then_inc(s["vn_made"], 1)
        elif step == "sd":
            dve.wait_ge(s["sd_ready"], n)
            for h in range(H):
                ins = dve.scalar_tensor_tensor(out=head(S, h), in0=head(S, h), scalar=cg[p][:, 5, h:h + 1], in1=head(bX, h),
                                               op0=ALU.mult, op1=ALU.add)
            ins.then_inc(s["s_updated"], 1)
        elif step == "o":
            dve.wait_ge(s["o_squared"], n)
            dve.tensor_reduce(oss[:], heads(sqo[:]), AX.X, ALU.add).then_inc(s["oss_made"], 1)
            dve.wait_ge(s["oss_made"], n)
            dve.tensor_scalar(oms[:], oss[:], 1.0 / DK, EPS, ALU.mult, ALU.add).then_inc(s["oms_made"], 1)
            dve.wait_ge(s["oms_made"], n)
            rsqrt(dve, s["orsqrt"], q * RSQRT_STEPS, ors[:], oms[:], ort[:])
            dve.tensor_tensor(heads(oa[:]), heads(bR), along(ors[:]), ALU.mult).then_inc(s["oa_part"], 1)
            dve.wait_ge(s["oa_part"], n)
            dve.tensor_tensor(oa[:], oa[:], gg[p][:], ALU.mult).then_inc(s["oa_made"], 1)

    def dve_O(dve, step, o):
        if step == "o.t":
            for i, bank in enumerate((bG, bH)):
                dve.wait_ge(s["oT_hi_made"], o * 2 + 1 + i)
                dve.tensor_tensor(oT_lo[:, 4 * i:4 * i + 4, :], heads(bank), oT_hi[:, 4 * i:4 * i + 4, :].bitcast(F32),
                                  ALU.subtract).then_inc(s["oT_lo_made"], 1)
        elif step in ("m5", "m11"):
            half = 0 if step == "m5" else 1
            cols = slice(half * 512, (half + 1) * 512)
            dve.wait_ge(s["wo_ready"], o * 2 + 1 + half)
            dve.wait_ge(s["xres_loaded"], o * 16 + 16)
            dve.wait_ge(s["x1_stored"], o * 16 + 16)
            dve.tensor_tensor(x1[:, cols], (bG, bH)[half], xres[:, cols], ALU.add).then_inc(s["x1_made"], 1)

    def act_F(act, step, f, p):
        n = f + 1
        if step == "f.vg":
            act.wait_ge(s["pt_v"], n)
            wait(act, s["pool_made"], f * 4)
            act.activation(vt[:], bD, ACT.Copy).then_inc(s["v_copied"], 1)
        elif step == "f.uq":
            wait(act, s["ob_made"], f - 1)
            act.wait_ge(s["pt_u"], n)
            act.activation(ut[p][:], bF, ACT.Copy).then_inc(s["u_copied"], 1)
            act.wait_ge(s["pt_q"], n)
            act.activation(sq[:, 0:HW], bD, ACT.Square)
        elif step == "f.kb":
            act.wait_ge(s["pt_k"], n)
            act.activation(sq[:, HW:2 * HW], bE, ACT.Square).then_inc(s["qk_squared"], 1)
            act.wait_ge(s["pt_b"], n)
            act.activation(sqv[:], bF, ACT.Square, accum_out=ss[:, 8:9]).then_inc(s["vb_squared"], 1)
        elif step == "f.T1":
            act.wait_ge(s["knT"], n)
            act.activation(kT[:], bD, ACT.Copy).then_inc(s["kT_made"], 1)
            act.wait_ge(s["kbT_ready"], n)
            act.activation(kbT[:], bE, ACT.Copy).then_inc(s["kbT_made"], 1)
        elif step == "f.T2":
            act.wait_ge(s["qnT"], n)
            act.activation(qT[:], bF, ACT.Copy).then_inc(s["qT_made"], 1)
            act.wait_ge(s["qeT_ready"], n)
            act.activation(qeT[p][:], bD, ACT.Copy).then_inc(s["qeT_made"], 1)
        elif step == "f.G":
            act.wait_ge(s["dif_made"], n)
            act.activation(em[:], dif[:], ACT.Exp).then_inc(s["e_made"], 1)
        elif step == "f.t2":
            act.wait_ge(s["t2_turned"], n)
            act.activation(tinv[:], bY, ACT.Copy).then_inc(s["t_copied"], 1)

    def act_L(act, step, q, p):
        n = q + 1
        kind, l = step[0], int(step[1]) if step[1:].isdigit() else 0
        if kind == "x":
            act.wait_ge(s["x_ready"], q * LEVELS + l)
            act.activation(xs[:], bX, ACT.Copy).then_inc(s["x_copied"], 1)
        elif kind == "r":
            act.wait_ge(s["t_turned"], q * (LEVELS - 1) + l)
            act.activation(ttinv[:], bR, ACT.Copy).then_inc(s["tt_copied"], 1)
        elif step == "w":
            act.wait_ge(s["wT_ready"], n)
            act.activation(nwT[:], bX, ACT.Copy, scale=-1.0).then_inc(s["nwT_made"], 1)
        elif step == "o":
            act.wait_ge(s["o_ready"], n)
            act.activation(sqo[:], bR, ACT.Square).then_inc(s["o_squared"], 1)

    def act_O(act, step, o):
        if step == "o.t":
            for i, bank in enumerate((bG, bH)):
                act.wait_ge(s["oT_ready"], o * 2 + 1 + i)
                act.activation(oT_hi[:, 4 * i:4 * i + 4, :], heads(bank), ACT.Copy).then_inc(s["oT_hi_made"], 1)

    def pool_F(pool, step, f, p):
        n = f + 1
        if step == "n3":
            pool.wait_ge(s["qn_made"], n)
            pool.tensor_tensor(heads(qe[:]), heads(qn[:]), along(cg[p][:, 3, :]), ALU.mult).then_inc(s["pool_made"], 1)
            pool.tensor_tensor(heads(kd[p][:]), heads(kn[:]), along(cg[p][:, 4, :]), ALU.mult).then_inc(s["pool_made"], 1)
            pool.wait_ge(s["v_copied"], n)
            pool.tensor_tensor(heads(vbt[p][:]), heads(vt[:]), along(cg[p][:, 1, :]), ALU.mult).then_inc(s["pool_made"], 1)
            pool.wait_ge(s["kb_made"], n)
            pool.tensor_tensor(heads(kbe[p][:]), heads(kb[:]), along(cg[p][:, 3, :]), ALU.mult).then_inc(s["pool_made"], 1)

    def pool_mask(pool, q, l, p):
        wait(pool, s["x_ready"], q * LEVELS + l - 2)
        pool.tensor_tensor(heads(mt[l % 2][:]), heads(nt[p][:]), across(c.masks[:, l, :]), ALU.mult).then_inc(s["m_made"], 1)

    def pool_L(pool, step, q, p):
        if step[0] == "x" and int(step[1]) + 2 <= LEVELS:
            pool_mask(pool, q, int(step[1]) + 2, p)

    def one_pass(eng, F, L, O, f):
        chunk, par = f
        for step in PASS:
            if step in F_STEPS and F:
                F(eng, step, chunk, par)
            if step in L_STEPS and L:
                L(eng, step, chunk - 1, 1 - par)
            if step in O_STEPS and O:
                O(eng, step, chunk - 2)

    def all_passes(eng, F, L, O, L_first=None):
        one_pass(eng, F, None, None, (0, 0))
        one_pass(eng, F, L_first or L, None, (1, 1))
        with eng.Fori(0, NCH // 2 - 1) as ii:
            for par in range(2):
                one_pass(eng, F, L, O, (ii * 2 + 2 + par, par))
        one_pass(eng, None, L, O, (NCH, 0))
        one_pass(eng, None, None, O, (NCH + 1, 1))

    with nc.Block() as block:
        @block.sync
        def _(sp):
            def load_pt(f):
                wait(sp, s["pt_b"], f)
                sp.dma_start(pt[:], pv[:, :, bass.ds(f * P, P)]).then_inc(s["pt_loaded"], 16)

            def rows(o):
                sp.dma_start(xres[:], io["x_prompt"][0, bass.ds(o * P, P), :]).then_inc(s["xres_loaded"], 16)
                sp.wait_ge(s["x1_made"], o * 2 + 3)
                sp.dma_start(io["x1_dram"][bass.ds(o * P, P), :], x1[:]).then_inc(s["x1_stored"], 16)

            load_pt(0)
            load_pt(1)
            load_pt(2)
            with sp.Fori(0, NCH - 3) as o:
                load_pt(o + 3)
                rows(o)
            for o in range(NCH - 3, NCH):
                rows(o)
            sp.wait_ge(s["s_updated"], NCH)
            sp.dma_start(io["new_delta_prompt"][0, 0].rearrange("h k v -> k h v"), heads(S[:])).then_inc(s["x1_stored"], 16)
            sp.wait_ge(s["x1_stored"], NCH * 16 + 32)

        @block.tensor
        def _(pe):
            all_passes(pe, pe_F, lambda e, st_, q, p: pe_L(e, st_, q, p, False), pe_O,
                       lambda e, st_, q, p: pe_L(e, st_, q, p, True))

        @block.vector
        def _(dve):
            dve.memset(S[:], 0.0).then_inc(s["S_zeroed"], 1)
            dve.wait_ge(s["S_zeroed"], 1)
            dve.sem_inc(s["x1_stored"], 16)
            dve.sem_inc(s["x1_made"], 1)
            all_passes(dve, dve_F, dve_L, dve_O)

        @block.scalar
        def _(act):
            all_passes(act, act_F, act_L, act_O)

        @block.gpsimd
        def _(pool):
            def pool_step(eng, step, f, p):
                pool_F(eng, step, f, p)
                if step == "f.prep":
                    eng.wait_ge(s["nt_made"], f + 1)
                    pool_mask(eng, f, 1, p)
                    pool_mask(eng, f, 2, p)
            all_passes(pool, pool_step, pool_L, None)


def mix_constants(c, io):
    nc, sem, psum = c.nc, c.sem, c.psum
    with ExitStack() as inner:
        st = Stage(nc, inner)
        ws = st.sb("ws", [P, H, P])
        loaded, masked, turned, copied = sem("ws_loaded"), sem("ws_masked"), sem("ws_turned"), sem("ws_copied")
        with nc.Block() as block:
            @block.sync
            def _(eng):
                eng.dma_start(ws[:], io["w_s"][0].rearrange("h i j -> i h j")).then_inc(loaded, 16)
                eng.dma_start(c.b_col[:], io["b_s"][0].rearrange("h i -> i h"), allow_slow_non_contiguous=True).then_inc(loaded, 16)
                eng.dma_start(c.o_gain[:], io["o_norm_g"][0:1, :].to_broadcast([P, P])).then_inc(loaded, 16)
                eng.dma_start(c.v_gain[:], io["v_norm_g"][0:1, :].to_broadcast([P, HW])).then_inc(loaded, 16)

            @block.gpsimd
            def _(eng):
                eng.wait_ge(loaded, 64)
                eng.affine_select(out=ws[:], in_=ws[:], compare_op=ALU.is_ge, fill=0.0, base=0,
                                  pattern=[[0, H], [-1, P]], channel_multiplier=1).then_inc(masked, 1)

            @block.tensor
            def _(eng):
                eng.wait_ge(masked, 1)
                for h in range(H):
                    last = eng.transpose(head(psum[3], h), ws[:, h, :], c.ident[:])
                last.then_inc(turned, 1)

            @block.vector
            def _(eng):
                eng.wait_ge(turned, 1)
                eng.tensor_copy(c.wsT[:], psum[3][:, :]).then_inc(copied, 1)


def sample(c, io, stack):
    nc, sem, psum = c.nc, c.sem, c.psum
    st = Stage(nc, stack)
    sb = st.sb
    N = NS
    names = """states_loaded small_loaded acc_made silu_made raw_turned turned ab_turned tok_made squared ms_made
        rsqrt knT_ready kT_made kv_ready delta_made outer_ready outer_added o_ready osq oms_made
        o_made oT_ready oT_hi_made oT_lo_made y_ready stored rows_made rest_made eg_ready eg_made masks_made""".split()
    s = {n: sem("s_" + n) for n in names}
    own_d, own_a = Own(sem("s_dve")), Own(sem("s_act"))

    states = sb("states", [P, N * H, DK])
    al, dtb = sb("s_al", [N, H]), sb("s_dtb", [N, H])
    w00, b00 = sb("s_w00", [N, H]), sb("s_b00", [N, H])
    acc, part = sb("s_acc", [P, NCONV, N]), sb("s_part", [P, NCONV, N])
    qkvT, gateT = sb("s_qkvT", [P, NCONV, N]), sb("s_gateT", [P, H, N])
    rows = sb("s_rows", [N, QKV])
    prow = sb("s_prow", [3, QKV])
    tok = [sb(f"s_tok{i}", [N, HW]) for i in range(6)]
    sq = sb("s_sq", [N, 3 * HW])
    ss, ms, rt, rs = (sb("s_" + n, [N, 9]) for n in ("ss", "ms", "rt", "rs"))
    oss, oms, ort, ors = (sb("so_" + n, [N, H]) for n in ("ss", "ms", "rt", "rs"))
    g, beta, eg = sb("s_g", [N, 1, H]), sb("s_beta", [N, 1, H]), sb("s_eg", [N, H])
    egm, egb = sb("s_egm", [N, N, H]), sb("s_egb", [P, N, H])
    kT, qT = sb("s_kT", [P, H, N]), sb("s_qT", [P, H, N])
    km, qm = sb("s_km", [P, H, N, N]), sb("s_qm", [P, H, N, N])
    delta = sb("s_delta", [N, HW])
    dmask = sb("s_dmask", [N, H, N, DK])
    oa, ob = sb("s_oa", [N, HW]), sb("s_ob", [N, HW])
    og, vg = sb("s_og", [N, HW]), sb("s_vg", [N, HW])
    oT_hi, oT_lo = sb("s_oT_hi", [P, KT, N], F32R), sb("s_oT_lo", [P, KT, N], F32R)
    i8 = c.ident[0:N, 0:N]
    bank = [b[0:N, :] for b in psum]
    act_g, dve_g, g_made = softplus_gates(c, None, st, psum[6][0:N, 0:8].unsqueeze(1), N, 1, al[:], dtb[:],
                                          g[:], beta[:], "gs_")
    st_view = states[:].rearrange("p (b h) v -> p b h v", h=H)

    with nc.Block() as block:
        @block.sync
        def _(eng):
            eng.dma_start(al[:], io["A_log"][0:1, :].to_broadcast([N, H])).then_inc(s["small_loaded"], 16)
            eng.dma_start(dtb[:], io["dt_bias"][0:1, :].to_broadcast([N, H])).then_inc(s["small_loaded"], 16)
            eng.dma_start(w00[:], io["w_s"][0, :, 0, 0:1].rearrange("h o -> o h").to_broadcast([N, H]),
                          allow_slow_non_contiguous=True).then_inc(s["small_loaded"], 16)
            eng.dma_start(b00[:], io["b_s"][0, :, 0:1].rearrange("h o -> o h").to_broadcast([N, H]),
                          allow_slow_non_contiguous=True).then_inc(s["small_loaded"], 16)
            eng.dma_start(states[:], io["state_delta"][0].rearrange("b h k v -> k (b h) v")).then_inc(s["states_loaded"], 16)
            eng.dma_start(io["new_conv_sample"][0, :, 0:2, :], io["state_conv"][0, :, 1:3, :]).then_inc(s["stored"], 16)
            eng.wait_ge(s["rows_made"], 6)
            eng.dma_start(io["new_conv_sample"][0, :, 2, :], rows[:]).then_inc(s["stored"], 16)
            eng.dma_start(io["new_conv_prompt"][0, 0], prow[:]).then_inc(s["stored"], 16)
            eng.wait_ge(s["tok_made"], 1)
            eng.dma_start(io["new_gmlp_v_sample"][0, :, 0, :], tok[5][:]).then_inc(s["stored"], 16)
            eng.wait_ge(s["outer_added"], 8)
            eng.dma_start(io["new_delta_sample"][0].rearrange("b h k v -> k (b h) v"), states[:]).then_inc(s["stored"], 16)
            eng.wait_ge(s["stored"], 16 * 5)

        @block.tensor
        def _(pe):
            for f in range(NCONV):
                pe.transpose(bank[f // 4][:, (f % 4) * P:(f % 4 + 1) * P], c.p_s[:, f, :], c.ident[:])
            for f in range(NCONV):
                last = pe.transpose(psum[3 + f // 4][0:3, (f % 4) * P:(f % 4 + 1) * P], c.tail[:, f, :], c.ident[:])
            last.then_inc(s["raw_turned"], 1)
            pe.transpose(bank[6][:, 0:8], c.ab[:, T:TW], c.ident[0:8, 0:8]).then_inc(s["ab_turned"], 1)
            pe.wait_ge(s["rows_made"], 6)
            pe.wait_ge(s["silu_made"], 2)
            for f in range(NCONV):
                pe.transpose(bank[f // 4][:, (f % 4) * P:(f % 4 + 1) * P], qkvT[:, f, :], c.ident[:])
            for f in range(H):
                pe.transpose(bank[3][:, f * P:(f + 1) * P], gateT[:, f, :], c.ident[:])
            for f in range(2 * H):
                last = pe.transpose(bank[4 + f // 4][:, (f % 4) * P:(f % 4 + 1) * P], c.p_s[:, 4 * H + f, :], c.ident[:])
            last.then_inc(s["turned"], 1)
            pe.wait_ge(s["tok_made"], 1)
            for i, t in enumerate((tok[1], tok[0])):
                for h in range(H):
                    last = pe.transpose(psum[7][:, (i * H + h) * N:(i * H + h + 1) * N], head(t, h), i8)
            last.then_inc(s["knT_ready"], 1)
            pe.wait_ge(s["eg_made"], 1)
            pe.matmul(psum[3][:, 0:N * H], c.ones[0:N, :], egm[:].rearrange("t b h -> t (b h)"), start=True, stop=True).then_inc(s["eg_ready"], 1)
            pe.wait_ge(s["states_loaded"], 16)
            pe.wait_ge(s["masks_made"], 1)
            for h in range(H):
                for b in range(N):
                    last = pe.matmul(head(bank[0], h), km[:, h, b, :], states[:, b * H + h, :], start=(b == 0), stop=(b == N - 1))
            last.then_inc(s["kv_ready"], 1)
            pe.wait_ge(s["delta_made"], 1)
            for h in range(H):
                for half in range(2):
                    u = 2 * h + half
                    wait(pe, s["outer_added"], u - 1)
                    pe.matmul(psum[1 + u % 2][:, :], head(tok[1], h),
                              dmask[:, h, 4 * half:4 * half + 4, :].rearrange("t b v -> t (b v)"),
                              start=True, stop=True).then_inc(s["outer_ready"], 1)
            pe.wait_ge(s["outer_added"], 8)
            for h in range(H):
                for b in range(N):
                    last = pe.matmul(head(bank[0], h), qm[:, h, b, :], states[:, b * H + h, :], start=(b == 0), stop=(b == N - 1))
            last.then_inc(s["o_ready"], 1)
            pe.wait_ge(s["o_made"], 1)
            for i, t in enumerate((oa, ob)):
                for h in range(H):
                    last = pe.transpose(psum[7][:, (i * H + h) * N:(i * H + h + 1) * N], head(t, h), i8)
            last.then_inc(s["oT_ready"], 1)
            pe.wait_ge(s["oT_lo_made"], 1)
            for half in range(2):
                cols = slice(half * 512, (half + 1) * 512)
                three_pass(pe, bank[1 + half], [(oT_hi[:, k, :], oT_lo[:, k, :], c.wo_hi[:, k, cols], c.wo_lo[:, k, cols])
                                                for k in range(KT)]).then_inc(s["y_ready"], 1)

        @block.scalar
        def _(act):
            act.wait_ge(s["small_loaded"], 64)
            act.wait_ge(s["acc_made"], 1)
            act.activation(qkvT[:], acc[:], ACT.Silu).then_inc(s["silu_made"], 1)
            act.activation(gateT[:], c.p_s[:, NCONV:NCONV + H, :], ACT.Silu).then_inc(s["silu_made"], 1)
            act.wait_ge(s["ab_turned"], 1)
            act_g(act)
            act.wait_ge(s["turned"], 1)
            for i, bk in enumerate((0, 1, 5)):
                act.activation(sq[:, i * HW:(i + 1) * HW], bank[bk], ACT.Square).then_inc(s["squared"], 1)
            act.wait_ge(g_made, 1)
            own_a.did(act, act.activation(eg[:], g[:, 0, :], ACT.Exp))
            act.activation(egm[:, 0, :], eg[:], ACT.Copy).then_inc(s["rest_made"], 1)
            act.wait_ge(s["o_ready"], 1)
            act.activation(sq[:, 0:HW], bank[0], ACT.Square).then_inc(s["osq"], 1)
            act.wait_ge(s["oT_ready"], 1)
            act.activation(oT_hi[:], psum[7][:, 0:KT * N].rearrange("p (k t) -> p k t", k=KT), ACT.Copy).then_inc(s["oT_hi_made"], 1)

        @block.vector
        def _(dve):
            did = lambda ins: own_d.did(dve, ins)
            old = c.taps[:, :, 0:24].rearrange("p f (b j) -> p f b j", j=3)
            tap = lambda j: c.taps[:, :, 24 + j:25 + j].to_broadcast([P, NCONV, N])
            did(dve.tensor_tensor(acc[:], old[:, :, :, 0], tap(0), ALU.mult))
            for j in (1, 2):
                did(dve.tensor_tensor(part[:], old[:, :, :, j], tap(j), ALU.mult))
                did(dve.tensor_tensor(acc[:], acc[:], part[:], ALU.add))
            did(dve.tensor_tensor(part[:], c.p_s[:, 0:NCONV, :], tap(3), ALU.mult))
            dve.tensor_tensor(acc[:], acc[:], part[:], ALU.add).then_inc(s["acc_made"], 1)
            dve.wait_ge(s["raw_turned"], 1)
            for i in range(3):
                dve.tensor_copy(rows[:, i * 512:(i + 1) * 512], bank[i]).then_inc(s["rows_made"], 1)
                dve.tensor_copy(prow[:, i * 512:(i + 1) * 512], psum[3 + i][0:3, :]).then_inc(s["rows_made"], 1)
            dve.wait_ge(s["small_loaded"], 64)
            dve.wait_ge(s["ab_turned"], 1)
            dve_g(dve)
            dve.wait_ge(s["squared"], 3)
            did(dve.tensor_reduce(ss[:, 0:8], sq[:, 0:2 * HW].rearrange("p (n d) -> p n d", d=P), AX.X, ALU.add))
            did(dve.tensor_reduce(ss[:, 8:9], sq[:, 2 * HW:3 * HW], AX.X, ALU.add))
            did(dve.tensor_scalar(ms[:, 0:8], ss[:, 0:8], EPS, None, ALU.add))
            dve.tensor_scalar(ms[:, 8:9], ss[:, 8:9], 1.0 / HW, EPS, ALU.mult, ALU.add).then_inc(s["ms_made"], 1)
            dve.wait_ge(s["ms_made"], 1)
            rsqrt(dve, s["rsqrt"], 0, rs[:], ms[:], rt[:])
            did(dve.tensor_scalar(rs[:, 0:4], rs[:, 0:4], DK ** -0.5, None, ALU.mult))
            did(dve.tensor_tensor(heads(tok[0][:]), heads(bank[0]), along(rs[:, 0:4]), ALU.mult))
            did(dve.tensor_tensor(heads(tok[1][:]), heads(bank[1]), along(rs[:, 4:8]), ALU.mult))
            did(dve.tensor_copy(tok[2][:], bank[2]))
            did(dve.tensor_tensor(heads(tok[3][:]), heads(bank[3]), across(c.o_gain[0:N, :]), ALU.mult))
            did(dve.tensor_copy(tok[4][:], bank[4]))
            dve.scalar_tensor_tensor(out=tok[5][:], in0=bank[5], scalar=rs[:, 8:9], in1=c.v_gain[0:N, :],
                                     op0=ALU.mult, op1=ALU.mult).then_inc(s["tok_made"], 1)
            dve.wait_ge(s["rest_made"], 1)
            dve.tensor_tensor(egm[:], eg[:].unsqueeze(1).to_broadcast([N, N, H]), along(i8, H), ALU.mult).then_inc(s["eg_made"], 1)
            dve.wait_ge(s["knT_ready"], 1)
            did(dve.tensor_copy(kT[:], psum[7][:, 0:H * N].rearrange("p (h t) -> p h t", h=H)))
            did(dve.tensor_copy(qT[:], psum[7][:, H * N:2 * H * N].rearrange("p (h t) -> p h t", h=H)))
            for h in range(H):
                dve.tensor_tensor(km[:, h], kT[:, h, :].unsqueeze(1).to_broadcast([P, N, N]), c.eye8[:], ALU.mult)
                ins = dve.tensor_tensor(qm[:, h], qT[:, h, :].unsqueeze(1).to_broadcast([P, N, N]), c.eye8[:], ALU.mult)
            ins.then_inc(s["masks_made"], 1)
            dve.wait_ge(s["eg_ready"], 1)
            did(dve.tensor_copy(egb[:], psum[3][:, 0:N * H].rearrange("p (b h) -> p b h", h=H)))
            dve.wait_ge(s["kv_ready"], 1)
            did(dve.tensor_tensor(heads(delta[:]), heads(bank[0]), along(eg[:]), ALU.mult))
            did(dve.tensor_tensor(delta[:], tok[2][:], delta[:], ALU.subtract))
            did(dve.tensor_tensor(heads(delta[:]), heads(delta[:]), along(beta[:, 0, :]), ALU.mult))
            for h in range(H):
                ins = dve.tensor_tensor(dmask[:, h], across(head(delta, h), N), along(i8, DK), ALU.mult)
            ins.then_inc(s["delta_made"], 1)
            for h in range(H):
                for half in range(2):
                    u = 2 * h + half
                    part_s = st_view[:, 4 * half:4 * half + 4, h, :]
                    if u == 0:
                        dve.wait_ge(s["states_loaded"], 16)
                    did(dve.tensor_tensor(part_s, part_s, along(egb[:, 4 * half:4 * half + 4, h], DK), ALU.mult))
                    dve.wait_ge(s["outer_ready"], u + 1)
                    dve.tensor_tensor(part_s, psum[1 + u % 2][:, :].rearrange("p (b v) -> p b v", b=4), part_s,
                                      ALU.add).then_inc(s["outer_added"], 1)
            dve.wait_ge(s["osq"], 1)
            did(dve.tensor_reduce(oss[:], heads(sq[:, 0:HW]), AX.X, ALU.add))
            dve.tensor_scalar(oms[:], oss[:], 1.0 / DK, EPS, ALU.mult, ALU.add).then_inc(s["oms_made"], 1)
            dve.wait_ge(s["oms_made"], 1)
            rsqrt(dve, s["rsqrt"], RSQRT_STEPS, ors[:], oms[:], ort[:])
            did(dve.tensor_tensor(heads(oa[:]), heads(bank[0]), along(ors[:]), ALU.mult))
            did(dve.tensor_tensor(oa[:], oa[:], tok[3][:], ALU.mult))
            did(dve.tensor_tensor(heads(ob[:]), heads(tok[5][:]), along(w00[:]), ALU.mult))
            did(dve.tensor_tensor(heads(ob[:]), heads(ob[:]), along(b00[:]), ALU.add))
            dve.tensor_tensor(ob[:], ob[:], tok[4][:], ALU.mult).then_inc(s["o_made"], 1)
            dve.wait_ge(s["oT_hi_made"], 1)
            dve.tensor_tensor(oT_lo[:], psum[7][:, 0:KT * N].rearrange("p (k t) -> p k t", k=KT), oT_hi[:].bitcast(F32),
                              ALU.subtract).then_inc(s["oT_lo_made"], 1)
            for half in range(2):
                cols = slice(half * 512, (half + 1) * 512)
                dve.wait_ge(s["y_ready"], half + 1)
                did(dve.tensor_tensor(c.x_s[:, cols], bank[1 + half], c.x_s[:, cols], ALU.add))


def ffn(c, io, stack, blk):
    c.acc = Stage(c.nc, stack).sb(f"f{blk}_acc", [P, NBT, D])
    with ExitStack() as inner:
        ffn_products(c, io, inner, blk)
    final_norm(c, io, stack, blk)


def ffn_products(c, io, stack, blk):
    nc, sem, psum = c.nc, c.sem, c.psum
    st = Stage(nc, stack)
    sb = st.sb
    tg = f"f{blk}_"
    extra = blk == 1
    n = NS if extra else 0
    W = BLK + n
    acc = c.acc
    h_hi = sb(tg + "h_hi", [P, KT, W], F32R)
    h_lo = sb(tg + "h_lo", [P, KT, W], F32R)
    with ExitStack() as inner:
        n_sp, n_act, n_dve, n_pe, _, _ = norm_transpose(
            c, None, Stage(nc, inner), io["x1_dram"][blk * BLK:(blk + 1) * BLK, :], io["norm_ffn_g"][0:1, :], h_hi, h_lo, acc, 1,
            n, None, c.x_s[:] if extra else None, tg + "n_", psum)
        with nc.Block() as block:
            block.sync(n_sp)
            block.scalar(n_act)
            block.vector(n_dve)
            block.tensor(n_pe)

    up_raw = sb(tg + "up_raw", [P, 2, KT, P])
    dn_raw = sb(tg + "dn_raw", [P, D])
    up_hi = [sb(f"{tg}up_hi{i}", [P, KT, P], F32R) for i in range(2)]
    up_lo = [sb(f"{tg}up_lo{i}", [P, KT, P], F32R) for i in range(2)]
    dn_hi = sb(tg + "dn_hi", [P, GH, D], F32R)
    dn_lo = sb(tg + "dn_lo", [P, GH, D], F32R)
    z_hi = sb(tg + "z_hi", [P, GH, W], F32R)
    z_lo = sb(tg + "z_lo", [P, GH, W], F32R)
    relu = [sb(f"{tg}relu{i}", [P, 512]) for i in range(3 if extra else 2)]
    sqr = sb(tg + "sqr", [P, 512])
    names = """up_loaded0 up_loaded1 dn_loaded up_hi_made up_lo_made dn_hi_made dn_lo_made z_ready relu_made zhi_made
        sqr_made zlo_made y_ready y_added""".split()
    s = {nm: sem(tg + nm) for nm in names}
    up_loaded = [s["up_loaded0"], s["up_loaded1"]]
    w_up = io["w_up"][0].rearrange("(k p) n -> p k n", p=P)
    w_down = io["w_down"][0]
    NZ = 3 if extra else 2
    UN = 2 * NBT + (2 if extra else 0)

    ZW = W // NZ
    ZB = 4

    def zblocks(j):
        return [(b, slice(b * ZW, (b + 1) * ZW), psum[(j * NZ + b) % ZB][:, 0:ZW]) for b in range(NZ)]

    def units():
        out = [(u, slice((u // 2) * P, (u // 2 + 1) * P), u % 2, psum[ZB + u % ZB][:, :],
                acc[:, u // 2, (u % 2) * 512:(u % 2 + 1) * 512]) for u in range(2 * NBT)]
        if extra:
            out += [(u, slice(BLK, W), u % 2, psum[ZB + u % ZB][0:n, :], c.x_s[:, (u % 2) * 512:(u % 2 + 1) * 512])
                    for u in range(2 * NBT, UN)]
        return out

    with nc.Block() as block:
        @block.sync
        def _(eng):
            for t in range(2):
                eng.dma_start(up_raw[:, t], w_up[:, :, t * P:(t + 1) * P]).then_inc(up_loaded[t], 16)
            eng.dma_start(dn_raw[:], w_down[0:P, :]).then_inc(s["dn_loaded"], 16)

            def step(t, p, up, dn):
                if up:
                    eng.wait_ge(s["up_lo_made"], t + 1)
                    eng.dma_start(up_raw[:, p], w_up[:, :, bass.ds(t * P + 2 * P, P)]).then_inc(up_loaded[p], 16)
                if dn:
                    eng.wait_ge(s["dn_lo_made"], t + 1)
                    eng.dma_start(dn_raw[:], w_down[bass.ds(t * P + P, P), :]).then_inc(s["dn_loaded"], 16)
            NTL = FF // P
            with eng.Fori(0, NTL // 2 - 1) as ii:
                for p in range(2):
                    step(ii * 2 + p, p, True, True)
            step(NTL - 2, 0, False, True)

        def up_hi_cut(act, t, p):
            act.wait_ge(up_loaded[p], (t - p) * 8 + 16)
            wait(act, s["z_ready"], (t - 1) * NZ + 1)
            act.activation(up_hi[p][:], up_raw[:, p], ACT.Copy).then_inc(s["up_hi_made"], 1)

        def act_group(act, gi, last):
            for j in range(GH):
                t = gi * GH + j
                if not (last and j == GH - 1):
                    up_hi_cut(act, t + 1, (j + 1) % 2)
                act.wait_ge(s["dn_loaded"], t * 16 + 16)
                act.wait_ge(s["y_ready"], gi * UN + 1)
                act.activation(dn_hi[:, j, :], dn_raw[:], ACT.Copy).then_inc(s["dn_hi_made"], 1)
                for b, cols, bank in zblocks(j):
                    q = t * NZ + b
                    act.wait_ge(s["z_ready"], q + 2)
                    act.wait_ge(s["sqr_made"], q + 1)
                    rl = relu[b][:, 0:cols.stop - cols.start]
                    act.activation(rl, bank, ACT.Relu).then_inc(s["relu_made"], 1)
                    act.wait_ge(s["relu_made"], q + 1 + ZB)
                    act.activation(z_hi[:, j, cols], rl, ACT.Square).then_inc(s["zhi_made"], 1)

        @block.scalar
        def _(act):
            up_hi_cut(act, 0, 0)
            with act.Fori(0, NG - 1) as gi:
                act_group(act, gi, False)
            act_group(act, NG - 1, True)

        def up_lo_cut(dve, t, p):
            dve.wait_ge(s["up_hi_made"], t + 1)
            dve.tensor_tensor(up_lo[p][:], up_raw[:, p], up_hi[p][:].bitcast(F32), ALU.subtract).then_inc(s["up_lo_made"], 1)

        def dve_group(dve, gi, last):
            for j in range(GH):
                t = gi * GH + j
                if not (last and j == GH - 1):
                    up_lo_cut(dve, t + 1, (j + 1) % 2)
                dve.wait_ge(s["dn_hi_made"], t + 1)
                dve.tensor_tensor(dn_lo[:, j, :], dn_raw[:], dn_hi[:, j, :].bitcast(F32), ALU.subtract).then_inc(s["dn_lo_made"], 1)
                for b, cols, bank in zblocks(j):
                    q = t * NZ + b
                    m = cols.stop - cols.start
                    dve.wait_ge(s["relu_made"], q + 1 + ZB)
                    dve.wait_ge(s["zlo_made"], q + 1)
                    dve.tensor_tensor(sqr[:, 0:m], relu[b][:, 0:m], relu[b][:, 0:m], ALU.mult).then_inc(s["sqr_made"], 1)
                    dve.wait_ge(s["zhi_made"], q + 1)
                    dve.wait_ge(s["sqr_made"], q + 3)
                    dve.tensor_tensor(z_lo[:, j, cols], sqr[:, 0:m], z_hi[:, j, cols].bitcast(F32), ALU.subtract).then_inc(s["zlo_made"], 1)
            for u, toks, half, bank, dst in units():
                dve.wait_ge(s["y_ready"], gi * UN + u + 2)
                dve.tensor_tensor(dst, bank, dst, ALU.add).then_inc(s["y_added"], 1)

        @block.vector
        def _(dve):
            dve.sem_inc(s["zlo_made"], 1)
            dve.sem_inc(s["sqr_made"], 2)
            dve.sem_inc(s["y_added"], 1)
            up_lo_cut(dve, 0, 0)
            with dve.Fori(0, NG - 1) as gi:
                dve_group(dve, gi, False)
            dve_group(dve, NG - 1, True)

        def down(pe, unit, js, first, last):
            u, toks, half, bank, _ = unit
            cols = slice(half * 512, (half + 1) * 512)
            return three_pass(pe, bank, [(z_hi[:, j, toks], z_lo[:, j, toks], dn_hi[:, j, cols], dn_lo[:, j, cols]) for j in js],
                              start=first, stop=last)

        def pe_group(pe, gi):
            for j in range(GH):
                t = gi * GH + j
                p = j % 2
                pe.wait_ge(s["up_lo_made"], t + 1)
                for b, cols, bank in zblocks(j):
                    pe.wait_ge(s["relu_made"], t * NZ + b + 1)
                    three_pass(pe, bank, [(up_hi[p][:, k, :], up_lo[p][:, k, :], h_hi[:, k, cols], h_lo[:, k, cols])
                                          for k in range(KT)]).then_inc(s["z_ready"], 1)
            us = units()
            pe.wait_ge(s["zlo_made"], gi * (GH * NZ) + (GH - 1) * NZ + 1)
            pe.wait_ge(s["dn_lo_made"], gi * GH + GH - 1)
            for unit in us[0:ZB]:
                pe.wait_ge(s["y_added"], gi * UN + 1)
                down(pe, unit, range(GH - 1), True, False)
            pe.wait_ge(s["zlo_made"], gi * (GH * NZ) + GH * NZ + 1)
            pe.wait_ge(s["dn_lo_made"], gi * GH + GH)
            for unit in us[0:ZB]:
                down(pe, unit, [GH - 1], False, True).then_inc(s["y_ready"], 1)
            for unit in us[ZB:]:
                pe.wait_ge(s["y_added"], gi * UN + unit[0] - ZB + 2)
                down(pe, unit, range(GH), True, True).then_inc(s["y_ready"], 1)

        @block.tensor
        def _(pe):
            pe.sem_inc(s["relu_made"], ZB)
            pe.sem_inc(s["z_ready"], 1)
            pe.sem_inc(s["y_ready"], 1)
            with pe.Fori(0, NG) as gi:
                pe_group(pe, gi)


def final_norm(c, io, stack, blk):
    nc, sem = c.nc, c.sem
    sb = Stage(nc, stack).sb
    tg = f"f{blk}_"
    extra = blk == 1
    n = NS if extra else 0
    acc = c.acc
    junk, fgain = sb(tg + "junk", [P, D]), sb(tg + "fgain", [P, D])
    fss, fms, frt, frs = (sb(tg + nm, [P, NBT + 1]) for nm in ("fss", "fms", "frt", "frs"))
    s = {nm: sem(tg + nm) for nm in "f_squared fms_made rsqrt fss_set out_made gain_loaded stored".split()}
    with nc.Block() as block:
        @block.scalar
        def _(act):
            act.wait_ge(s["fss_set"], 1)
            for m in range(NBT + (1 if extra else 0)):
                src, r = (acc[:, m, :], P) if m < NBT else (c.x_s[:], n)
                wait(act, s["f_squared"], m)
                act.activation(junk[0:r, :], src, ACT.Square, accum_out=fss[0:r, m:m + 1]).then_inc(s["f_squared"], 1)

        @block.vector
        def _(dve):
            dve.memset(fss[:], 1.0).then_inc(s["fss_set"], 1)
            nm = NBT + (1 if extra else 0)
            dve.wait_ge(s["f_squared"], nm)
            dve.tensor_scalar(fms[:], fss[:], 1.0 / D, EPS, ALU.mult, ALU.add).then_inc(s["fms_made"], 1)
            dve.wait_ge(s["fms_made"], 1)
            rsqrt(dve, s["rsqrt"], 0, frs[:], fms[:], frt[:])
            dve.wait_ge(s["gain_loaded"], 16)
            for m in range(nm):
                src, r = (acc[:, m, :], P) if m < NBT else (c.x_s[:], n)
                dve.scalar_tensor_tensor(out=src, in0=src, scalar=frs[0:r, m:m + 1], in1=fgain[0:r, :],
                                         op0=ALU.mult, op1=ALU.mult).then_inc(s["out_made"], 1)

        @block.gpsimd
        def _(pool):
            pool.dma_start(fgain[:], io["norm_f_g"].rearrange("(a d) -> a d", a=1).to_broadcast([P, D])).then_inc(s["gain_loaded"], 16)
            for m in range(NBT):
                pool.wait_ge(s["out_made"], m + 1)
                pool.dma_start(io["y_prompt"][0, blk * BLK + m * P:blk * BLK + (m + 1) * P, :], acc[:, m, :]).then_inc(s["stored"], 16)
            if extra:
                pool.wait_ge(s["out_made"], NBT + 1)
                pool.dma_start(io["y_sample"].rearrange("b s d -> (b s) d"), c.x_s[:]).then_inc(s["stored"], 16)
            pool.wait_ge(s["stored"], 16 * (NBT + (1 if extra else 0)))


def build(nc, named):
    with ExitStack() as stack:
        c, io = Shared(), named
        c.nc = nc
        zeroing = []

        def done(st):
            for owner, zero in zeroing:
                if owner is st:
                    zero()
        def use(st):
            mine = []

            def sem(name):
                mine.append(st.enter_context(nc.semaphore(name)))
                return mine[-1]

            def zero():
                nums = sorted(x.num for x in mine)
                runs = []
                for n in nums:
                    if runs and runs[-1][1] == n:
                        runs[-1][1] = n + 1
                    else:
                        runs.append([n, n + 1])
                for a, z in runs:
                    nc.gpsimd.sem_clear(range(a, z))
                nc.all_engine_barrier()
            c.sem = sem
            zeroing.append((st, zero))
        use(stack)
        io["p_dram"] = nc.dram_tensor("p_dram", (NF * P, T), F32).ap()
        io["x1_dram"] = nc.dram_tensor("x1_dram", (T, D), F32).ap()
        c.psum = [stack.enter_context(nc.psum_tensor(f"bank{i}", [P, 512], F32)) for i in range(8)]
        keep = Stage(nc, stack)
        c.ident = keep.sb("ident", [P, P])
        c.x_s = keep.sb("x_s", [NS, D])
        with ExitStack() as mixing:
            keep = Stage(nc, mixing)
            c.ones = keep.sb("ones", [P, P])
            c.upto = keep.sb("upto", [P, P])
            c.masks = keep.sb("masks", [P, LEVELS + 1, P])
            c.eye8 = keep.sb("eye8", [P, NS, NS])
            c.p_s = keep.sb("p_s", [P, NF, NS])
            c.tail = keep.sb("tail", [P, NCONV, 3])
            c.taps = keep.sb("taps", [P, NCONV, 28])
            c.ab = keep.sb("ab", [2 * H, TW])
            constants(c)
            with ExitStack() as s1:
                use(s1)
                project(c, io, s1)
                done(s1)
            with ExitStack() as s2:
                k2 = Stage(nc, s2)
                use(s2)
                c.ga = k2.sb("ga", [P, NCH, 6, H])
                c.S = k2.sb("S", [P, HW])
                c.wsT = k2.sb("wsT", [P, HW])
                c.b_col = k2.sb("b_col", [P, H])
                c.o_gain = k2.sb("o_gain", [P, P])
                c.v_gain = k2.sb("v_gain", [P, HW])
                mix_constants(c, io)
                gates(c, io)
                load_w_o(c, io, s2)
                with ExitStack() as s3:
                    use(s3)
                    mix(c, io, s3)
                    done(s3)
                with ExitStack() as s4:
                    use(s4)
                    sample(c, io, s4)
                    done(s4)
                done(s2)
        for blk in range(T // BLK):
            with ExitStack() as s5:
                use(s5)
                ffn(c, io, s5, blk)
                done(s5)


_INS = ['x_prompt', 'x_sample', 'state_delta', 'state_conv', 'norm_mix_g', 'w_in', 'conv_w', 'A_log', 'dt_bias',
        'o_norm_g', 'v_norm_g', 'w_s', 'b_s', 'w_o', 'norm_ffn_g', 'w_up', 'w_down', 'norm_f_g']
_OUTS = [('y_prompt', (1, 2048, 1024)), ('y_sample', (8, 1, 1024)), ('new_delta_prompt', (1, 1, 4, 128, 128)),
         ('new_conv_prompt', (1, 1, 3, 1536)), ('new_delta_sample', (1, 8, 4, 128, 128)),
         ('new_conv_sample', (1, 8, 3, 1536)), ('new_gmlp_v_sample', (1, 8, 1, 512))]


def kernel(**inputs):
    import numpy as _np
    import concourse.bacc as _bacc
    from concourse import mybir as _mybir
    from concourse.bass_utils import run_bass_kernel_spmd as _run

    nc = _bacc.Bacc("TRN2", target_bir_lowering=False, num_devices=1)
    arrays, io = {}, {}
    for name in _INS:
        a = _np.ascontiguousarray(inputs[name])
        arrays[f"in_{name}_dram"] = a
        io[name] = nc.dram_tensor(f"in_{name}_dram", a.shape, _mybir.dt.from_np(a.dtype), kind="ExternalInput").ap()
    for name, shape in _OUTS:
        io[name] = nc.dram_tensor(f"out_{name}_dram", shape, _mybir.dt.float32, kind="ExternalOutput").ap()
    build(nc, io)
    r = _run(nc, [arrays], core_ids=[0])
    return tuple(r.results[0][f"out_{name}_dram"] for name, _ in _OUTS)
```

```python
from contextlib import ExitStack

import concourse.bass as bass
from concourse import mybir

F32 = mybir.dt.float32
F32R = mybir.dt.float32r
I32 = mybir.dt.int32
ALU = mybir.AluOpType
ACT = mybir.ActivationFunctionType
AX = mybir.AxisListType

P = 128
D = 1024
KT = D // P
T = 2048
NCH = T // P
NS = 8
TW = T + NS
H = 4
DK = 128
HW = H * DK
QKV = 3 * HW
OFF_A = QKV + HW
OFF_U = OFF_A + 2 * H
NF = 24
NCONV = QKV // P
FF = 4 * D
BLK = 1024
NBT = BLK // P
GH = 2
NG = FF // P // GH
EPS = 1e-6
LEVELS = 6


def head(ap, h, w=P):
    return ap[:, h * w:(h + 1) * w]


def heads(ap, n=H):
    return ap.rearrange("p (h d) -> p h d", h=n)


def along(ap, w=P):
    return ap.unsqueeze(2).to_broadcast([ap.shape[0], ap.shape[1], w])


def across(ap, n=H):
    return ap.unsqueeze(1).to_broadcast([ap.shape[0], n, ap.shape[1]])


def wait(eng, sem, value):
    if isinstance(value, int) and value <= 0:
        return
    eng.wait_ge(sem, value)


class Own:

    def __init__(self, sem):
        self.sem, self.n = sem, 0

    def did(self, eng, ins):
        self.n += 1
        ins.then_inc(self.sem, 1)
        eng.wait_ge(self.sem, self.n)


RSQRT_STEPS = 13
DVE_RSQRT_STEPS = 10


def rsqrt(eng, sem, base, r, m, tmp, fused=False):
    n = 0

    def did(ins):
        nonlocal n
        n += 1
        ins.then_inc(sem, 1)
        eng.wait_ge(sem, base + n)

    did(eng.tensor_scalar(r.bitcast(I32), m.bitcast(I32), -0.5, float(0x5F3759DF), ALU.mult, ALU.add))
    for _ in range(3):
        if fused:
            did(eng.scalar_tensor_tensor(out=tmp, in0=r, scalar=-0.5, in1=r, op0=ALU.mult, op1=ALU.mult))
            did(eng.tensor_tensor(tmp, tmp, m, ALU.mult))
            did(eng.scalar_tensor_tensor(out=r, in0=tmp, scalar=1.5, in1=r, op0=ALU.add, op1=ALU.mult))
        else:
            did(eng.tensor_tensor(tmp, r, r, ALU.mult))
            did(eng.tensor_tensor(tmp, tmp, m, ALU.mult))
            did(eng.tensor_scalar(tmp, tmp, -0.5, 1.5, ALU.mult, ALU.add))
            did(eng.tensor_tensor(r, r, tmp, ALU.mult))


def dve_rsqrt(dve, sem, base, r, m, tmp):
    rsqrt(dve, sem, base, r, m, tmp, fused=True)


def three_pass(pe, out, pairs, start=True, stop=True, skip=False):
    n = len(pairs)
    for k, (wh, wl, xh, xl) in enumerate(pairs):
        pe.matmul(out, wl, xh, start=start and k == 0, stop=False, skip_group_check=skip)
        pe.matmul(out, wh, xl, start=False, stop=False, skip_group_check=skip)
        last = pe.matmul(out, wh, xh, start=False, stop=stop and k == n - 1, skip_group_check=skip)
    return last


class Stats:

    def __init__(self, c, st, tag, junk):
        self.c, self.junk = c, junk
        self.ss, self.ms, self.rt, self.rs = (st.sb(tag + n, [P, 10]) for n in ("ss", "ms", "rt", "rs"))
        self.squared, self.ms_made, self.refined = c.sem(tag + "squared"), c.sem(tag + "ms_made"), c.sem(tag + "refined")

    def square(self, act, m, col, src, r=P):
        wait(act, self.squared, m)
        act.activation(self.junk[0:r, :], src, ACT.Square, accum_out=self.ss[0:r, col:col + 1]).then_inc(self.squared, 1)

    def scales(self, eng, pair, col, n=2, r=P):
        eng.wait_ge(self.squared, pair * 2 + n)
        cols = slice(col, col + n)
        eng.tensor_scalar(self.ms[0:r, cols], self.ss[0:r, cols], 1.0 / D, EPS, ALU.mult, ALU.add).then_inc(self.ms_made, 1)
        eng.wait_ge(self.ms_made, pair + 1)
        rsqrt(eng, self.refined, pair * RSQRT_STEPS, self.rs[0:r, cols], self.ms[0:r, cols], self.rt[0:r, cols])

    def scaled(self, eng, pair, col, out, src, gain, r=P):
        eng.wait_ge(self.refined, (pair + 1) * RSQRT_STEPS)
        return eng.scalar_tensor_tensor(out=out, in0=src, scalar=self.rs[0:r, col:col + 1], in1=gain[0:r, :],
                                        op0=ALU.mult, op1=ALU.mult)


class Norm(Stats):

    def __init__(self, c, st, tag, gain, junk, xn, hi, lo, bank, two_banks):
        super().__init__(c, st, tag, junk)
        self.gain, self.xn, self.hi, self.lo, self.bank, self.two_banks = gain, xn, hi, lo, bank, two_banks
        self.xn_made, self.turned, self.hi_made, self.lo_made = (c.sem(tag + n) for n in
                                                                 ("xn_made", "turned", "hi_made", "lo_made"))

    def normalise(self, dve, m, k, pair, col, src, r=P):
        self.scaled(dve, pair, col, self.xn[0:r, k % 2, :], src, self.gain, r).then_inc(self.xn_made, 1)

    def turn(self, pe, m, k, r=P):
        pe.wait_ge(self.xn_made, m + 1)
        for half in range(2):
            if self.two_banks:
                wait(pe, self.lo_made, m * 2 + half - 1)
            for q in range(4):
                last = pe.transpose(self.bank(k, half)[:, q * r:(q + 1) * r],
                                    self.xn[0:r, k % 2, (4 * half + q) * P:(4 * half + q + 1) * P], self.c.ident[0:r, 0:r])
            last.then_inc(self.turned, 1)

    def cut_hi(self, act, m, k, cols, r=P):
        for half in range(2):
            act.wait_ge(self.turned, m * 2 + half + 1)
            act.activation(self.hi[:, 4 * half:4 * half + 4, cols], heads(self.bank(k, half)[:, 0:4 * r]),
                           ACT.Copy).then_inc(self.hi_made, 1)

    def cut_lo(self, dve, m, k, cols, r=P):
        for half in range(2):
            dve.wait_ge(self.hi_made, m * 2 + half + 1)
            dve.tensor_tensor(self.lo[:, 4 * half:4 * half + 4, cols], heads(self.bank(k, half)[:, 0:4 * r]),
                              self.hi[:, 4 * half:4 * half + 4, cols].bitcast(F32), ALU.subtract).then_inc(self.lo_made, 1)


class Shared:
    pass


class Stage:

    def __init__(self, nc, stack):
        self.nc, self.stack = nc, stack

    def sb(self, name, shape, dt=F32):
        return self.stack.enter_context(self.nc.sbuf_tensor(name, shape, dt))


IDENT_MADE = 2


def identity(c, pool, made):
    pool.memset(c.ident[:], 0.0).then_inc(made, 1)
    pool.wait_ge(made, 1)
    pool.affine_select(out=c.ident[:], in_=c.ident[:], compare_op=ALU.not_equal, fill=1.0, base=0,
                       pattern=[[-1, P]], channel_multiplier=1).then_inc(made, 1)


def constants(c, pool, made):
    n = IDENT_MADE

    def did(ins):
        nonlocal n
        n += 1
        ins.then_inc(made, 1)
        pool.wait_ge(made, n)

    did(pool.memset(c.ones[:], 1.0))
    did(pool.affine_select(out=c.upto[:], in_=c.ones[:], compare_op=ALU.is_ge, fill=0.0, base=0,
                           pattern=[[1, P]], channel_multiplier=-1))
    did(pool.memset(c.eye8[:], 0.0))
    did(pool.affine_select(out=c.eye8[:], in_=c.eye8[:], compare_op=ALU.not_equal, fill=1.0, base=0,
                           pattern=[[1, NS], [-1, NS]], channel_multiplier=0))
    for l in range(LEVELS + 1):
        s = 1 << l
        m = c.masks[:, l, :]
        did(pool.memset(m, -1.0))
        v = m.rearrange("p (g two i) -> p g two i", two=2, i=s)
        did(pool.affine_select(out=v, in_=v, compare_op=ALU.is_ge, fill=0.0, base=0,
                               pattern=[[-2 * s, P // (2 * s)], [0, 2], [0, s]], channel_multiplier=1))
        did(pool.affine_select(out=v, in_=v, compare_op=ALU.is_ge, fill=0.0, base=s - 1,
                               pattern=[[2 * s, P // (2 * s)], [0, 2], [0, s]], channel_multiplier=-1))
        did(pool.memset(v[:, :, 0, :], 0.0))


def project(c, io, stack):
    nc, sem, psum = c.nc, c.sem, c.psum
    st = Stage(nc, stack)
    sb = st.sb
    h_hi = sb("h_hi", [P, KT, TW], F32R)
    h_lo = sb("h_lo", [P, KT, TW], F32R)
    w_raw = sb("w_raw", [P, 2, KT, P])
    w_hi = [sb(f"w_hi{i}", [P, KT, P], F32R) for i in range(2)]
    w_lo = [sb(f"w_lo{i}", [P, KT, P], F32R) for i in range(2)]
    line = sb("line", [P, 3 + T])
    y = sb("y", [P, T])
    cwt = sb("cwt", [P, 4])
    xn = sb("xn", [P, 2, D])
    raw = [y[:, 0:D], y[:, D:2 * D], line[:, 0:D], line[:, D:2 * D]]
    gain, junk = c.ab_room[:, 0:D], c.ab_room[:, D:2 * D]
    norm = Norm(c, st, "n0_", gain, junk, xn, h_hi, h_lo, lambda k, half: psum[4 + 2 * (k % 2) + half], False)
    cw_in = xn[0:28, :, :].rearrange("p a d -> p (a d)")[:, 0:QKV]
    cw_loaded, cw_turned, taps_made, const_made = sem("cw_loaded"), sem("cw_turned"), sem("taps_made"), sem("const_made")
    x_loaded = [sem(f"x_loaded{k}") for k in range(4)]
    xs_loaded, gain_loaded = sem("xs_loaded"), sem("gain_loaded")
    XQ = NCH // 4
    w_loaded = [sem("w_loaded0"), sem("w_loaded1")]
    whi_made = sem("whi_made")
    wlo_made = sem("wlo_made")
    p_ready = sem("p_ready")
    bank_free = sem("bank_free")
    tail_made = sem("tail_made")
    zeroed = sem("zeroed")
    conv = sem("conv")
    conv_made = sem("conv_made")
    y_made = sem("y_made")
    y_stored = sem("y_stored")
    NB5 = 5
    WB = 412
    w_in = io["w_in"][0].rearrange("(k p) n -> p k n", p=P)

    def blocks():
        out = []
        for g in range(NB5):
            cols = slice(g * WB, min((g + 1) * WB, TW))
            out.append((g, cols, psum[g][:, 0:cols.stop - cols.start]))
        return out

    with nc.Block() as block:
        @block.sync
        def _(eng):
            def load_x(q, k):
                eng.dma_start(raw[k], io["x_prompt"][0, bass.ds(q * (4 * P) + k * P, P), :]).then_inc(x_loaded[k], 16)

            load_x(0, 0)
            eng.dma_start(gain, io["norm_mix_g"][0:1, :].to_broadcast([P, D])).then_inc(gain_loaded, 16)
            for k in range(1, 4):
                load_x(0, k)
            eng.dma_start(w_raw[:, 0], w_in[:, :, 0:P]).then_inc(w_loaded[0], 16)
            eng.dma_start(w_raw[:, 1], w_in[:, :, P:2 * P]).then_inc(w_loaded[1], 16)
            eng.dma_start(c.x_s[:], io["x_sample"].rearrange("b s d -> (b s) d")).then_inc(xs_loaded, 16)
            with eng.Fori(1, XQ) as q:
                for k in range(4):
                    eng.wait_ge(norm.xn_made, q * 4 + k - 3)
                    load_x(q, k)
            eng.wait_ge(norm.turned, 2 * NCH + 2)
            eng.dma_start(cw_in[0:24, :], io["state_conv"][0].rearrange("b j f -> (b j) f")).then_inc(cw_loaded, 16)
            eng.dma_start(cw_in[24:28, :], io["conv_w"][0]).then_inc(cw_loaded, 16)

            eng.sem_inc(y_stored, 16)

            def step(ii, s, off, kind):
                t = ii * 2 + s
                eng.wait_ge(wlo_made, t + 1)
                if off is None and s == 0:
                    eng.dma_start(w_raw[:, 0, :, 0:2 * H], w_in[:, :, OFF_A:OFF_U],
                                  allow_slow_non_contiguous=True).then_inc(w_loaded[0], 16)
                elif off is not None:
                    eng.dma_start(w_raw[:, s], w_in[:, :, bass.ds(ii * (2 * P) + (s + 2) * P + off, P)]).then_inc(w_loaded[s], 16)
                if kind == "conv":
                    eng.wait_ge(y_made, t + 1)
                else:
                    eng.wait_ge(bank_free, t * NB5 + NB5 + NB5)
                eng.dma_start(io["p_dram"][bass.ds(t * P, P), :], y[:]).then_inc(y_stored, 16)

            for a, b, off, kind in ((0, 6, 0, "conv"), (6, 7, 0, "plain"), (7, 11, 2 * H, "plain"), (11, 12, None, "plain")):
                with eng.Fori(a, b) as ii:
                    for s in range(2):
                        step(ii, s, off, kind)
            eng.wait_ge(y_stored, NF * 16 + 16)

        def split_hi(eng, ii, s):
            eng.wait_ge(w_loaded[s], ii * 16 + 16)
            wait(eng, p_ready, (ii * 2 + s - 1) * NB5 + 1)
            eng.activation(w_hi[s][:], w_raw[:, s], ACT.Copy).then_inc(whi_made, 1)

        @block.gpsimd
        def _(eng):
            identity(c, eng, const_made)
            for pair in range(NCH // 2):
                norm.scales(eng, pair, 2 * (pair % 2))
            norm.scales(eng, NCH // 2, 4, 1, NS)
            constants(c, eng, const_made)

        @block.scalar
        def _(eng):
            def squares(q, pair):
                for k in (2 * pair, 2 * pair + 1):
                    eng.wait_ge(x_loaded[k], q * 16 + 16)
                    norm.square(eng, q * 4 + k, k, raw[k])

            def norm_quad(q, last):
                squares(q, 1)
                for pair in range(2):
                    for k in (2 * pair, 2 * pair + 1):
                        norm.cut_hi(eng, q * 4 + k, k, bass.ds(q * (4 * P) + k * P, P))
                    if pair == 0 and not last:
                        squares(q + 1, 0)

            squares(0, 0)
            split_hi(eng, 0, 0)
            with eng.Fori(0, XQ - 1) as q:
                norm_quad(q, False)
            norm_quad(XQ - 1, True)
            eng.wait_ge(xs_loaded, 16)
            norm.square(eng, NCH, 4, c.x_s[:], NS)
            norm.cut_hi(eng, NCH, 0, slice(T, TW), NS)

            def tile(ii, s, kind):
                t = ii * 2 + s
                if s == 0:
                    split_hi(eng, ii, 1)
                else:
                    split_hi(eng, ii + 1, 0)
                if kind == "conv":
                    eng.wait_ge(tail_made, t + 1)
                else:
                    eng.wait_ge(y_stored, t * 16 + 16)
                for g, cols, bank in blocks():
                    eng.wait_ge(p_ready, t * NB5 + g + 2)
                    m = min(cols.stop, T) - cols.start
                    if kind == "conv":
                        ins = eng.activation(line[:, 3 + cols.start:3 + cols.start + m], bank[:, 0:m], ACT.Copy)
                    else:
                        ins = eng.activation(y[:, cols.start:cols.start + m], bank[:, 0:m],
                                             ACT.Silu if kind == "gate" else ACT.Copy)
                    if g == NB5 - 1:
                        ins = eng.activation(c.p_s[:, bass.ds(t, 1), :], bank[:, m:].unsqueeze(1), ACT.Copy)
                    ins.then_inc(bank_free, 1)
                if kind == "conv":
                    eng.wait_ge(conv_made, t + 1)
                    eng.activation(y[:], y[:], ACT.Silu).then_inc(y_made, 1)

            for kind, a, b in (("conv", 0, 6), ("gate", 6, 8), ("plain", 8, 12)):
                with eng.Fori(a, b) as ii:
                    for s in range(2):
                        tile(ii, s, kind)
            for g, cols, bank in blocks():
                eng.wait_ge(p_ready, NF * NB5 + g + 2)
                eng.activation(c.ab[:, cols], bank[0:2 * H, :], ACT.Copy).then_inc(bank_free, 1)

        @block.vector
        def _(eng):
            def split_lo(t, s):
                eng.wait_ge(whi_made, t + 1)
                eng.tensor_tensor(w_lo[s][:], w_raw[:, s], w_hi[s][:].bitcast(F32), ALU.subtract).then_inc(wlo_made, 1)

            def norm_quad(q, last):
                for k in range(4):
                    if k < 3:
                        norm.normalise(eng, q * 4 + k + 1, k + 1, q * 2 + (k + 1) // 2, k + 1, raw[k + 1])
                    elif not last:
                        norm.normalise(eng, q * 4 + 4, 0, q * 2 + 2, 0, raw[0])
                    norm.cut_lo(eng, q * 4 + k, k, bass.ds(q * (4 * P) + k * P, P))

            eng.wait_ge(gain_loaded, 16)
            norm.normalise(eng, 0, 0, 0, 0, raw[0])
            split_lo(0, 0)
            with eng.Fori(0, XQ - 1) as q:
                norm_quad(q, False)
            norm_quad(XQ - 1, True)
            norm.normalise(eng, NCH, 0, NCH // 2, 4, c.x_s[:], NS)
            norm.cut_lo(eng, NCH, 0, slice(T, TW), NS)
            eng.memset(line[:, 0:3], 0.0).then_inc(zeroed, 1)
            eng.wait_ge(zeroed, 1)
            eng.sem_inc(tail_made, 1)
            eng.wait_ge(cw_turned, 1)
            eng.tensor_copy(c.taps[:], psum[7][:, 0:NCONV * 28].rearrange("p (f r) -> p f r", r=28)).then_inc(taps_made, 1)
            eng.wait_ge(taps_made, 1)
            with eng.Fori(0, 6) as ii:
                for s in range(2):
                    t = ii * 2 + s
                    split_lo(t + 1, 1 - s)
                    eng.tensor_copy(cwt[:].unsqueeze(1), c.taps[:, bass.ds(t, 1), 24:28]).then_inc(conv, 1)
                    eng.wait_ge(conv, t * 4 + 1)
                    eng.wait_ge(bank_free, t * NB5 + NB5 + NB5)
                    eng.wait_ge(y_stored, t * 16 + 16)
                    eng.tensor_scalar(y[:], line[:, 0:T], cwt[:, 0:1], None, ALU.mult).then_inc(conv, 1)
                    for j in range(1, 4):
                        eng.wait_ge(conv, t * 4 + 1 + j)
                        ins = eng.scalar_tensor_tensor(out=y[:], in0=line[:, j:j + T], scalar=cwt[:, j:j + 1], in1=y[:],
                                                       op0=ALU.mult, op1=ALU.add)
                        if j == 3:
                            ins.then_inc(conv_made, 1)
                        else:
                            ins.then_inc(conv, 1)
                    eng.tensor_copy(c.tail[:, bass.ds(t, 1), :], line[:, T:T + 3].unsqueeze(1)).then_inc(tail_made, 1)
            with eng.Fori(6, 12) as ii:
                for s in range(2):
                    split_lo(ii * 2 + s + 1, 1 - s)

        @block.tensor
        def _(eng):
            eng.sem_inc(bank_free, NB5)
            eng.sem_inc(p_ready, 1)

            def product(t, s, m, block):
                g, cols, bank = block
                eng.wait_ge(bank_free, t * NB5 + g + 1)
                three_pass(eng, bank[0:m, :], [(w_hi[s][:, k, 0:m], w_lo[s][:, k, 0:m], h_hi[:, k, cols], h_lo[:, k, cols])
                                               for k in range(KT)]).then_inc(p_ready, 1)

            def tile(t, s, m):
                eng.wait_ge(wlo_made, t + 1)
                for block in blocks():
                    product(t, s, m, block)

            eng.wait_ge(const_made, IDENT_MADE)
            for m in range(NCH):
                norm.turn(eng, m, m % 4)
                if m % 4 == 1 and m > 4:
                    if m == 5:
                        eng.wait_ge(wlo_made, 1)
                    eng.wait_ge(norm.lo_made, (m - 1) * 2)
                    product(0, 0, P, blocks()[m // 4 - 1])
            norm.turn(eng, NCH, 0, NS)
            eng.wait_ge(norm.lo_made, 2 * NCH)
            product(0, 0, P, blocks()[3])
            eng.wait_ge(norm.lo_made, 2 * NCH + 2)
            product(0, 0, P, blocks()[4])
            eng.wait_ge(cw_loaded, 32)
            for f in range(NCONV):
                last = eng.transpose(psum[7][:, f * 28:(f + 1) * 28], cw_in[:, f * P:(f + 1) * P], c.ident[0:28, 0:28])
            last.then_inc(cw_turned, 1)
            tile(1, 1, P)
            with eng.Fori(1, 12) as ii:
                for s in range(2):
                    t = ii * 2 + s
                    tile(t, s, P)
            tile(NF, 0, 2 * H)


def softplus_gates(c, st, ab_tok, rows, cols, a_log, dtb, g, beta, tag):
    sb, sem = st.sb, c.sem
    shape = [rows, cols, H]
    x, ax, e, l1, eb, nea, eb1 = (sb(tag + n, shape if n != "nea" else [rows, H])
                                  for n in ("x", "ax", "e", "l1", "eb", "nea", "eb1"))
    own_d, own_a = Own(sem(tag + "dve")), Own(sem(tag + "act"))
    x_made, e_made, logs, g_made = sem(tag + "x_made"), sem(tag + "e_made"), sem(tag + "logs"), sem(tag + "g_made")

    def act(eng):
        eng.activation(nea[:], a_log, ACT.Exp).then_inc(e_made, 1)
        eng.wait_ge(x_made, 1)
        own_a.did(eng, eng.activation(e[:], ax[:], ACT.Exp, scale=-1.0))
        eng.activation(eb[:], ab_tok[:, :, H:2 * H], ACT.Exp, scale=-1.0).then_inc(e_made, 1)
        eng.activation(l1[:], e[:], ACT.Ln, bias=1.0).then_inc(logs, 1)

    def dve(eng):
        bc = lambda ap: ap.unsqueeze(1).to_broadcast(shape)
        own_d.did(eng, eng.tensor_tensor(x[:], ab_tok[:, :, 0:H], bc(dtb), ALU.add))
        own_d.did(eng, eng.tensor_scalar(ax[:], x[:], -1.0, None, ALU.mult))
        eng.tensor_tensor(ax[:], ax[:], x[:], ALU.max).then_inc(x_made, 1)
        own_d.did(eng, eng.tensor_scalar(x[:], x[:], 0.0, None, ALU.max))
        eng.wait_ge(e_made, 2)
        own_d.did(eng, eng.tensor_scalar(eb1[:], eb[:], 1.0, None, ALU.add))
        own_d.did(eng, eng.reciprocal(beta, eb1[:]))
        eng.wait_ge(logs, 1)
        own_d.did(eng, eng.tensor_tensor(x[:], x[:], l1[:], ALU.add))
        own_d.did(eng, eng.tensor_tensor(x[:], x[:], bc(nea[:]), ALU.mult))
        eng.tensor_scalar(g, x[:], -1.0, None, ALU.mult).then_inc(g_made, 1)

    return act, dve, g_made


def gates(c, io, st):
    nc, sem, psum = c.nc, c.sem, c.psum
    al = st.sb("al_b", [P, H])
    dtb = st.sb("dtb_b", [P, H])
    ab_turned, sums, sums_copied, loaded = sem("ab_turned"), sem("sums"), sem("sums_copied"), sem("al_loaded")
    ab_tok = psum[0][:, 0:NCH * 8].rearrange("p (c q) -> p c q", q=8)
    ga = c.ga
    g_flat = st.sb("g_flat", [P, NCH, H])
    dif = st.sb("g_dif", [P, NCH, H])
    own = Own(sem("gates_dve"))
    ga_exp = sem("ga_exp")
    act_g, dve_g, g_made = softplus_gates(c, st, ab_tok, P, NCH, al[:], dtb[:], g_flat[:], ga[:, :, 1, :], "gp_")

    def sp(eng):
        eng.dma_start(al[:], io["A_log"][0:1, :].to_broadcast([P, H])).then_inc(loaded, 16)
        eng.dma_start(dtb[:], io["dt_bias"][0:1, :].to_broadcast([P, H])).then_inc(loaded, 16)

    def pe(eng):
        for t in range(NCH):
            last = eng.transpose(psum[0][:, t * 8:(t + 1) * 8], c.ab[:, t * P:(t + 1) * P], c.ident[0:8, 0:8])
        last.then_inc(ab_turned, 1)
        eng.wait_ge(g_made, 1)
        flat = g_flat[:].rearrange("p c h -> p (c h)")
        eng.matmul(psum[1][:, 0:NCH * H], c.upto[:], flat, start=True, stop=True).then_inc(sums, 1)
        eng.matmul(psum[2][:, 0:NCH * H], c.ones[:], flat, start=True, stop=True).then_inc(sums, 1)

    def act(eng):
        eng.wait_ge(loaded, 32)
        eng.wait_ge(ab_turned, 1)
        act_g(eng)
        eng.wait_ge(sums, 2)
        upto = psum[1][:, 0:NCH * H].rearrange("p (c h) -> p c h", h=H)
        total = psum[2][:, 0:NCH * H].rearrange("p (c h) -> p c h", h=H)
        eng.activation(ga[:, :, 3, :], upto, ACT.Exp).then_inc(ga_exp, 1)
        eng.activation(ga[:, :, 5, :], total, ACT.Exp).then_inc(ga_exp, 1)
        eng.wait_ge(sums_copied, 1)
        eng.activation(ga[:, :, 4, :], dif[:], ACT.Exp).then_inc(ga_exp, 1)

    def dve(eng):
        eng.wait_ge(loaded, 32)
        eng.wait_ge(ab_turned, 1)
        dve_g(eng)
        eng.wait_ge(g_made, 1)
        own.did(eng, eng.tensor_copy(ga[:, :, 0, :], g_flat[:]))
        eng.wait_ge(ga_exp, 2)
        own.did(eng, eng.tensor_copy(ga[:, :, 2, :], psum[1][:, 0:NCH * H].rearrange("p (c h) -> p c h", h=H)))
        own.did(eng, eng.tensor_tensor(dif[:], psum[2][:, 0:NCH * H].rearrange("p (c h) -> p c h", h=H),
                                       ga[:, :, 2, :], ALU.subtract))
        eng.tensor_scalar(dif[:], dif[:], 0.0, None, ALU.min).then_inc(sums_copied, 1)
        eng.wait_ge(ga_exp, 3)

    return sp, pe, act, dve


def mix_constants(c, io, ws):
    nc, sem, psum = c.nc, c.sem, c.psum
    loaded, masked, turned, copied = sem("ws_loaded"), sem("ws_masked"), sem("ws_turned"), sem("ws_copied")

    def sp(eng):
        eng.dma_start(ws, io["w_s"][0].rearrange("h i j -> i h j")).then_inc(loaded, 16)
        eng.dma_start(c.b_col[:], io["b_s"][0].rearrange("h i -> i h"), allow_slow_non_contiguous=True).then_inc(loaded, 16)
        eng.dma_start(c.o_gain[:], io["o_norm_g"][0:1, :].to_broadcast([P, P])).then_inc(loaded, 16)
        eng.dma_start(c.v_gain[:], io["v_norm_g"][0:1, :].to_broadcast([P, HW])).then_inc(loaded, 16)

    def pool(eng):
        eng.wait_ge(loaded, 64)
        eng.affine_select(out=ws, in_=ws, compare_op=ALU.is_ge, fill=0.0, base=0,
                          pattern=[[0, H], [-1, P]], channel_multiplier=1).then_inc(masked, 1)

    def pe(eng):
        eng.wait_ge(masked, 1)
        for h in range(H):
            last = eng.transpose(head(psum[3], h), ws[:, h, :], c.ident[:])
        last.then_inc(turned, 1)

    def dve(eng):
        eng.wait_ge(turned, 1)
        eng.tensor_copy(c.wsT[:], psum[3][:, :]).then_inc(copied, 1)

    return sp, pool, pe, dve, copied


F_STEPS = "f.vg f.uq f.kb n1 n2 n3 n4 f.T1 f.T2 f.G ge g2 f.kk f.qk f.prep f.t2".split()
L_STEPS = "x1 y1 r1 x2 y2 r2 x3 y3 r3 x4 y4 r4 x5 y5 r5 x6 yt w u gm ns qs sd o".split()
O_STEPS = "o.t m0 m1 m2 m3 m4 m5 m6 m7 m8 m9 m10 m11".split()
PASS = """f.vg x1 f.uq y1 f.kb o.t r1 n1 x2 m0 y2 m1 n2 r2 m2 x3 m3 n3 y3 m4 r3 n4 m5 x4 m6 f.T1 y4 f.T2 r4 f.G
    x5 m7 ge y5 g2 f.kk r5 m8 x6 f.qk yt m9 w u gm m10 ns f.prep qs m11 sd f.t2 o""".split()
PART = 2 * KT * 3 // 12


def mix(c, io, stack):
    nc, sem, psum = c.nc, c.sem, c.psum
    st = Stage(nc, stack)
    sb = st.sb
    sqo = sb("sqo", [P, HW])
    g_sp, g_pe, g_act, g_dve = gates(c, io, st)
    w_sp, w_pool, w_pe, w_dve, ws_copied = mix_constants(c, io, heads(sqo[:]))
    wo_loaded = [sem("wo_loaded0"), sem("wo_loaded1")]
    wo_hi_made, wo_lo_made = sem("wo_hi_made"), sem("wo_lo_made")
    W_STEPS = ("m0", "m3", "m6", "m9")
    bX, bY, bR, bD, bE, bF, bG, bH = (b[:, :] for b in psum)

    def two(name, shape=(P, HW)):
        return [sb(f"{name}{i}", list(shape)) for i in range(2)]

    pt = sb("pt", [P, NF, P])
    xres = sb("xres", [P, D])
    x1 = sb("x1", [P, D])
    wo_raw = (x1[:], xres[:])
    sq = sb("sq", [P, 2 * HW])
    ss, ms, rt, rs = (sb("mx_" + n, [P, 9]) for n in ("ss", "ms", "rt", "rs"))
    qn, kn, vt, kb, qe, kT, kbT, qT, em, dif, sqv, gt = (sb(n, [P, HW]) for n in
                                                    ("qn", "kn", "vt", "kb", "qe", "kT", "kbT", "qT", "em", "dif", "sqv", "gt"))
    cg = two("cg", (P, 6, H))
    ut, gg, vbn, kbe, kd, vbt, qeT, nt, qkm = (two(n) for n in
                                               ("ut", "gg", "vbn", "kbe", "kd", "vbt", "qeT", "nt", "qkm"))
    tinv, ttinv, xs = (sb(n, [P, HW]) for n in ("tinv", "ttinv", "xs"))
    mt = two("mt")
    nwT, vn, oa, ob = (sb(n, [P, HW]) for n in ("nwT", "vn", "oa", "ob"))
    oss, oms, ort, ors = (sb("mo_" + n, [P, H]) for n in ("ss", "ms", "rt", "rs"))
    oT_hi = sb("oT_hi", [P, KT, P], F32R)
    oT_lo = sb("oT_lo", [P, KT, P], F32R)
    S = c.S

    names = """g_copied pt_loaded xres_loaded x1_stored cg_made pt_v pt_g pt_u pt_q pt_k pt_b
        qk_squared vb_squared v_copied u_copied ss_made ms_made rsqrt rs_made
        qn_made kn_made vbn_made gg_made kb_made pool_made knT kbT_ready qnT qeT_ready kT_made kbT_made qT_made qeT_made
        g_ready dif_made e_made em_made kk_ready qk_ready nt_made qkm_made tt0_part t2_made t2_turned t_copied
        m_made x_ready x_copied y_ready yt_ready t_added t_turned tt_copied tt_final
        wT_ready nwT_made gm_ready vn_ready vn_made o_ready sd_ready s_updated ob_made
        o_squared oss_made oms_made orsqrt oa_part oa_made
        oT_ready oT_hi_made oT_lo_made wo_ready x1_made S_zeroed""".split()
    s = {n: sem("m_" + n) for n in names}
    pv = io["p_dram"].rearrange("(f p) t -> p f t", p=P)
    products = [(half, k, q) for half in range(2) for k in range(KT) for q in range(3)]

    def turn(pe, bank, src):
        for h in range(H):
            last = pe.transpose(head(bank, h), head(src, h), c.ident[:])
        return last

    def turn_pt(pe, bank, group):
        for h in range(H):
            last = pe.transpose(head(bank, h), pt[:, group * H + h, :], c.ident[:])
        return last

    def by_head(pe, bank, lhsT, rhs):
        for h in range(H):
            last = pe.matmul(head(bank, h), head(lhsT, h), head(rhs, h), start=True, stop=True)
        return last

    def pe_F(pe, step, f, p):
        n = f + 1
        if step == "f.vg":
            wait(pe, s["pt_loaded"], n * 16)
            wait(pe, s["qkm_made"], f)
            turn_pt(pe, bD, 2).then_inc(s["pt_v"], 1)
            wait(pe, s["dif_made"], f)
            turn_pt(pe, bE, 3).then_inc(s["pt_g"], 1)
        elif step == "f.uq":
            wait(pe, s["nt_made"], f)
            turn_pt(pe, bF, 4).then_inc(s["pt_u"], 1)
            pe.wait_ge(s["v_copied"], n)
            turn_pt(pe, bD, 0).then_inc(s["pt_q"], 1)
        elif step == "f.kb":
            pe.wait_ge(s["g_copied"], n)
            turn_pt(pe, bE, 1).then_inc(s["pt_k"], 1)
            pe.wait_ge(s["u_copied"], n)
            turn_pt(pe, bF, 5).then_inc(s["pt_b"], 1)
        elif step == "f.T1":
            pe.wait_ge(s["kn_made"], n)
            pe.wait_ge(s["qn_made"], n)
            turn(pe, bD, kn).then_inc(s["knT"], 1)
            pe.wait_ge(s["kb_made"], n)
            turn(pe, bE, kb).then_inc(s["kbT_ready"], 1)
        elif step == "f.T2":
            pe.wait_ge(s["vbn_made"], n)
            turn(pe, bF, qn).then_inc(s["qnT"], 1)
            pe.wait_ge(s["kT_made"], n)
            pe.wait_ge(s["pool_made"], n * 4)
            turn(pe, bD, qe).then_inc(s["qeT_ready"], 1)
        elif step == "f.G":
            pe.wait_ge(s["kbT_made"], n)
            pe.wait_ge(s["cg_made"], n)
            for h in range(H):
                last = pe.transpose(head(bE, h), cg[p][:, 2, h:h + 1].to_broadcast([P, P]), c.ident[:])
            last.then_inc(s["g_ready"], 1)
        elif step == "f.kk":
            pe.wait_ge(s["qT_made"], n)
            by_head(pe, bF, kT, kbT).then_inc(s["kk_ready"], 1)
        elif step == "f.qk":
            pe.wait_ge(s["qeT_made"], n)
            by_head(pe, bD, kT, qT).then_inc(s["qk_ready"], 1)
        elif step == "f.t2":
            wait(pe, s["vn_made"], f)
            pe.wait_ge(s["t2_made"], n)
            turn(pe, bY, ttinv).then_inc(s["t2_turned"], 1)

    def pe_L(pe, step, q, p, first):
        n = q + 1
        kind, l = step[0], int(step[1]) if step[1:].isdigit() else 0
        if kind == "x":
            pe.wait_ge(s["m_made"], q * LEVELS + l)
            if l == 1:
                wait(pe, s["s_updated"], q)
                pe.wait_ge(s["t_copied"], n)
            else:
                pe.wait_ge(s["t_added"], q * (LEVELS - 1) + l - 1)
            by_head(pe, bX, mt[l % 2], tinv).then_inc(s["x_ready"], 1)
        elif step == "yt":
            pe.wait_ge(s["x_copied"], q * LEVELS + LEVELS)
            pe.wait_ge(s["tt_copied"], (q + 1) * (LEVELS - 1))
            by_head(pe, bY, xs, ttinv).then_inc(s["yt_ready"], 1)
        elif kind == "y":
            pe.wait_ge(s["x_copied"], q * LEVELS + l)
            if l > 1:
                pe.wait_ge(s["tt_copied"], q * (LEVELS - 1) + l - 1)
            by_head(pe, bY, ttinv, xs).then_inc(s["y_ready"], 1)
        elif kind == "r":
            pe.wait_ge(s["t_added"], q * (LEVELS - 1) + l)
            if l == 1:
                wait(pe, s["oa_part"], q)
            turn(pe, bR, tinv).then_inc(s["t_turned"], 1)
        elif step == "w":
            pe.wait_ge(s["tt_final"], n)
            by_head(pe, bX, kbe[p], ttinv).then_inc(s["wT_ready"], 1)
        elif step == "u":
            for h in range(H):
                pe.matmul(head(bY, h), head(ttinv, h), head(vbt[p], h), start=(h == 0), stop=False, skip_group_check=True)
        elif step == "gm":
            by_head(pe, bR, c.wsT, vbn[p]).then_inc(s["gm_ready"], 1)
        elif step == "ns":
            pe.wait_ge(s["nwT_made"], n)
            if first:
                pe.wait_ge(s["S_zeroed"], 1)
            for h in range(H):
                last = pe.matmul(head(bY, h), head(nwT, h), head(S, h), start=False, stop=(h == H - 1), skip_group_check=True)
            last.then_inc(s["vn_ready"], 1)
        elif step == "qs":
            pe.wait_ge(s["ob_made"], n)
            for h in range(H):
                pe.matmul(head(bR, h), head(qeT[p], h), head(S, h), start=(h == 0), stop=False, skip_group_check=True)
        elif step == "sd":
            pe.wait_ge(s["vn_made"], n)
            by_head(pe, bX, kd[p], vn).then_inc(s["sd_ready"], 1)
        elif step == "o":
            for h in range(H):
                last = pe.matmul(head(bR, h), head(qkm[p], h), head(vn, h), start=False, stop=(h == H - 1), skip_group_check=True)
            last.then_inc(s["o_ready"], 1)

    def pe_O(pe, step, o):
        if step == "o.t":
            pe.wait_ge(s["oa_made"], o + 1)
            pe.wait_ge(s["ob_made"], o + 1)
            wait(pe, s["x1_made"], o * 2 + 1)
            turn(pe, bG, oa).then_inc(s["oT_ready"], 1)
            turn(pe, bH, ob).then_inc(s["oT_ready"], 1)
        else:
            i = int(step[1:]) * PART
            pe.wait_ge(s["oT_lo_made"], o * 2 + (2 if i >= 12 else 1))
            for half, k, q in products[i:i + PART]:
                if (half, k, q) == (0, KT // 2, 0):
                    pe.wait_ge(s["oT_lo_made"], o * 2 + 2)
                w, v = ((c.wo_lo, oT_hi), (c.wo_hi, oT_lo), (c.wo_hi, oT_hi))[q]
                last = pe.matmul((bG, bH)[half], v[:, k, :], w[:, k, half * 512:(half + 1) * 512],
                                 start=(k == 0 and q == 0), stop=(k == KT - 1 and q == 2))
                if k == KT - 1 and q == 2:
                    last.then_inc(s["wo_ready"], 1)

    def dve_F(dve, step, f, p):
        n = f + 1
        if step == "f.vg":
            wait(dve, s["s_updated"], f - 1)
            dve.tensor_copy(cg[p][:].unsqueeze(1), c.ga[:, bass.ds(f, 1), :, :]).then_inc(s["cg_made"], 1)
        elif step == "n1":
            dve.wait_ge(s["qk_squared"], n)
            dve.tensor_reduce(ss[:, 0:8], sq[:].rearrange("p (n d) -> p n d", d=P), AX.X, ALU.add).then_inc(s["ss_made"], 1)
            dve.wait_ge(s["vb_squared"], n)
            dve.tensor_scalar(ms[:, 8:9], ss[:, 8:9], 1.0 / HW, EPS, ALU.mult, ALU.add).then_inc(s["ms_made"], 1)
            dve.wait_ge(s["ss_made"], n)
            dve.tensor_scalar(ms[:, 0:8], ss[:, 0:8], EPS, None, ALU.add).then_inc(s["ms_made"], 1)
            dve.wait_ge(s["ms_made"], n * 2)
        elif step == "n2":
            dve_rsqrt(dve, s["rsqrt"], f * DVE_RSQRT_STEPS, rs[:], ms[:], rt[:])
            dve.tensor_scalar(rs[:, 0:H], rs[:, 0:H], DK ** -0.5, None, ALU.mult).then_inc(s["rs_made"], 1)
        elif step == "n3":
            dve.tensor_tensor(heads(kn[:]), heads(bE), along(rs[:, 4:8]), ALU.mult).then_inc(s["kn_made"], 1)
            dve.wait_ge(s["rs_made"], n)
            dve.tensor_tensor(heads(qn[:]), heads(bD), along(rs[:, 0:4]), ALU.mult).then_inc(s["qn_made"], 1)
        elif step == "n4":
            dve.wait_ge(s["kn_made"], n)
            dve.wait_ge(s["cg_made"], n)
            dve.tensor_tensor(heads(kb[:]), heads(kn[:]), along(cg[p][:, 1, :]), ALU.mult).then_inc(s["kb_made"], 1)
            dve.scalar_tensor_tensor(out=vbn[p][:], in0=bF, scalar=rs[:, 8:9], in1=c.v_gain[:],
                                     op0=ALU.mult, op1=ALU.mult).then_inc(s["vbn_made"], 1)
        elif step == "f.G":
            dve.wait_ge(s["g_ready"], n)
            for h in range(H):
                ins = dve.tensor_scalar(head(dif, h), head(bE, h), cg[p][:, 2, h:h + 1], 0.0, ALU.subtract, ALU.min)
            ins.then_inc(s["dif_made"], 1)
        elif step == "g2":
            dve.wait_ge(s["e_made"], n)
            dve.tensor_tensor(heads(em[:]), heads(em[:]), across(c.upto[:]), ALU.mult).then_inc(s["em_made"], 1)
        elif step == "f.kk":
            dve.wait_ge(s["em_made"], n)
            dve.wait_ge(s["kk_ready"], n)
            dve.tensor_tensor(nt[p][:], bF, em[:], ALU.mult).then_inc(s["nt_made"], 1)
        elif step == "f.qk":
            dve.wait_ge(s["qk_ready"], n)
            dve.tensor_tensor(qkm[p][:], bD, em[:], ALU.mult).then_inc(s["qkm_made"], 1)
        elif step == "f.prep":
            dve.wait_ge(s["nt_made"], n)
            dve.tensor_tensor(heads(ttinv[:]), heads(nt[p][:]), across(c.masks[:, 0, :]), ALU.mult).then_inc(s["tt0_part"], 1)
            dve.wait_ge(s["tt0_part"], n)
            dve.tensor_tensor(heads(ttinv[:]), heads(ttinv[:]), across(c.ident[:]), ALU.add).then_inc(s["t2_made"], 1)

    def dve_L(dve, step, q, p):
        n = q + 1
        kind, l = step[0], int(step[1]) if step[1:].isdigit() else 0
        if step == "yt":
            dve.wait_ge(s["yt_ready"], n)
            dve.tensor_tensor(ttinv[:], bY, ttinv[:], ALU.add).then_inc(s["tt_final"], 1)
        elif kind == "y":
            dve.wait_ge(s["y_ready"], q * (LEVELS - 1) + l)
            if l == 1:
                dve.wait_ge(s["t_copied"], n)
            else:
                dve.wait_ge(s["t_added"], q * (LEVELS - 1) + l - 1)
            dve.tensor_tensor(tinv[:], bY, tinv[:], ALU.add).then_inc(s["t_added"], 1)
        elif step == "gm":
            dve.wait_ge(s["gm_ready"], n)
            for h in range(H):
                ins = dve.scalar_tensor_tensor(out=head(ob, h), in0=head(bR, h), scalar=c.b_col[:, h:h + 1],
                                               in1=head(ut[p], h), op0=ALU.add, op1=ALU.mult)
            ins.then_inc(s["ob_made"], 1)
        elif step == "ns":
            dve.wait_ge(s["vn_ready"], n)
            dve.tensor_copy(vn[:], bY).then_inc(s["vn_made"], 1)
        elif step == "sd":
            dve.wait_ge(s["sd_ready"], n)
            for h in range(H):
                ins = dve.scalar_tensor_tensor(out=head(S, h), in0=head(S, h), scalar=cg[p][:, 5, h:h + 1], in1=head(bX, h),
                                               op0=ALU.mult, op1=ALU.add)
            ins.then_inc(s["s_updated"], 1)
        elif step == "o":
            dve.wait_ge(s["o_squared"], n)
            dve.tensor_reduce(oss[:], heads(sqo[:]), AX.X, ALU.add).then_inc(s["oss_made"], 1)
            dve.wait_ge(s["oss_made"], n)
            dve.tensor_scalar(oms[:], oss[:], 1.0 / DK, EPS, ALU.mult, ALU.add).then_inc(s["oms_made"], 1)
            dve.wait_ge(s["oms_made"], n)
            dve_rsqrt(dve, s["orsqrt"], q * DVE_RSQRT_STEPS, ors[:], oms[:], ort[:])
            dve.tensor_tensor(heads(oa[:]), heads(bR), along(ors[:]), ALU.mult).then_inc(s["oa_part"], 1)
            dve.wait_ge(s["oa_part"], n)
            dve.wait_ge(s["gg_made"], n)
            dve.tensor_tensor(oa[:], oa[:], gg[p][:], ALU.mult).then_inc(s["oa_made"], 1)

    def dve_O(dve, step, o):
        if step == "o.t":
            for i, bank in enumerate((bG, bH)):
                dve.wait_ge(s["oT_hi_made"], o * 2 + 1 + i)
                dve.tensor_tensor(oT_lo[:, 4 * i:4 * i + 4, :], heads(bank), oT_hi[:, 4 * i:4 * i + 4, :].bitcast(F32),
                                  ALU.subtract).then_inc(s["oT_lo_made"], 1)
        elif step in ("m5", "m11"):
            half = 0 if step == "m5" else 1
            cols = slice(half * 512, (half + 1) * 512)
            dve.wait_ge(s["wo_ready"], o * 2 + 1 + half)
            dve.wait_ge(s["xres_loaded"], o * 16 + 16)
            dve.wait_ge(s["x1_stored"], o * 16 + 16)
            dve.tensor_tensor(x1[:, cols], (bG, bH)[half], xres[:, cols], ALU.add).then_inc(s["x1_made"], 1)

    def act_F(act, step, f, p):
        n = f + 1
        if step == "f.vg":
            act.wait_ge(s["pt_v"], n)
            wait(act, s["pool_made"], f * 4)
            act.activation(vt[:], bD, ACT.Copy).then_inc(s["v_copied"], 1)
            wait(act, s["gg_made"], f)
            act.wait_ge(s["pt_g"], n)
            act.activation(gt[:], bE, ACT.Copy).then_inc(s["g_copied"], 1)
        elif step == "f.uq":
            wait(act, s["ob_made"], f - 1)
            act.wait_ge(s["pt_u"], n)
            act.activation(ut[p][:], bF, ACT.Copy).then_inc(s["u_copied"], 1)
            act.wait_ge(s["pt_q"], n)
            act.activation(sq[:, 0:HW], bD, ACT.Square)
        elif step == "f.kb":
            act.wait_ge(s["pt_k"], n)
            act.activation(sq[:, HW:2 * HW], bE, ACT.Square).then_inc(s["qk_squared"], 1)
            act.wait_ge(s["pt_b"], n)
            act.activation(sqv[:], bF, ACT.Square, accum_out=ss[:, 8:9]).then_inc(s["vb_squared"], 1)
        elif step == "f.T1":
            act.wait_ge(s["knT"], n)
            act.activation(kT[:], bD, ACT.Copy).then_inc(s["kT_made"], 1)
            act.wait_ge(s["kbT_ready"], n)
            act.activation(kbT[:], bE, ACT.Copy).then_inc(s["kbT_made"], 1)
        elif step == "f.T2":
            act.wait_ge(s["qnT"], n)
            act.activation(qT[:], bF, ACT.Copy).then_inc(s["qT_made"], 1)
            act.wait_ge(s["qeT_ready"], n)
            act.activation(qeT[p][:], bD, ACT.Copy).then_inc(s["qeT_made"], 1)
        elif step == "ge":
            act.wait_ge(s["dif_made"], n)
            act.activation(em[:], dif[:], ACT.Exp).then_inc(s["e_made"], 1)
        elif step == "f.t2":
            act.wait_ge(s["t2_turned"], n)
            act.activation(tinv[:], bY, ACT.Copy).then_inc(s["t_copied"], 1)

    def act_L(act, step, q, p):
        n = q + 1
        kind, l = step[0], int(step[1]) if step[1:].isdigit() else 0
        if kind == "x":
            act.wait_ge(s["x_ready"], q * LEVELS + l)
            act.activation(xs[:], bX, ACT.Copy).then_inc(s["x_copied"], 1)
        elif kind == "r":
            act.wait_ge(s["t_turned"], q * (LEVELS - 1) + l)
            act.activation(ttinv[:], bR, ACT.Copy).then_inc(s["tt_copied"], 1)
        elif step == "w":
            act.wait_ge(s["wT_ready"], n)
            act.activation(nwT[:], bX, ACT.Copy, scale=-1.0).then_inc(s["nwT_made"], 1)
        elif step == "o":
            act.wait_ge(s["o_ready"], n)
            act.activation(sqo[:], bR, ACT.Square).then_inc(s["o_squared"], 1)

    def act_O(act, step, o):
        if step == "o.t":
            for i, bank in enumerate((bG, bH)):
                act.wait_ge(s["oT_ready"], o * 2 + 1 + i)
                act.activation(oT_hi[:, 4 * i:4 * i + 4, :], heads(bank), ACT.Copy).then_inc(s["oT_hi_made"], 1)

    def pool_F(pool, step, f, p):
        n = f + 1
        if step == "f.vg":
            pool.wait_ge(s["g_copied"], n)
            wait(pool, s["oa_made"], f - 1)
            pool.tensor_tensor(heads(gg[p][:]), heads(gt[:]), across(c.o_gain[:]), ALU.mult).then_inc(s["gg_made"], 1)
        elif step == "n3":
            pool.wait_ge(s["qn_made"], n)
            pool.tensor_tensor(heads(qe[:]), heads(qn[:]), along(cg[p][:, 3, :]), ALU.mult).then_inc(s["pool_made"], 1)
            pool.tensor_tensor(heads(kd[p][:]), heads(kn[:]), along(cg[p][:, 4, :]), ALU.mult).then_inc(s["pool_made"], 1)
            pool.wait_ge(s["v_copied"], n)
            pool.tensor_tensor(heads(vbt[p][:]), heads(vt[:]), along(cg[p][:, 1, :]), ALU.mult).then_inc(s["pool_made"], 1)
            pool.wait_ge(s["kb_made"], n)
            pool.tensor_tensor(heads(kbe[p][:]), heads(kb[:]), along(cg[p][:, 3, :]), ALU.mult).then_inc(s["pool_made"], 1)

    def pool_mask(pool, q, l, p):
        wait(pool, s["x_ready"], q * LEVELS + l - 2)
        pool.tensor_tensor(heads(mt[l % 2][:]), heads(nt[p][:]), across(c.masks[:, l, :]), ALU.mult).then_inc(s["m_made"], 1)

    def pool_L(pool, step, q, p):
        if step[0] == "x" and int(step[1]) + 2 <= LEVELS:
            pool_mask(pool, q, int(step[1]) + 2, p)

    def cut_w_o(eng, which, k):
        if which == "hi":
            eng.wait_ge(wo_loaded[k % 2], 16 * (k // 2) + 16)
            eng.activation(c.wo_hi[:, k, :], wo_raw[k % 2], ACT.Copy).then_inc(wo_hi_made, 1)
        elif which == "lo":
            eng.wait_ge(wo_hi_made, k + 1)
            eng.tensor_tensor(c.wo_lo[:, k, :], wo_raw[k % 2], c.wo_hi[:, k, :].bitcast(F32), ALU.subtract).then_inc(wo_lo_made, 1)

    def one_pass(eng, F, L, O, f, which=None):
        chunk, par = f
        for step in PASS:
            if which and step in W_STEPS:
                cut_w_o(eng, which, chunk * len(W_STEPS) + W_STEPS.index(step))
            if step in F_STEPS and F:
                F(eng, step, chunk, par)
            if step in L_STEPS and L:
                L(eng, step, chunk - 1, 1 - par)
            if step in O_STEPS and O:
                O(eng, step, chunk - 2)

    def all_passes(eng, F, L, O, L_first=None, which=None):
        one_pass(eng, F, None, None, (0, 0), which)
        one_pass(eng, F, L_first or L, None, (1, 1), which)
        if L_first:
            eng.wait_ge(wo_lo_made, KT)
        with eng.Fori(0, NCH // 2 - 1) as ii:
            for par in range(2):
                one_pass(eng, F, L, O, (ii * 2 + 2 + par, par))
        one_pass(eng, None, L, O, (NCH, 0))
        one_pass(eng, None, None, O, (NCH + 1, 1))

    with nc.Block() as block:
        @block.sync
        def _(sp):
            def load_pt(f):
                wait(sp, s["pt_b"], f)
                sp.dma_start(pt[:], pv[:, :, bass.ds(f * P, P)]).then_inc(s["pt_loaded"], 16)

            def rows(o):
                sp.dma_start(xres[:], io["x_prompt"][0, bass.ds(o * P, P), :]).then_inc(s["xres_loaded"], 16)
                sp.wait_ge(s["x1_made"], o * 2 + 3)
                sp.dma_start(io["x1_dram"][bass.ds(o * P, P), :], x1[:]).then_inc(s["x1_stored"], 16)

            def load_w_o(k):
                wait(sp, wo_lo_made, k - 1)
                sp.dma_start(wo_raw[k % 2], io["w_o"][0, k * P:(k + 1) * P, :]).then_inc(wo_loaded[k % 2], 16)

            g_sp(sp)
            w_sp(sp)
            load_pt(0)
            load_w_o(0)
            load_w_o(1)
            load_pt(1)
            for k in range(2, 6):
                load_w_o(k)
            load_pt(2)
            load_w_o(6)
            load_w_o(7)
            sp.wait_ge(wo_lo_made, KT)
            with sp.Fori(0, NCH - 3) as o:
                load_pt(o + 3)
                rows(o)
            for o in range(NCH - 3, NCH):
                rows(o)
            sp.wait_ge(s["s_updated"], NCH)
            sp.dma_start(io["new_delta_prompt"][0, 0].rearrange("h k v -> k h v"), heads(S[:])).then_inc(s["x1_stored"], 16)
            sp.wait_ge(s["x1_stored"], NCH * 16 + 32)

        @block.tensor
        def _(pe):
            g_pe(pe)
            w_pe(pe)
            pe.wait_ge(ws_copied, 1)
            all_passes(pe, pe_F, lambda e, st_, q, p: pe_L(e, st_, q, p, False), pe_O,
                       lambda e, st_, q, p: pe_L(e, st_, q, p, True))

        @block.vector
        def _(dve):
            dve.memset(S[:], 0.0).then_inc(s["S_zeroed"], 1)
            dve.wait_ge(s["S_zeroed"], 1)
            dve.sem_inc(s["x1_stored"], 16)
            dve.sem_inc(s["x1_made"], 1)
            g_dve(dve)
            w_dve(dve)
            all_passes(dve, dve_F, dve_L, dve_O, which="lo")

        @block.scalar
        def _(act):
            g_act(act)
            all_passes(act, act_F, act_L, act_O, which="hi")

        @block.gpsimd
        def _(pool):
            def pool_step(eng, step, f, p):
                pool_F(eng, step, f, p)
                if step == "f.prep":
                    eng.wait_ge(s["nt_made"], f + 1)
                    pool_mask(eng, f, 1, p)
                    pool_mask(eng, f, 2, p)
            w_pool(pool)
            all_passes(pool, pool_step, pool_L, None)


def sample(c, io, stack):
    nc, sem, psum = c.nc, c.sem, c.psum
    st = Stage(nc, stack)
    sb = st.sb
    N = NS
    names = """states_loaded small_loaded acc_made silu_made raw_turned turned ab_turned tok_made squared ms_made
        rsqrt knT_ready kT_made kv_ready qs_ready egb_made s_decayed delta_made outer_ready outer_added o_summed osq oms_made
        o_made oT_ready oT_hi_made oT_lo_made y_ready stored rows_made rest_made eg_ready eg_made masks_made""".split()
    s = {n: sem("s_" + n) for n in names}
    own_d, own_a = Own(sem("s_dve")), Own(sem("s_act"))

    states = sb("states", [P, N * H, DK])
    al, dtb = sb("s_al", [N, H]), sb("s_dtb", [N, H])
    w00, b00 = sb("s_w00", [N, H]), sb("s_b00", [N, H])
    acc, part = sb("s_acc", [P, NCONV, N]), sb("s_part", [P, NCONV, N])
    qkvT, gateT = sb("s_qkvT", [P, NCONV, N]), sb("s_gateT", [P, H, N])
    rows = sb("s_rows", [N, QKV])
    prow = sb("s_prow", [3, QKV])
    tok = [sb(f"s_tok{i}", [N, HW]) for i in range(6)]
    sq = sb("s_sq", [N, 3 * HW])
    ss, ms, rt, rs = (sb("s_" + n, [N, 9]) for n in ("ss", "ms", "rt", "rs"))
    oss, oms, ort, ors = (sb("so_" + n, [N, H]) for n in ("ss", "ms", "rt", "rs"))
    g, beta, eg = sb("s_g", [N, 1, H]), sb("s_beta", [N, 1, H]), sb("s_eg", [N, H])
    egm, egb = sb("s_egm", [N, N, H]), sb("s_egb", [P, N, H])
    kT, qT = sb("s_kT", [P, H, N]), sb("s_qT", [P, H, N])
    km, qm = sb("s_km", [P, H, N, N]), sb("s_qm", [P, H, N, N])
    delta, o, qk_prod, qkd = sb("s_delta", [N, HW]), sb("s_o", [N, HW]), sb("s_qk_prod", [N, HW]), sb("s_qkd", [N, H])
    dmask = sb("s_dmask", [N, H, N, DK])
    oa, ob = sb("s_oa", [N, HW]), sb("s_ob", [N, HW])
    og, vg = sb("s_og", [N, HW]), sb("s_vg", [N, HW])
    oT_hi, oT_lo = sb("s_oT_hi", [P, KT, N], F32R), sb("s_oT_lo", [P, KT, N], F32R)
    i8 = c.ident[0:N, 0:N]
    bank = [b[0:N, :] for b in psum]
    outer_banks = [psum[i][:, :] for i in (1, 2, 5, 6)]
    y_banks = (bank[3], bank[0])
    act_g, dve_g, g_made = softplus_gates(c, st, psum[6][0:N, 0:8].unsqueeze(1), N, 1, al[:], dtb[:],
                                          g[:], beta[:], "gs_")
    st_view = states[:].rearrange("p (b h) v -> p b h v", h=H)

    with nc.Block() as block:
        @block.sync
        def _(eng):
            eng.dma_start(al[:], io["A_log"][0:1, :].to_broadcast([N, H])).then_inc(s["small_loaded"], 16)
            eng.dma_start(dtb[:], io["dt_bias"][0:1, :].to_broadcast([N, H])).then_inc(s["small_loaded"], 16)
            eng.dma_start(w00[:], io["w_s"][0, :, 0, 0:1].rearrange("h o -> o h").to_broadcast([N, H]),
                          allow_slow_non_contiguous=True).then_inc(s["small_loaded"], 16)
            eng.dma_start(b00[:], io["b_s"][0, :, 0:1].rearrange("h o -> o h").to_broadcast([N, H]),
                          allow_slow_non_contiguous=True).then_inc(s["small_loaded"], 16)
            eng.dma_start(states[:], io["state_delta"][0].rearrange("b h k v -> k (b h) v")).then_inc(s["states_loaded"], 16)
            eng.dma_start(io["new_conv_sample"][0, :, 0:2, :], io["state_conv"][0, :, 1:3, :]).then_inc(s["stored"], 16)
            eng.wait_ge(s["rows_made"], 6)
            eng.dma_start(io["new_conv_sample"][0, :, 2, :], rows[:]).then_inc(s["stored"], 16)
            eng.dma_start(io["new_conv_prompt"][0, 0], prow[:]).then_inc(s["stored"], 16)
            eng.wait_ge(s["tok_made"], 1)
            eng.dma_start(io["new_gmlp_v_sample"][0, :, 0, :], tok[5][:]).then_inc(s["stored"], 16)
            eng.wait_ge(s["outer_added"], 8)
            eng.dma_start(io["new_delta_sample"][0].rearrange("b h k v -> k (b h) v"), states[:]).then_inc(s["stored"], 16)
            eng.wait_ge(s["stored"], 16 * 5)

        @block.tensor
        def _(pe):
            for f in range(NCONV):
                pe.transpose(bank[f // 4][:, (f % 4) * P:(f % 4 + 1) * P], c.p_s[:, f, :], c.ident[:])
            for f in range(NCONV):
                last = pe.transpose(psum[3 + f // 4][0:3, (f % 4) * P:(f % 4 + 1) * P], c.tail[:, f, :], c.ident[:])
            last.then_inc(s["raw_turned"], 1)
            pe.transpose(bank[6][:, 0:8], c.ab[:, T:TW], c.ident[0:8, 0:8]).then_inc(s["ab_turned"], 1)
            pe.wait_ge(s["rows_made"], 6)
            pe.wait_ge(s["silu_made"], 2)
            for f in range(NCONV):
                pe.transpose(bank[f // 4][:, (f % 4) * P:(f % 4 + 1) * P], qkvT[:, f, :], c.ident[:])
            for f in range(H):
                pe.transpose(bank[3][:, f * P:(f + 1) * P], gateT[:, f, :], c.ident[:])
            for f in range(2 * H):
                last = pe.transpose(bank[4 + f // 4][:, (f % 4) * P:(f % 4 + 1) * P], c.p_s[:, 4 * H + f, :], c.ident[:])
            last.then_inc(s["turned"], 1)
            pe.wait_ge(s["tok_made"], 1)
            for i, t in enumerate((tok[1], tok[0])):
                for h in range(H):
                    last = pe.transpose(psum[7][:, (i * H + h) * N:(i * H + h + 1) * N], head(t, h), i8)
            last.then_inc(s["knT_ready"], 1)
            pe.wait_ge(s["eg_made"], 1)
            pe.matmul(psum[3][:, 0:N * H], c.ones[0:N, :], egm[:].rearrange("t b h -> t (b h)"), start=True, stop=True).then_inc(s["eg_ready"], 1)
            pe.wait_ge(s["states_loaded"], 16)
            pe.wait_ge(s["masks_made"], 1)
            for h in range(H):
                for b in range(N):
                    last = pe.matmul(head(bank[0], h), km[:, h, b, :], states[:, b * H + h, :], start=(b == 0), stop=(b == N - 1))
            last.then_inc(s["kv_ready"], 1)
            for h in range(H):
                for b in range(N):
                    last = pe.matmul(head(bank[4], h), qm[:, h, b, :], states[:, b * H + h, :], start=(b == 0), stop=(b == N - 1))
            last.then_inc(s["qs_ready"], 1)

            def outer(u):
                h, half = u // 2, u % 2
                pe.wait_ge(s["delta_made"], h + 1)
                wait(pe, s["outer_added"], u - 3)
                pe.matmul(outer_banks[u % 4], head(tok[1], h),
                          dmask[:, h, 4 * half:4 * half + 4, :].rearrange("t b v -> t (b v)"),
                          start=True, stop=True).then_inc(s["outer_ready"], 1)

            for u in range(4):
                outer(u)
            pe.wait_ge(s["o_made"], 1)
            for i, t in enumerate((oa, ob)):
                for h in range(H):
                    last = pe.transpose(psum[7][:, (i * H + h) * N:(i * H + h + 1) * N], head(t, h), i8)
            last.then_inc(s["oT_ready"], 1)
            pe.wait_ge(s["oT_lo_made"], 1)
            for half in range(2):
                cols = slice(half * 512, (half + 1) * 512)
                three_pass(pe, y_banks[half], [(oT_hi[:, k, :], oT_lo[:, k, :], c.wo_hi[:, k, cols], c.wo_lo[:, k, cols])
                                               for k in range(KT)]).then_inc(s["y_ready"], 1)
            for u in range(4, 8):
                outer(u)

        @block.gpsimd
        def _(pool):
            pool.wait_ge(s["egb_made"], 1)
            pool.wait_ge(s["qs_ready"], 1)
            for u in range(8):
                h, half = u // 2, u % 2
                part_s = st_view[:, 4 * half:4 * half + 4, h, :]
                pool.tensor_tensor(part_s, part_s, along(egb[:, 4 * half:4 * half + 4, h], DK), ALU.mult).then_inc(s["s_decayed"], 1)

        @block.scalar
        def _(act):
            act.wait_ge(s["small_loaded"], 64)
            act.wait_ge(s["acc_made"], 1)
            act.activation(qkvT[:], acc[:], ACT.Silu).then_inc(s["silu_made"], 1)
            act.activation(gateT[:], c.p_s[:, NCONV:NCONV + H, :], ACT.Silu).then_inc(s["silu_made"], 1)
            act.wait_ge(s["ab_turned"], 1)
            act_g(act)
            act.wait_ge(s["turned"], 1)
            for i, bk in enumerate((0, 1, 5)):
                act.activation(sq[:, i * HW:(i + 1) * HW], bank[bk], ACT.Square).then_inc(s["squared"], 1)
            act.wait_ge(g_made, 1)
            own_a.did(act, act.activation(eg[:], g[:, 0, :], ACT.Exp))
            act.activation(egm[:, 0, :], eg[:], ACT.Copy).then_inc(s["rest_made"], 1)
            act.wait_ge(s["o_summed"], 1)
            act.activation(sq[:, 0:HW], o[:], ACT.Square).then_inc(s["osq"], 1)
            act.wait_ge(s["oT_ready"], 1)
            act.activation(oT_hi[:], psum[7][:, 0:KT * N].rearrange("p (k t) -> p k t", k=KT), ACT.Copy).then_inc(s["oT_hi_made"], 1)

        @block.vector
        def _(dve):
            did = lambda ins: own_d.did(dve, ins)
            old = c.taps[:, :, 0:24].rearrange("p f (b j) -> p f b j", j=3)
            tap = lambda j: c.taps[:, :, 24 + j:25 + j].to_broadcast([P, NCONV, N])
            did(dve.tensor_tensor(acc[:], old[:, :, :, 0], tap(0), ALU.mult))
            for j in (1, 2):
                did(dve.tensor_tensor(part[:], old[:, :, :, j], tap(j), ALU.mult))
                did(dve.tensor_tensor(acc[:], acc[:], part[:], ALU.add))
            did(dve.tensor_tensor(part[:], c.p_s[:, 0:NCONV, :], tap(3), ALU.mult))
            dve.tensor_tensor(acc[:], acc[:], part[:], ALU.add).then_inc(s["acc_made"], 1)
            dve.wait_ge(s["raw_turned"], 1)
            for i in range(3):
                dve.tensor_copy(rows[:, i * 512:(i + 1) * 512], bank[i]).then_inc(s["rows_made"], 1)
                dve.tensor_copy(prow[:, i * 512:(i + 1) * 512], psum[3 + i][0:3, :]).then_inc(s["rows_made"], 1)
            dve.wait_ge(s["small_loaded"], 64)
            dve.wait_ge(s["ab_turned"], 1)
            dve_g(dve)
            dve.wait_ge(s["squared"], 3)
            did(dve.tensor_reduce(ss[:, 0:8], sq[:, 0:2 * HW].rearrange("p (n d) -> p n d", d=P), AX.X, ALU.add))
            did(dve.tensor_reduce(ss[:, 8:9], sq[:, 2 * HW:3 * HW], AX.X, ALU.add))
            did(dve.tensor_scalar(ms[:, 0:8], ss[:, 0:8], EPS, None, ALU.add))
            dve.tensor_scalar(ms[:, 8:9], ss[:, 8:9], 1.0 / HW, EPS, ALU.mult, ALU.add).then_inc(s["ms_made"], 1)
            dve.wait_ge(s["ms_made"], 1)
            dve_rsqrt(dve, s["rsqrt"], 0, rs[:], ms[:], rt[:])
            did(dve.tensor_scalar(rs[:, 0:4], rs[:, 0:4], DK ** -0.5, None, ALU.mult))
            did(dve.tensor_tensor(heads(tok[0][:]), heads(bank[0]), along(rs[:, 0:4]), ALU.mult))
            did(dve.tensor_tensor(heads(tok[1][:]), heads(bank[1]), along(rs[:, 4:8]), ALU.mult))
            did(dve.tensor_copy(tok[2][:], bank[2]))
            did(dve.tensor_tensor(heads(tok[3][:]), heads(bank[3]), across(c.o_gain[0:N, :]), ALU.mult))
            did(dve.tensor_copy(tok[4][:], bank[4]))
            dve.scalar_tensor_tensor(out=tok[5][:], in0=bank[5], scalar=rs[:, 8:9], in1=c.v_gain[0:N, :],
                                     op0=ALU.mult, op1=ALU.mult).then_inc(s["tok_made"], 1)
            dve.wait_ge(s["rest_made"], 1)
            dve.tensor_tensor(egm[:], eg[:].unsqueeze(1).to_broadcast([N, N, H]), along(i8, H), ALU.mult).then_inc(s["eg_made"], 1)
            dve.wait_ge(s["knT_ready"], 1)
            did(dve.tensor_copy(kT[:], psum[7][:, 0:H * N].rearrange("p (h t) -> p h t", h=H)))
            did(dve.tensor_copy(qT[:], psum[7][:, H * N:2 * H * N].rearrange("p (h t) -> p h t", h=H)))
            for h in range(H):
                dve.tensor_tensor(km[:, h], kT[:, h, :].unsqueeze(1).to_broadcast([P, N, N]), c.eye8[:], ALU.mult)
                ins = dve.tensor_tensor(qm[:, h], qT[:, h, :].unsqueeze(1).to_broadcast([P, N, N]), c.eye8[:], ALU.mult)
            ins.then_inc(s["masks_made"], 1)
            dve.wait_ge(s["eg_ready"], 1)
            dve.tensor_copy(egb[:], psum[3][:, 0:N * H].rearrange("p (b h) -> p b h", h=H)).then_inc(s["egb_made"], 1)
            did(dve.tensor_tensor(qk_prod[:], tok[0][:], tok[1][:], ALU.mult))
            did(dve.tensor_reduce(qkd[:], heads(qk_prod[:]), AX.X, ALU.add))
            dve.wait_ge(s["kv_ready"], 1)
            did(dve.tensor_tensor(heads(delta[:]), heads(bank[0]), along(eg[:]), ALU.mult))
            did(dve.tensor_tensor(delta[:], tok[2][:], delta[:], ALU.subtract))
            did(dve.tensor_tensor(heads(delta[:]), heads(delta[:]), along(beta[:, 0, :]), ALU.mult))

            def delta_diagonal(h):
                dve.tensor_tensor(dmask[:, h], across(head(delta, h), N), along(i8, DK), ALU.mult).then_inc(s["delta_made"], 1)

            delta_diagonal(0)
            delta_diagonal(1)
            did(dve.tensor_tensor(heads(qk_prod[:]), heads(delta[:]), along(qkd[:]), ALU.mult))
            dve.wait_ge(s["qs_ready"], 1)
            did(dve.tensor_tensor(heads(o[:]), heads(bank[4]), along(eg[:]), ALU.mult))
            dve.tensor_tensor(o[:], o[:], qk_prod[:], ALU.add).then_inc(s["o_summed"], 1)
            did(dve.tensor_tensor(heads(ob[:]), heads(tok[5][:]), along(w00[:]), ALU.mult))
            did(dve.tensor_tensor(heads(ob[:]), heads(ob[:]), along(b00[:]), ALU.add))
            did(dve.tensor_tensor(ob[:], ob[:], tok[4][:], ALU.mult))
            dve.wait_ge(s["osq"], 1)
            did(dve.tensor_reduce(oss[:], heads(sq[:, 0:HW]), AX.X, ALU.add))
            dve.tensor_scalar(oms[:], oss[:], 1.0 / DK, EPS, ALU.mult, ALU.add).then_inc(s["oms_made"], 1)
            dve.wait_ge(s["oms_made"], 1)
            dve_rsqrt(dve, s["rsqrt"], DVE_RSQRT_STEPS, ors[:], oms[:], ort[:])
            did(dve.tensor_tensor(heads(oa[:]), heads(o[:]), along(ors[:]), ALU.mult))
            dve.tensor_tensor(oa[:], oa[:], tok[3][:], ALU.mult).then_inc(s["o_made"], 1)

            def update(u):
                h, half = u // 2, u % 2
                part_s = st_view[:, 4 * half:4 * half + 4, h, :]
                dve.wait_ge(s["s_decayed"], u + 1)
                dve.wait_ge(s["outer_ready"], u + 1)
                dve.tensor_tensor(part_s, outer_banks[u % 4].rearrange("p (b v) -> p b v", b=4), part_s,
                                  ALU.add).then_inc(s["outer_added"], 1)

            delta_diagonal(2)
            delta_diagonal(3)
            dve.wait_ge(s["oT_hi_made"], 1)
            dve.tensor_tensor(oT_lo[:], psum[7][:, 0:KT * N].rearrange("p (k t) -> p k t", k=KT), oT_hi[:].bitcast(F32),
                              ALU.subtract).then_inc(s["oT_lo_made"], 1)
            for u in range(4):
                update(u)
            for half in range(2):
                cols = slice(half * 512, (half + 1) * 512)
                dve.wait_ge(s["y_ready"], half + 1)
                did(dve.tensor_tensor(c.x_s[:, cols], y_banks[half], c.x_s[:, cols], ALU.add))
            for u in range(4, 8):
                update(u)


def ffn(c, io, stack):
    nc, sem, psum = c.nc, c.sem, c.psum
    st = Stage(nc, stack)
    sb = lambda name, shape, dt=F32: st.sb("f_" + name, shape, dt)
    n = NS
    W = BLK + n
    ACCS = 12
    acc = sb("acc", [P, ACCS, D])
    h_hi = sb("h_hi", [P, KT, W], F32R)
    h_lo = sb("h_lo", [P, KT, W], F32R)
    up_raw = sb("up_raw", [P, 2, KT, P])
    dn_raw = sb("dn_raw", [P, D])
    up_hi = [sb(f"up_hi{i}", [P, KT, P], F32R) for i in range(2)]
    up_lo = [sb(f"up_lo{i}", [P, KT, P], F32R) for i in range(2)]
    dn_hi = sb("dn_hi", [P, GH, D], F32R)
    dn_lo = sb("dn_lo", [P, GH, D], F32R)
    z_hi = sb("z_hi", [P, GH, W], F32R)
    z_lo = sb("z_lo", [P, GH, W], F32R)
    NZ = 3
    ZW = W // NZ
    ZB = 4
    relu = sb("relu", [P, NZ * ZW])
    sqr = sb("sqr", [P, ZW])
    xn = sb("xn", [P, 2, D])
    gain, fgain = sb("gain", [P, D]), sb("fgain", [P, D])
    names = """up_loaded0 up_loaded1 dn_loaded up_hi_made up_lo_made dn_hi_made dn_lo_made z_ready relu_made zhi_made
        sqr_made zlo_made y_ready y_added gain_loaded fgain_loaded""".split()
    s = {nm: sem("f_" + nm) for nm in names}
    up_loaded = [s["up_loaded0"], s["up_loaded1"]]
    acc_loaded = [[sem(f"acc_loaded{b}_{i}") for i in range(4)] for b in range(2)]
    out_made = [sem(f"out_made{b}") for b in range(2)]
    row_scaled = sem("row_scaled")
    stored = [sem(f"stored{i}") for i in range(2)]
    junk = relu[:, 0:D]
    norms = [Norm(c, st, f"fn{b}_", gain, junk, xn, h_hi, h_lo, lambda k, half: psum[2 + half], True) for b in range(2)]
    finals = [Stats(c, st, f"ff{b}_", junk) for b in range(2)]
    w_up = io["w_up"][0].rearrange("(k p) n -> p k n", p=P)
    w_down = io["w_down"][0]
    NTL = FF // P
    UNITS = (2 * NBT, 2 * NBT + 2)

    def slot(blk, m):
        return acc[:, (blk * NBT + m) % ACCS, :]

    def zblocks(blk, i):
        ends = (ZW, 2 * ZW, W if blk else BLK)
        return [(b, slice(b * ZW, ends[b]), psum[(i * NZ + b) % ZB][:, 0:ends[b] - b * ZW]) for b in range(NZ)]

    def units(blk):
        out = [(u, slice((u // 2) * P, (u // 2 + 1) * P), u % 2, psum[ZB + u % ZB][:, :],
                slot(blk, u // 2)[:, (u % 2) * 512:(u % 2 + 1) * 512]) for u in range(2 * NBT)]
        if blk == 1:
            out += [(u, slice(BLK, W), u % 2, psum[ZB + u % ZB][0:n, :], c.x_s[:, (u % 2) * 512:(u % 2 + 1) * 512])
                    for u in range(2 * NBT, UNITS[1])]
        return out

    def outputs_before(blk, gi):
        return (NG * UNITS[0] if blk else 0) + gi * UNITS[blk]

    with nc.Block() as block:
        @block.sync
        def _(eng):
            def load_rows(blk, m):
                row = blk * BLK + m * P
                eng.dma_start(slot(blk, m), io["x1_dram"][row:row + P, :]).then_inc(acc_loaded[blk][m % 4], 16)

            def store_rows(blk, m):
                row = blk * BLK + m * P
                eng.wait_ge(out_made[blk], m + 1)
                eng.dma_start(io["y_prompt"][0, row:row + P, :], slot(blk, m)).then_inc(stored[m % 2], 16)

            def weights(tn, p, up, dn):
                if up is not None:
                    eng.wait_ge(s["up_lo_made"], tn + 1)
                    eng.dma_start(up_raw[:, p], w_up[:, :, bass.ds(up * P, P)]).then_inc(up_loaded[p], 16)
                if dn is not None:
                    eng.wait_ge(s["dn_lo_made"], tn + 1)
                    eng.dma_start(dn_raw[:], w_down[bass.ds(dn * P, P), :]).then_inc(s["dn_loaded"], 16)

            eng.dma_start(gain[:], io["norm_ffn_g"][0:1, :].to_broadcast([P, D])).then_inc(s["gain_loaded"], 16)
            for m in range(4):
                load_rows(0, m)
            eng.dma_start(up_raw[:, 0], w_up[:, :, 0:P]).then_inc(up_loaded[0], 16)
            for m in range(4, NBT):
                eng.wait_ge(norms[0].xn_made, m - 3)
                load_rows(0, m)
            eng.dma_start(up_raw[:, 1], w_up[:, :, P:2 * P]).then_inc(up_loaded[1], 16)
            eng.dma_start(dn_raw[:], w_down[0:P, :]).then_inc(s["dn_loaded"], 16)
            eng.dma_start(fgain[:], io["norm_f_g"].rearrange("(a d) -> a d", a=1).to_broadcast([P, D])).then_inc(s["fgain_loaded"], 16)
            for m in range(4):
                load_rows(1, m)
            for blk in range(2):
                base = blk * NTL
                with eng.Fori(0, NTL // 2 - 1) as ii:
                    for p in range(2):
                        weights(base + ii * 2 + p, p, ii * 2 + p + 2, ii * 2 + p + 1)
                if blk == 0:
                    weights(NTL - 2, 0, 0, NTL - 1)
                    weights(NTL - 1, 1, 1, 0)
                    for m in range(NBT):
                        if 2 <= m < 6:
                            eng.wait_ge(stored[m % 2], 16 * (m // 2))
                            load_rows(1, m + 2)
                        elif m >= 6:
                            eng.wait_ge(stored[m % 2], 16 * (m // 2))
                        if m < 4:
                            store_rows(0, m)
                        elif m == 5:
                            store_rows(0, 4)
                            store_rows(0, 5)
                        elif m > 5:
                            store_rows(0, m)
                else:
                    weights(2 * NTL - 2, 0, None, NTL - 1)
            for m in range(NBT):
                eng.wait_ge(stored[m % 2], 16 * (NBT // 2 + m // 2))
                store_rows(1, m)
            eng.wait_ge(out_made[1], NBT + 1)
            eng.wait_ge(stored[0], 16 * NBT)
            eng.dma_start(io["y_sample"].rearrange("b s d -> (b s) d"), c.x_s[:]).then_inc(stored[0], 16)
            eng.wait_ge(stored[0], 16 * NBT + 16)
            eng.wait_ge(stored[1], 16 * NBT)

        @block.gpsimd
        def _(pool):
            for pair in range(NBT // 2):
                norms[0].scales(pool, pair, 2 * pair)
            norms[1].scales(pool, 0, 0)
            norms[1].scales(pool, 1, 2)
            pool.wait_ge(s["fgain_loaded"], 16)
            for pair in range(2):
                finals[0].scales(pool, pair, 2 * pair)
                for m in (2 * pair, 2 * pair + 1):
                    row = slot(0, m)
                    pool.tensor_tensor(row, row, finals[0].rs[:, m:m + 1].to_broadcast([P, D]), ALU.mult).then_inc(row_scaled, 1)
                    pool.wait_ge(row_scaled, m + 1)
                    pool.tensor_tensor(row, row, fgain[:], ALU.mult).then_inc(out_made[0], 1)
            norms[1].scales(pool, 2, 4)
            norms[1].scales(pool, 3, 6)
            norms[1].scales(pool, 4, 8, 1, NS)
            finals[0].scales(pool, 2, 4)
            finals[0].scales(pool, 3, 6)
            for pair in range(NBT // 2):
                finals[1].scales(pool, pair, 2 * pair)
            finals[1].scales(pool, NBT // 2, NBT, 1, NS)

        @block.scalar
        def _(act):
            def up_hi_cut(t, p):
                act.wait_ge(up_loaded[p], (t - p) * 8 + 16)
                wait(act, s["z_ready"], (t - 1) * NZ + 1)
                act.activation(up_hi[p][:], up_raw[:, p], ACT.Copy).then_inc(s["up_hi_made"], 1)

            def group(blk, gi, par, last):
                for j in range(GH):
                    t = blk * NTL + gi * GH + j
                    if not (last and blk == 1 and j == GH - 1):
                        up_hi_cut(t + 1, (j + 1) % 2)
                    act.wait_ge(s["dn_loaded"], t * 16 + 16)
                    act.wait_ge(s["y_ready"], outputs_before(blk, gi) + 1)
                    act.activation(dn_hi[:, j, :], dn_raw[:], ACT.Copy).then_inc(s["dn_hi_made"], 1)
                    for b, cols, bank in zblocks(blk, par * GH + j):
                        q = t * NZ + b
                        act.wait_ge(s["z_ready"], q + 2)
                        act.wait_ge(s["sqr_made"], q + 1)
                        rl = relu[:, cols]
                        act.activation(rl, bank, ACT.Relu).then_inc(s["relu_made"], 1)
                        act.wait_ge(s["relu_made"], q + 1 + ZB)
                        act.activation(z_hi[:, j, cols], rl, ACT.Square).then_inc(s["zhi_made"], 1)

            def square(blk, m):
                act.wait_ge(acc_loaded[blk][m % 4], 16 * (m // 4) + 16)
                norms[blk].square(act, m, m, slot(blk, m))

            def finished_square(blk, m):
                act.wait_ge(s["y_added"], outputs_before(blk, NG - 1) + 2 * m + 3)
                finals[blk].square(act, m, m, slot(blk, m))

            def cut_hi(blk, m):
                norms[blk].cut_hi(act, m, m % 4, slice(m * P, (m + 1) * P))

            square(0, 0)
            square(0, 1)
            up_hi_cut(0, 0)
            for m in range(NBT):
                if m % 2 == 0 and m + 2 < NBT:
                    square(0, m + 2)
                    square(0, m + 3)
                cut_hi(0, m)
            with act.Fori(0, NG // 2 - 1) as ii:
                for par in range(2):
                    group(0, ii * 2 + par, par, False)
            group(0, NG - 2, 0, False)
            group(0, NG - 1, 1, True)
            act.wait_ge(s["sqr_made"], NTL * NZ + 2)
            act.wait_ge(s["zhi_made"], NTL * NZ)
            for m in range(4):
                square(1, m)
            act.wait_ge(norms[1].squared, 4)
            for m in range(NBT):
                finished_square(0, m)
                if 2 <= m < 6:
                    cut_hi(1, m - 2)
            act.wait_ge(finals[0].squared, NBT)
            for m in (4, 5):
                square(1, m)
            cut_hi(1, 4)
            for m in (6, 7):
                square(1, m)
            norms[1].square(act, NBT, NBT, c.x_s[:], NS)
            for m in range(5, NBT):
                cut_hi(1, m)
            norms[1].cut_hi(act, NBT, 0, slice(BLK, W), NS)
            act.wait_ge(norms[1].squared, NBT + 1)
            with act.Fori(0, NG // 2 - 1) as ii:
                for par in range(2):
                    group(1, ii * 2 + par, par, False)
            group(1, NG - 2, 0, False)
            group(1, NG - 1, 1, True)
            act.wait_ge(s["sqr_made"], 2 * NTL * NZ + 2)
            act.wait_ge(s["zhi_made"], 2 * NTL * NZ)
            for m in range(NBT):
                finished_square(1, m)
            act.wait_ge(s["y_added"], outputs_before(1, NG) + 1)
            finals[1].square(act, NBT, NBT, c.x_s[:], NS)

        @block.vector
        def _(dve):
            def up_lo_cut(t, p):
                dve.wait_ge(s["up_hi_made"], t + 1)
                dve.tensor_tensor(up_lo[p][:], up_raw[:, p], up_hi[p][:].bitcast(F32), ALU.subtract).then_inc(s["up_lo_made"], 1)

            def add(blk, gi, unit):
                u, toks, half, bank, dst = unit
                dve.wait_ge(s["y_ready"], outputs_before(blk, gi) + u + 2)
                dve.tensor_tensor(dst, bank, dst, ALU.add).then_inc(s["y_added"], 1)

            def group(blk, gi, par, last):
                for j in range(GH):
                    t = blk * NTL + gi * GH + j
                    if not (last and blk == 1 and j == GH - 1):
                        up_lo_cut(t + 1, (j + 1) % 2)
                    dve.wait_ge(s["dn_hi_made"], t + 1)
                    dve.tensor_tensor(dn_lo[:, j, :], dn_raw[:], dn_hi[:, j, :].bitcast(F32), ALU.subtract).then_inc(s["dn_lo_made"], 1)
                    for b, cols, bank in zblocks(blk, par * GH + j):
                        q = t * NZ + b
                        dve.wait_ge(s["relu_made"], q + 1 + ZB)
                        dve.wait_ge(s["zlo_made"], q + 1)
                        sq = sqr[:, 0:cols.stop - cols.start]
                        dve.tensor_tensor(sq, relu[:, cols], relu[:, cols], ALU.mult).then_inc(s["sqr_made"], 1)
                        dve.wait_ge(s["zhi_made"], q + 1)
                        dve.wait_ge(s["sqr_made"], q + 3)
                        dve.tensor_tensor(z_lo[:, j, cols], sq, z_hi[:, j, cols].bitcast(F32), ALU.subtract).then_inc(s["zlo_made"], 1)
                if not last:
                    for unit in units(blk):
                        add(blk, gi, unit)

            def normalise(blk, m):
                norms[blk].normalise(dve, m, m, m // 2, m, slot(blk, m))

            def finish(blk, m):
                row = slot(blk, m)
                finals[blk].scaled(dve, m // 2, m, row, row, fgain).then_inc(out_made[blk], 1)

            def cut_lo(blk, m):
                norms[blk].cut_lo(dve, m, m % 4, slice(m * P, (m + 1) * P))

            dve.sem_inc(s["zlo_made"], 1)
            dve.sem_inc(s["sqr_made"], 2)
            dve.sem_inc(s["y_added"], 1)
            dve.wait_ge(s["gain_loaded"], 16)
            normalise(0, 0)
            up_lo_cut(0, 0)
            for m in range(NBT):
                if m + 1 < NBT:
                    normalise(0, m + 1)
                cut_lo(0, m)
            with dve.Fori(0, NG // 2 - 1) as ii:
                for par in range(2):
                    group(0, ii * 2 + par, par, False)
            group(0, NG - 2, 0, False)
            group(0, NG - 1, 1, True)
            us = units(0)
            for m in range(NBT):
                add(0, NG - 1, us[2 * m])
                add(0, NG - 1, us[2 * m + 1])
                if 2 <= m < 6:
                    cut_lo(1, m - 2)
                if m < 4:
                    normalise(1, m)
            normalise(1, 4)
            for m in range(4, NBT):
                if m + 1 < NBT:
                    normalise(1, m + 1)
                else:
                    norms[1].normalise(dve, NBT, 0, NBT // 2, NBT, c.x_s[:], NS)
                cut_lo(1, m)
            norms[1].cut_lo(dve, NBT, 0, slice(BLK, W), NS)
            for m in range(4, NBT):
                finish(0, m)
            with dve.Fori(0, NG // 2 - 1) as ii:
                for par in range(2):
                    group(1, ii * 2 + par, par, False)
            group(1, NG - 2, 0, False)
            group(1, NG - 1, 1, True)
            for unit in units(1):
                add(1, NG - 1, unit)
                u = unit[0]
                if u % 4 == 3 and u > 4:
                    finish(1, (u - 7) // 2)
                    finish(1, (u - 7) // 2 + 1)
            finish(1, NBT - 2)
            finish(1, NBT - 1)
            finals[1].scaled(dve, NBT // 2, NBT, c.x_s[:], c.x_s[:], fgain, NS).then_inc(out_made[1], 1)

        @block.tensor
        def _(pe):
            def up_block(t, p, zb):
                b, cols, bank = zb
                pe.wait_ge(s["relu_made"], t * NZ + b + 1)
                three_pass(pe, bank, [(up_hi[p][:, k, :], up_lo[p][:, k, :], h_hi[:, k, cols], h_lo[:, k, cols])
                                      for k in range(KT)]).then_inc(s["z_ready"], 1)

            def up_tile(blk, gi, par, j):
                t = blk * NTL + gi * GH + j
                pe.wait_ge(s["up_lo_made"], t + 1)
                for zb in zblocks(blk, par * GH + j):
                    up_block(t, j % 2, zb)

            def down(unit, js, first, last):
                u, toks, half, bank, _ = unit
                cols = slice(half * 512, (half + 1) * 512)
                return three_pass(pe, bank, [(z_hi[:, j, toks], z_lo[:, j, toks], dn_hi[:, j, cols], dn_lo[:, j, cols]) for j in js],
                                  start=first, stop=last)

            def down_group(blk, gi, between=None):
                us = units(blk)
                t = blk * NTL + gi * GH
                before = outputs_before(blk, gi)
                pe.wait_ge(s["zlo_made"], t * NZ + (GH - 1) * NZ + 1)
                pe.wait_ge(s["dn_lo_made"], t + GH - 1)
                pe.wait_ge(s["y_added"], before + 1)
                for unit in us[0:ZB]:
                    down(unit, range(GH - 1), True, False)
                pe.wait_ge(s["zlo_made"], t * NZ + GH * NZ + 1)
                pe.wait_ge(s["dn_lo_made"], t + GH)
                for unit in us[0:ZB]:
                    down(unit, [GH - 1], False, True).then_inc(s["y_ready"], 1)
                for unit in us[ZB:]:
                    pe.wait_ge(s["y_added"], before + unit[0] - ZB + 2)
                    down(unit, range(GH), True, True).then_inc(s["y_ready"], 1)
                    if between and unit[0] % 2:
                        between(unit[0] // 2)

            def group(blk, gi, par):
                for j in range(GH):
                    up_tile(blk, gi, par, j)
                down_group(blk, gi)

            def turn(blk, m):
                norms[blk].turn(pe, m, m % 4)

            def first_block(blk, b):
                zb = zblocks(blk, 0)
                tiles = (3, 6, NBT)[b]
                if b == 0:
                    pe.wait_ge(s["up_lo_made"], blk * NTL + 1)
                pe.wait_ge(norms[blk].lo_made, 2 * tiles + (2 if b == 2 and blk == 1 else 0))
                up_block(blk * NTL, 0, zb[b])

            pe.sem_inc(s["relu_made"], ZB)
            pe.sem_inc(s["z_ready"], 1)
            pe.sem_inc(s["y_ready"], 1)
            for blk in range(2):
                if blk == 0:
                    for m in range(4):
                        turn(0, m)
                first_block(blk, 0)
                for m in range(4, NBT):
                    turn(blk, m)
                    if m == 6:
                        first_block(blk, 1)
                if blk == 1:
                    norms[1].turn(pe, NBT, 0, NS)
                first_block(blk, 2)
                up_tile(blk, 0, 0, 1)
                down_group(blk, 0)
                group(blk, 1, 1)
                with pe.Fori(1, NG // 2 - (1 if blk == 0 else 0)) as ii:
                    for par in range(2):
                        group(blk, ii * 2 + par, par)
                if blk == 0:
                    group(0, NG - 2, 0)
                    for j in range(GH):
                        up_tile(0, NG - 1, 1, j)
                    pe.wait_ge(s["relu_made"], NTL * NZ + ZB)
                    down_group(0, NG - 1, lambda m: turn(1, m - 2) if 2 <= m < 6 else None)


def build(nc, named):
    with ExitStack() as stack:
        c, io = Shared(), named
        c.nc = nc
        zeroing = []

        def done(st):
            for owner, zero in zeroing:
                if owner is st:
                    zero()
        def use(st):
            mine = []

            def sem(name):
                mine.append(st.enter_context(nc.semaphore(name)))
                return mine[-1]

            def zero():
                nums = sorted(x.num for x in mine)
                runs = []
                for n in nums:
                    if runs and runs[-1][1] == n:
                        runs[-1][1] = n + 1
                    else:
                        runs.append([n, n + 1])
                for a, z in runs:
                    nc.gpsimd.sem_clear(range(a, z))
                nc.all_engine_barrier()
            c.sem = sem
            zeroing.append((st, zero))
        use(stack)
        io["p_dram"] = nc.dram_tensor("p_dram", (NF * P, T), F32).ap()
        io["x1_dram"] = nc.dram_tensor("x1_dram", (T, D), F32).ap()
        c.psum = [stack.enter_context(nc.psum_tensor(f"bank{i}", [P, 512], F32)) for i in range(8)]
        keep = Stage(nc, stack)
        c.ident = keep.sb("ident", [P, P])
        c.x_s = keep.sb("x_s", [NS, D])
        with ExitStack() as mixing:
            keep = Stage(nc, mixing)
            c.ones = keep.sb("ones", [P, P])
            c.upto = keep.sb("upto", [P, P])
            c.masks = keep.sb("masks", [P, LEVELS + 1, P])
            c.eye8 = keep.sb("eye8", [P, NS, NS])
            c.p_s = keep.sb("p_s", [P, NF, NS])
            c.tail = keep.sb("tail", [P, NCONV, 3])
            c.taps = keep.sb("taps", [P, NCONV, 28])
            c.ab_room = keep.sb("ab", [P, TW])
            c.ab = c.ab_room[0:2 * H, :]
            with ExitStack() as s1:
                use(s1)
                project(c, io, s1)
                done(s1)
            with ExitStack() as s2:
                k2 = Stage(nc, s2)
                use(s2)
                c.ga = k2.sb("ga", [P, NCH, 6, H])
                c.S = k2.sb("S", [P, HW])
                c.wsT = k2.sb("wsT", [P, HW])
                c.b_col = k2.sb("b_col", [P, H])
                c.o_gain = k2.sb("o_gain", [P, P])
                c.v_gain = k2.sb("v_gain", [P, HW])
                c.wo_hi = k2.sb("wo_hi", [P, KT, D], F32R)
                c.wo_lo = k2.sb("wo_lo", [P, KT, D], F32R)
                with ExitStack() as s3:
                    use(s3)
                    mix(c, io, s3)
                    done(s3)
                with ExitStack() as s4:
                    use(s4)
                    sample(c, io, s4)
                    done(s4)
                done(s2)
        with ExitStack() as s5:
            use(s5)
            ffn(c, io, s5)
            done(s5)


_INS = ['x_prompt', 'x_sample', 'state_delta', 'state_conv', 'norm_mix_g', 'w_in', 'conv_w', 'A_log', 'dt_bias',
        'o_norm_g', 'v_norm_g', 'w_s', 'b_s', 'w_o', 'norm_ffn_g', 'w_up', 'w_down', 'norm_f_g']
_OUTS = [('y_prompt', (1, 2048, 1024)), ('y_sample', (8, 1, 1024)), ('new_delta_prompt', (1, 1, 4, 128, 128)),
         ('new_conv_prompt', (1, 1, 3, 1536)), ('new_delta_sample', (1, 8, 4, 128, 128)),
         ('new_conv_sample', (1, 8, 3, 1536)), ('new_gmlp_v_sample', (1, 8, 1, 512))]


def kernel(**inputs):
    import numpy as _np
    import concourse.bacc as _bacc
    from concourse import mybir as _mybir
    from concourse.bass_utils import run_bass_kernel_spmd as _run

    nc = _bacc.Bacc("TRN2", target_bir_lowering=False, num_devices=1)
    arrays, io = {}, {}
    for name in _INS:
        a = _np.ascontiguousarray(inputs[name])
        arrays[f"in_{name}_dram"] = a
        io[name] = nc.dram_tensor(f"in_{name}_dram", a.shape, _mybir.dt.from_np(a.dtype), kind="ExternalInput").ap()
    for name, shape in _OUTS:
        io[name] = nc.dram_tensor(f"out_{name}_dram", shape, _mybir.dt.float32, kind="ExternalOutput").ap()
    build(nc, io)
    r = _run(nc, [arrays], core_ids=[0])
    return tuple(r.results[0][f"out_{name}_dram"] for name, _ in _OUTS)
```
